# Optimizing a Trainium2 kernel written in Bass

```python
import math
import jax, jax.numpy as jnp
from jax import lax
import numpy as np

D_MODEL = 1024
BATCH = 1
SEQ = 1024
DEPTH = 1
DEC_BATCH = 8
DEC_SEQ = 4
PAST_LEN = 512
PAGE_SIZE = 128

ATT_HEADS = 4
QK_DIM = D_MODEL // (4 * ATT_HEADS)
QK2 = 2 * QK_DIM
V_DIM = 2 * QK_DIM
Q_W = ATT_HEADS * QK2
ATT_W = ATT_HEADS * V_DIM
POOL_WINDOWS = (2, 4, 8, 16)
POOL_GROUPS = len(POOL_WINDOWS)
POOL_GW = D_MODEL // (2 * POOL_GROUPS)
POOL_W = POOL_GROUPS * POOL_GW
POOL_PAD = max(POOL_WINDOWS) - 1
MIX_W = ATT_W + POOL_W
IN_W = 2 * Q_W + ATT_W + POOL_W
REL_BUCKETS = 32
REL_MAX_DIST = 128
Q_BLOCK = 128
PEER_HEADS = 8
PEER_KEYS = 128
PEER_EXPERTS = PEER_KEYS * PEER_KEYS
PEER_QDIM = 256
PEER_HALF = PEER_QDIM // 2
PEER_TOPK = 16
PEER_BLOCK = 128
PLE_DIM = 256
NEG_INF = -1e30
EPS = 1e-6

kernel_name = 'hymba_diffattn_pool_peer_decode_step'

def _rmsnorm(x, g):
    xf = x.astype(jnp.float32)
    y = xf * lax.rsqrt(jnp.mean(xf * xf, axis=-1, keepdims=True) + EPS)
    return (y * g.astype(jnp.float32)).astype(x.dtype)

def _t5_bucket(rel):
    n = jnp.maximum(rel, 0)
    exact = REL_BUCKETS // 2
    large = exact + (jnp.log(jnp.maximum(n, 1).astype(jnp.float32) / exact)
                     / math.log(REL_MAX_DIST / exact) * (REL_BUCKETS - exact)).astype(jnp.int32)
    large = jnp.minimum(large, REL_BUCKETS - 1)
    return jnp.where(n < exact, n, large)

def _diff_attn_block(q, k, v, q_pos, k_pos, lam, rel_bias):
    scale = QK_DIM ** -0.5
    bias = rel_bias[_t5_bucket(q_pos[:, None] - k_pos[None, :])]
    bias = jnp.transpose(bias, (2, 0, 1))[None].astype(jnp.float32)
    mask = (k_pos[None, :] <= q_pos[:, None])[None, None]

    def probs(qa, ka):
        s = jnp.einsum('bqhd,bkhd->bhqk', qa, ka).astype(jnp.float32) * scale + bias
        return jax.nn.softmax(jnp.where(mask, s, NEG_INF), axis=-1)

    a = probs(q[..., :QK_DIM], k[..., :QK_DIM]) - lam * probs(q[..., QK_DIM:], k[..., QK_DIM:])
    return jnp.einsum('bhqk,bkhd->bqhd', a.astype(v.dtype), v)

def _diff_attention(q, k, v, q_pos, k_pos, lam, rel_bias):
    B, L = q.shape[0], q.shape[1]
    if L > Q_BLOCK and L % Q_BLOCK == 0:
        nb = L // Q_BLOCK
        qb = jnp.moveaxis(q.reshape(B, nb, Q_BLOCK, ATT_HEADS, QK2), 1, 0)
        pb = q_pos.reshape(nb, Q_BLOCK)
        out = lax.map(lambda a: _diff_attn_block(a[0], k, v, a[1], k_pos, lam, rel_bias), (qb, pb))
        return jnp.moveaxis(out, 0, 1).reshape(B, L, ATT_HEADS, V_DIM)
    return _diff_attn_block(q, k, v, q_pos, k_pos, lam, rel_bias)

def _pool_mixer(u, prev, start_pos, pool_w, pool_scale):
    L = u.shape[1]
    z = jnp.concatenate([prev, u], axis=1)
    zf = z.astype(jnp.float32)
    cs = jnp.concatenate([jnp.zeros_like(zf[:, :1]), jnp.cumsum(zf, axis=1)], axis=1)
    pos = start_pos + jnp.arange(L, dtype=jnp.int32)
    outs = []
    for g, w in enumerate(POOL_WINDOWS):
        c0, c1 = g * POOL_GW, (g + 1) * POOL_GW
        hi = cs[:, POOL_PAD + 1: POOL_PAD + 1 + L, c0:c1]
        lo = cs[:, POOL_PAD + 1 - w: POOL_PAD + 1 - w + L, c0:c1]
        cnt = jnp.minimum(pos + 1, w).astype(jnp.float32)[None, :, None]
        d = ((hi - lo) / cnt - u[..., c0:c1].astype(jnp.float32)).astype(u.dtype)
        outs.append(d @ pool_w[g])
    out = jnp.concatenate(outs, axis=-1) * pool_scale
    return out, z[:, -POOL_PAD:, :]

def _peer_block(xb, wq, sub_keys, u_tab, v_tab):
    T = xb.shape[0]
    q = (xb @ wq).reshape(T, PEER_HEADS, 2, PEER_HALF)
    s = jnp.einsum('thpd,hpkd->thpk', q, sub_keys).astype(jnp.float32)
    s1, i1 = lax.top_k(s[:, :, 0], PEER_TOPK)
    s2, i2 = lax.top_k(s[:, :, 1], PEER_TOPK)
    cand = (s1[..., :, None] + s2[..., None, :]).reshape(T, PEER_HEADS, PEER_TOPK * PEER_TOPK)
    cidx = (i1[..., :, None] * PEER_KEYS + i2[..., None, :]).reshape(T, PEER_HEADS, PEER_TOPK * PEER_TOPK)
    top, sel = lax.top_k(cand, PEER_TOPK)
    idx = jnp.take_along_axis(cidx, sel, axis=-1)
    gate = jax.nn.softmax(top, axis=-1)
    u = u_tab[idx]
    h = jax.nn.gelu(jnp.einsum('td,thkd->thk', xb, u).astype(jnp.float32), approximate=False)
    v = v_tab[idx]
    return jnp.einsum('thk,thkd->td', (gate * h).astype(xb.dtype), v)

def _peer(xn, wq, sub_keys, u_tab, v_tab):
    T = xn.shape[0]
    nb = -(-T // PEER_BLOCK)
    xp = jnp.pad(xn, ((0, nb * PEER_BLOCK - T), (0, 0))).reshape(nb, PEER_BLOCK, D_MODEL)
    out = lax.map(lambda xb: _peer_block(xb, wq, sub_keys, u_tab, v_tab), xp)
    return out.reshape(nb * PEER_BLOCK, D_MODEL)[:T]

def _layer(x, p, past_k, past_v, pool_prev, start_pos, lam_init,
           norm_attn_g, w_in, lq1, lk1, lq2, lk2, subln_g, rel_bias, pool_w, pool_scale,
           w_out, norm_ffn_g, peer_wq, peer_keys, peer_u, peer_v, norm_pl_g, w_pl, w_pl_gate):
    B, L, _ = x.shape
    xn = _rmsnorm(x, norm_attn_g)
    proj = xn @ w_in
    q = proj[..., :Q_W].reshape(B, L, ATT_HEADS, QK2)
    k = proj[..., Q_W:2 * Q_W].reshape(B, L, ATT_HEADS, QK2)
    v = proj[..., 2 * Q_W:2 * Q_W + ATT_W].reshape(B, L, ATT_HEADS, V_DIM)
    u = proj[..., 2 * Q_W + ATT_W:]
    past_len = past_k.shape[1]
    k_all = jnp.concatenate([past_k, k], axis=1)
    v_all = jnp.concatenate([past_v, v], axis=1)
    k_pos = start_pos - past_len + jnp.arange(past_len + L, dtype=jnp.int32)
    q_pos = start_pos + jnp.arange(L, dtype=jnp.int32)
    lam = (jnp.exp(jnp.sum(lq1.astype(jnp.float32) * lk1.astype(jnp.float32)))
           - jnp.exp(jnp.sum(lq2.astype(jnp.float32) * lk2.astype(jnp.float32))) + lam_init)
    attn = _diff_attention(q, k_all, v_all, q_pos, k_pos, lam, rel_bias)
    attn = _rmsnorm(attn, subln_g) * (1.0 - lam_init)
    pool_out, new_pool = _pool_mixer(u, pool_prev, start_pos, pool_w, pool_scale)
    mixed = jnp.concatenate([attn.reshape(B, L, ATT_W), pool_out], axis=-1)
    x = x + mixed @ w_out
    xn2 = _rmsnorm(x, norm_ffn_g)
    x = x + _peer(xn2.reshape(B * L, D_MODEL), peer_wq, peer_keys, peer_u, peer_v).reshape(B, L, D_MODEL)
    gate = jax.nn.sigmoid(_rmsnorm(x, norm_pl_g) @ w_pl_gate)
    x = x + gate * (p @ w_pl)
    return x, k, v, new_pool

def setup_inputs(seed: int = 0) -> dict:
    key = jax.random.key(seed)
    ks = jax.random.split(key, 32)
    f32 = jnp.float32

    def nrm(k, shape, scale):
        return jax.random.normal(k, shape, f32) * scale

    n_pages = PAST_LEN // PAGE_SIZE
    n_used = DEC_BATCH * n_pages
    n_phys = n_used + max(1, n_used // 4)
    perm = jax.random.permutation(ks[0], n_phys)
    page_table = perm[:n_used].reshape(DEC_BATCH, n_pages).astype(jnp.int32)
    return {
        'x_prompt': nrm(ks[1], (BATCH, SEQ, D_MODEL), 1.0),
        'x_sample': nrm(ks[2], (DEC_BATCH, DEC_SEQ, D_MODEL), 1.0),
        'cache_k': nrm(ks[3], (DEPTH, n_phys, PAGE_SIZE, ATT_HEADS, QK2), 1.0),
        'cache_v': nrm(ks[4], (DEPTH, n_phys, PAGE_SIZE, ATT_HEADS, V_DIM), 1.0),
        'page_table': page_table,
        'state_pool': nrm(ks[5], (DEPTH, DEC_BATCH, POOL_PAD, POOL_W), 1.0),
        'p_prompt': nrm(ks[6], (DEPTH, BATCH, SEQ, PLE_DIM), 1.0),
        'p_sample': nrm(ks[7], (DEPTH, DEC_BATCH, DEC_SEQ, PLE_DIM), 1.0),
        'norm_attn_g': 1.0 + nrm(ks[8], (DEPTH, D_MODEL), 0.05),
        'w_in': nrm(ks[9], (DEPTH, D_MODEL, IN_W), D_MODEL ** -0.5),
        'lambda_q1': nrm(ks[10], (DEPTH, QK_DIM), 0.1),
        'lambda_k1': nrm(ks[11], (DEPTH, QK_DIM), 0.1),
        'lambda_q2': nrm(ks[12], (DEPTH, QK_DIM), 0.1),
        'lambda_k2': nrm(ks[13], (DEPTH, QK_DIM), 0.1),
        'subln_g': 1.0 + nrm(ks[14], (DEPTH, V_DIM), 0.05),
        'rel_bias': nrm(ks[15], (REL_BUCKETS, ATT_HEADS), 0.5),
        'pool_w': nrm(ks[16], (DEPTH, POOL_GROUPS, POOL_GW, POOL_GW), POOL_GW ** -0.5),
        'pool_scale': 1.0 + nrm(ks[17], (DEPTH, POOL_W), 0.05),
        'w_out': nrm(ks[18], (DEPTH, MIX_W, D_MODEL), MIX_W ** -0.5),
        'norm_ffn_g': 1.0 + nrm(ks[19], (DEPTH, D_MODEL), 0.05),
        'peer_wq': nrm(ks[20], (DEPTH, D_MODEL, PEER_HEADS * PEER_QDIM), D_MODEL ** -0.5),
        'peer_keys': nrm(ks[21], (DEPTH, PEER_HEADS, 2, PEER_KEYS, PEER_HALF), PEER_HALF ** -0.5),
        'peer_u': nrm(ks[22], (DEPTH, PEER_EXPERTS, D_MODEL), D_MODEL ** -0.5),
        'peer_v': nrm(ks[23], (DEPTH, PEER_EXPERTS, D_MODEL), 0.3),
        'norm_pl_g': 1.0 + nrm(ks[24], (DEPTH, D_MODEL), 0.05),
        'w_pl': nrm(ks[25], (DEPTH, PLE_DIM, D_MODEL), 0.5 * PLE_DIM ** -0.5),
        'w_pl_gate': nrm(ks[26], (DEPTH, D_MODEL, D_MODEL), D_MODEL ** -0.5),
        'final_norm_g': 1.0 + nrm(ks[27], (D_MODEL,), 0.05),
    }

def reference(x_prompt, x_sample, cache_k, cache_v, page_table, state_pool, p_prompt, p_sample,
              norm_attn_g, w_in, lambda_q1, lambda_k1, lambda_q2, lambda_k2, subln_g, rel_bias,
              pool_w, pool_scale, w_out, norm_ffn_g, peer_wq, peer_keys, peer_u, peer_v,
              norm_pl_g, w_pl, w_pl_gate, final_norm_g):
    hp, hs = x_prompt, x_sample
    kp_l, vp_l, pp_l, ks_l, vs_l, ps_l = [], [], [], [], [], []
    for i in range(DEPTH):
        lam_init = 0.8 - 0.6 * math.exp(-0.3 * i)
        wts = (norm_attn_g[i], w_in[i], lambda_q1[i], lambda_k1[i], lambda_q2[i], lambda_k2[i],
               subln_g[i], rel_bias, pool_w[i], pool_scale[i], w_out[i], norm_ffn_g[i],
               peer_wq[i], peer_keys[i], peer_u[i], peer_v[i], norm_pl_g[i], w_pl[i], w_pl_gate[i])
        empty_k = jnp.zeros((BATCH, 0, ATT_HEADS, QK2), x_prompt.dtype)
        empty_v = jnp.zeros((BATCH, 0, ATT_HEADS, V_DIM), x_prompt.dtype)
        zero_pool = jnp.zeros((BATCH, POOL_PAD, POOL_W), x_prompt.dtype)
        hp, kp, vp, pp = _layer(hp, p_prompt[i], empty_k, empty_v, zero_pool, 0, lam_init, *wts)
        past_k = cache_k[i][page_table].reshape(DEC_BATCH, -1, ATT_HEADS, QK2)
        past_v = cache_v[i][page_table].reshape(DEC_BATCH, -1, ATT_HEADS, V_DIM)
        hs, ksm, vsm, psm = _layer(hs, p_sample[i], past_k, past_v, state_pool[i], PAST_LEN, lam_init, *wts)
        kp_l.append(kp); vp_l.append(vp); pp_l.append(pp)
        ks_l.append(ksm); vs_l.append(vsm); ps_l.append(psm)
    y_prompt = _rmsnorm(hp, final_norm_g)
    y_sample = _rmsnorm(hs, final_norm_g)
    new_k_prompt = jnp.stack(kp_l, axis=0)
    new_v_prompt = jnp.stack(vp_l, axis=0)
    new_pool_prompt = jnp.stack(pp_l, axis=0)
    new_k_sample = jnp.stack(ks_l, axis=0)
    new_v_sample = jnp.stack(vs_l, axis=0)
    new_pool_sample = jnp.stack(ps_l, axis=0)
    return (y_prompt, y_sample, new_k_prompt, new_v_prompt, new_pool_prompt, new_k_sample, new_v_sample, new_pool_sample)


_drawn_inputs = setup_inputs


def setup_inputs(seed=0):
    import zlib

    import numpy as np

    out = dict(_drawn_inputs(seed))
    spreads = {}
    factors = {'lambda_q1': 116.966, 'norm_pl_g': 34.688, 'lambda_q2': 27.824, 'lambda_k2': 8.0}
    for name, (base, spread) in spreads.items():
        noise = np.random.default_rng([zlib.crc32(name.encode()), seed]).standard_normal(out[name].shape)
        drawn = base * np.exp(spread * noise) if base else spread * noise
        out[name] = __import__('jax').numpy.asarray(drawn.astype(out[name].dtype))
    for name, factor in factors.items():
        out[name] = (out[name] * factor).astype(out[name].dtype)
    return out
```

```python
from contextlib import ExitStack

import numpy as np

import concourse.bass as bass
from concourse import mybir

D = 1024
T = 128
SEQ = 1024
NT = SEQ // T
DB, DS = 8, 4
NS = DB * DS
PAST, PAGE = 512, 128
NPG = PAST // PAGE
H = 4
QK = 64
HV = 128
W4 = 512
WINDOWS = (2, 4, 8, 16)
PAD = 15
KD = D // 128
BUCKETS, MAX_DIST = 32, 128
PH, NK, TOPK = 8, 128, 16
PLE = 256
EPS = 1e-6
NEG = -1e30
LAM_INIT = 0.2
SCALE = QK ** -0.5
FMAX = -3.0e38
RING = 8
B = 2
NB = TOPK // B
SPAN = (NT - 1) * T
BW = 1408
STRIP = 1536
PT_P = 9


def front_and_experts(nc, x, xs, cache_k, cache_v, page_table, state, p_t, norm_attn_g, w_in,
                      lams, subln_g, rel_bias, pool_w, pool_scale, w_out, norm_ffn_g, wq_t,
                      keys_t, uv, norm_pl_g, w_pl, w_gate, final_g, c_ident, c_onehot, c_bands,
                      c_band_prev, c_band_s, c_band_sp, c_mask_s, c_half, c_row, c_iota, outs):
    (y_p, y_s, nk_p, nv_p, npool_p, nk_s, nv_s, npool_s) = outs
    f32, i32, u32, bf16 = mybir.dt.float32, mybir.dt.int32, mybir.dt.uint32, mybir.dt.bfloat16
    ALU, ACT, AX = mybir.AluOpType, mybir.ActivationFunctionType, mybir.AxisListType
    ds = bass.ds

    x1_d = nc.dram_tensor("x1_scratch", ((NT + 1) * T, D), f32, kind="Internal").ap()
    strip_h = nc.dram_tensor("strip_scratch", (H * T * STRIP,), f32, kind="Internal")
    strip_d = strip_h.ap()

    def strip_view(offset, dims):
        return bass.AP(tensor=strip_d.tensor, offset=offset, ap=dims)

    with ExitStack() as whole:
        def sb(name, shape, dt=f32, stack=whole):
            return stack.enter_context(nc.sbuf_tensor(name, shape, dt))

        def sem(name):
            return whole.enter_context(nc.semaphore(name))

        big = sb("big", [T, KD, 2048])
        mid = sb("mid", [T, KD, D])
        ring = sb("ring", [T, RING, 2 * D])
        ident = sb("ident", [T, T])
        rf = ring[:, :, :].rearrange("p a b -> p (a b)")

        def part(at, *shape):
            n = int(np.prod(shape))
            v = rf[:, at:at + n]
            if len(shape) == 2:
                return v.rearrange("p (a b) -> p a b", b=shape[1])
            return v

        kT = part(0, H, SEQ)
        vals = part(4096, NT, W4)
        biasw = part(8192, H, BW)
        q_sb = part(13824, W4)
        k_sb = part(14336, W4)
        qT = part(14848, H, T)
        dT = part(15360, H, T)
        bandc = part(15872, H, T)
        pages = part(0, RING, W4)
        pkT = part(4096, 2, W4)
        s_T = part(5120, NPG * 256)
        s_Tn = part(6144, 256)
        s_row = part(6400, 2, 544)
        pr_T = part(7488, NPG * 256)
        pr_Tn = part(8512, 256)
        o_ps = part(8768, 256)
        o_T = part(9024, H * NS)
        st_sb = part(9152, W4)
        qTs = part(9664, H * NS)
        kTs = part(9792, H * NS)
        bf_T = part(9920, H * DS)
        b_raw = part(9936, H * DS)
        bx_raw = part(9952, H * DS)
        wq_st = part(0, 2, D)
        keys_sb = part(2048, 2 * PH, NK)

        with ExitStack() as first:
            def fb(name, shape, dt=f32):
                return sb(name, shape, dt, first)

            xt = fb("xt", [T, 2, D])
            xT = fb("xT", [T, KD, T])
            u_sb = fb("u_sb", [T, 2, W4])
            S = fb("S", [T, 2, 2, SEQ])
            AT = fb("AT", [T, KD, T])
            bandp = fb("bandp", [T, H, T])
            pw = fb("pw", [T, H, T])
            bs_c = fb("bs_c", [NS, H * NS])
            bs_p = fb("bs_p", [DB * PAD, H * NS])
            avs = fb("avs", [T, W4])
            g_attn = fb("g_attn", [T, KD])
            g_sub = fb("g_sub", [T, 1])
            psc = fb("psc", [T, H])
            lam_in = fb("lam_in", [T, 4, QK])
            relb = fb("relb", [BUCKETS + 1, H])
            ptab = fb("ptab", [T, DB * NPG], i32)
            pidx = fb("pidx", [T, DB * NPG], i32)
            mask_s = fb("mask_s", [NS, DB])
            half = fb("half", [T, 2])
            pagef = fb("pagef", [T, DB * NPG])[:, :]
            row = fb("row", [T, 1])
            far = fb("far", [T, H])
            st = fb("st", [T, 48])
            sq = AT[:, :, :].rearrange("p a b -> p (a b)")
        XSS, XRT, XR = 0, 2, 4
        LAMS, LAME, NLAM = 6, 8, 10
        NMAX, LSUM, LREC = 12, 16, 20
        OSS, ORT, OREC = 24, 28, 32
        SMX, SSUM, SREC, SCO = 36, 38, 40, 42

        with ExitStack() as second:
            def gb(name, shape, dt=f32):
                return sb(name, shape, dt, second)

            xn_next = gb("xn_next", [T, D])
            xn_cur = gb("xn_cur", [T, D])
            xnT = gb("xnT", [T, KD, T])
            x2 = gb("x2", [T, D])
            g_ffn = gb("g_ffn", [T, D])
            g_fin = gb("g_fin", [T, D])
            wpl = gb("wpl", [T, 2, D])
            p_sb = gb("p_sb", [T, 2, T])
            diag = gb("diag", [T, RING, T])
            x2T = gb("x2T", [T, KD, T])
            sg = gb("sg", [T, W4])
            junk = sg[:, :].bitcast(bf16)
            g_pl = gb("g_pl", [T, KD])
            iota = gb("iota", [T, TOPK])
            idx = gb("idx", [T, 2, TOPK], i32)
            gate = gb("gate", [T, 2, TOPK])
            ex = gb("ex", [T, 2, TOPK])
            hdot = gb("hdot", [T, 2, TOPK])
            hgelu = gb("hgelu", [T, 2, TOPK])
            sc_sb = gb("sc_sb", [T, 256])
            sc_lo = sg[:, 0:256]
            cand = sg[:, 256:512]
            cand_lo = sc_sb
            top1 = gb("top1", [T, 2, TOPK])
            ind1 = gb("ind1", [T, 2, TOPK], u32)
            ind1f = gb("ind1f", [T, 2, TOPK])
            top2 = gb("top2", [T, TOPK])
            ind2 = gb("ind2", [T, TOPK], u32)
            ab = gb("ab", [T, 2, TOPK], u32)
            abf = gb("abf", [T, 2, TOPK])
            pick = gb("pick", [T, 2, TOPK])
            gst = gb("gst", [T, 16])
        NS1, RT1, R1 = 0, 1, 2
        NS2, RT2, R2 = 3, 4, 5
        NS3, RT3, R3 = 6, 7, 8
        NTOP, ESUM, EREC = 10, 12, 14

        sc = whole.enter_context(nc.psum_tensor("sc", [T, 4, 512], f32))
        pb = [whole.enter_context(nc.psum_tensor(f"proj{i}", [T, 512], f32)) for i in range(2)]
        tb = [whole.enter_context(nc.psum_tensor(f"turn{i}", [T, 512], f32)) for i in range(2)]

        const_in = sem("const_in")
        w_in_in = sem("w_in_in")
        w_out_in = sem("w_out_in")
        onehot_in = sem("onehot_in")
        strip_ps = sem("strip_ps")
        strip_sb = sem("strip_sb")
        strip_out = [sem(f"strip_out{i}") for i in range(2)]
        bias_in = sem("bias_in")
        gain_ready = sem("gain_ready")
        lam_sum = sem("lam_sum")
        lam_exp = sem("lam_exp")
        zeroed = sem("zeroed")
        pad_zero = sem("pad_zero")
        x_in = [sem(f"x_in{i}") for i in range(2)]
        band_in = sem("band_in")
        pad_out = sem("pad_out")
        x_sq = sem("x_sq")
        x_root = sem("x_root")
        x_norm = sem("x_norm")
        pb_ready = [sem(f"proj_ready{i}") for i in range(2)]
        pb_free = [sem(f"proj_free{i}") for i in range(2)]
        tb_ready = [sem(f"turn_ready{i}") for i in range(2)]
        tb_free = [sem(f"turn_free{i}") for i in range(2)]
        s_ready = [sem(f"score_ready{i}") for i in range(2)]
        s_read = [sem(f"score_read{i}") for i in range(2)]
        s_max = [sem(f"score_max{i}") for i in range(2)]
        s_exp = [sem(f"score_exp{i}") for i in range(2)]
        a_ready = sem("a_ready")
        av_done = sem("av_done")
        o_sq = sem("o_sq")
        o_root = sem("o_root")
        o_norm = sem("o_norm")
        k_out = sem("k_out")
        v_out = sem("v_out")
        new_rows_out = sem("new_rows_out")
        old_rows_out = sem("old_rows_out")
        x1_out = [sem(f"x1_out{i}") for i in range(2)]
        turns = sem("turns")
        st_in = sem("st_in")
        page_idx = sem("page_idx")
        page_in = [sem(f"page_in{i}") for i in range(RING)]
        page_read = sem("page_read")
        kp_ready = sem("kp_ready")
        kp_read = sem("kp_read")
        ss_ready = sem("ss_ready")
        bT_in = sem("bT_in")
        bT_ready = sem("bT_ready")
        sT_ready = sem("sT_ready")
        sx_ready = sem("sx_ready")
        sx_exp = sem("sx_exp")
        sp_ready = sem("sp_ready")
        prT_ready = sem("prT_ready")
        o_sum = sem("o_sum")
        wq_in = [sem(f"wq_in{i}") for i in range(2)]
        keys_in = sem("keys_in")
        wk_ready = [sem(f"wk_ready{i}") for i in range(2)]
        wk_kept = [sem(f"wk_kept{i}") for i in range(2)]
        gate_w_in = sem("gate_w_in")
        g_in = sem("g_in")
        xn_in = sem("xn_in")
        xn_sq = sem("xn_sq")
        xn_root = sem("xn_root")
        xn_ready = sem("xn_ready")
        xn_turned = sem("xn_turned")
        xnT_ready = sem("xnT_ready")
        xn_moved = sem("xn_moved")
        x1_in = sem("x1_in")
        p_in = sem("p_in")
        route_ready = sem("route_ready")
        route_read = sem("route_read")
        top_ready = sem("top_ready")
        top_exp = sem("top_exp")
        idx_ready = sem("idx_ready")
        gathered = [sem(f"gathered{i}") for i in range(RING)]
        slot_free = sem("slot_free")
        dots_done = sem("dots_done")
        gelu_done = sem("gelu_done")
        diag_ready = sem("diag_ready")
        x2_ready = sem("x2_ready")
        x2_sq = sem("x2_sq")
        x2_root = sem("x2_root")
        r2_ready = sem("r2_ready")
        x2_turned = sem("x2_turned")
        x2T_ready = sem("x2T_ready")
        gate_ready = sem("gate_ready")
        ple_ready = sem("ple_ready")
        ple_read = sem("ple_read")
        sig_ready = sem("sig_ready")
        sig_read = sem("sig_read")
        y_sq = sem("y_sq")
        y_root = sem("y_root")
        y_ready = sem("y_ready")
        y_out = sem("y_out")

        block = whole.enter_context(nc.Block())

        def hold(eng, s, value):
            eng.wait_ge(s, value)
            eng.sem_inc(turns, 1)

        def proj(i, par, o):
            n = par * PT_P + o
            return n % 2, i * PT_P + n // 2
        Q_, K_, V_, U_, BAND, POOL, AV, WO = range(8)

        class Region:
            def __init__(self, first, last, width, before):
                self.first, self.last, self.width = first, last, width
                self.nb = width // 512
                self.per = 5 + H * self.nb
                self.before = before
                self.after = before + (last - first) * self.per

            def turn(self, i, par, o):
                n = par * self.per + o
                return n % 2, (i - self.first) * self.per + self.before + n // 2

            def a_turn(self, i, par, h, c):
                return self.turn(i, par, 4 + h * self.nb + c)

            def o_turn(self, i, par):
                return self.turn(i, par, 4 + H * self.nb)

        RA = Region(0, 2, 512, 0)
        RB = Region(2, 4, 1024, RA.after)
        REGIONS = (RA, RB)
        ST0 = RB.after
        SI = NT // 2

        def s_turn(o):
            return o % 2, ST0 + o // 2
        S_PAGE, S_ROW, S_BACK, S_O = 4, 36, 39, 42
        ST_N = 44
        N_FIRST_LOADS = 15

        @block.sync
        def _(sp):
            for dst, src in (
                (ident[:, :], c_ident), (bandp[:, :, :], c_band_prev), (pw[:, :, :], pool_w),
                (bs_c[:, :], c_band_s), (bs_p[:, :], c_band_sp), (g_attn[:, :], norm_attn_g),
                (g_sub[:, :], subln_g), (psc[:, :], pool_scale),
                (relb[0:BUCKETS, :], rel_bias), (mask_s[:, :], c_mask_s), (half[:, :], c_half),
                (row[:, :], c_row),
                (ptab[:, :], page_table.rearrange("a b -> (a b)").partition_broadcast(T)),
                (lam_in[:, :, :], lams.partition_broadcast(T)),
            ):
                sp.dma_start(dst, src).then_inc(const_in, 16)
            sp.dma_start(mid[0:BUCKETS + 1, 0:2, 0:768],
                         c_onehot.rearrange("p (a b) -> p a b", b=768)).then_inc(onehot_in, 16)
            sp.dma_start(xt[:, 0, :], x[0:T, :]).then_inc(x_in[0], 16)
            for c in range(4):
                sp.dma_start(big[:, :, c * W4:(c + 1) * W4],
                             w_in[:, c * W4:(c + 1) * W4].rearrange("(k p) n -> p k n", p=T)
                             ).then_inc(w_in_in, 16)
                if c == 0:
                    sp.dma_start(xt[:, 1, :], x[T:2 * T, :]).then_inc(x_in[1], 16)
            sp.dma_start(bandc, c_bands[0:T, :].rearrange("p (g t) -> p g t", g=H)).then_inc(band_in, 16)
            for h in range(H):
                sp.wait_ge(strip_sb, h + 1)
                sp.dma_start(strip_view(h * T * STRIP, [[STRIP, T], [1, STRIP]]),
                             S[:, h % 2, :, :].rearrange("p a b -> p (a b)")[:, 0:STRIP]
                             ).then_inc(strip_out[h % 2], 16)
            for c in range(2):
                sp.dma_start(mid[:, :, c * W4:(c + 1) * W4],
                             w_out[:, c * W4:(c + 1) * W4].rearrange("(k p) n -> p k n", p=T)
                             ).then_inc(w_out_in, 16)
            sp.wait_ge(strip_out[0], 16 * H // 2)
            sp.wait_ge(strip_out[1], 16 * H // 2)
            sp.dma_start(biasw, strip_view(T - 1, [[STRIP - 1, T], [T * STRIP, H], [1, BW]])
                         ).then_inc(bias_in, 16)
            with sp.Fori(1, NT // 2) as i:
                for par in range(2):
                    b, m = proj(i - 1, par, BAND)
                    sp.wait_ge(pb_ready[b], m + 1)
                    sp.dma_start(bandc, c_bands[ds(i * (2 * T) + (par - 1) * T, T), :].rearrange(
                        "p (g t) -> p g t", g=H)).then_inc(band_in, 16)
                    sp.wait_ge(x1_out[par], i * 16)
                    sp.dma_start(xt[:, par, :], x[ds(i * (2 * T) + par * T, T), :]
                                 ).then_inc(x_in[par], 16)
            b, m = proj(SI - 1, 0, BAND)
            sp.wait_ge(pb_ready[b], m + 1)
            sp.dma_start(bandc, c_bands[SEQ - T:SEQ, :].rearrange("p (g t) -> p g t", g=H)
                         ).then_inc(band_in, 16)
            sp.wait_ge(x1_out[0], 16 * SI)
            sp.dma_start(xt[0:NS, 0, :], xs).then_inc(x_in[0], 16)
            sp.wait_ge(av_done, H * NT + H)
            sp.dma_start(st_sb[0:DB * PAD, :], state).then_inc(st_in, 16)
            near0 = SPAN + T - 1 - T
            with nc.allow_non_contiguous_dma(reason="small bias tables"):
                for h in range(H):
                    sp.dma_start(b_raw[:, h * DS:(h + 1) * DS],
                                 strip_view(h * T * STRIP + near0, [[1, T], [STRIP - 1, DS]]),
                                 allow_slow_non_contiguous=True).then_inc(bT_in, 16)
                    for b in range(DB):
                        sp.dma_start(bx_raw[b * DS:(b + 1) * DS, h * DS:(h + 1) * DS],
                                     strip_view(h * T * STRIP + SPAN + T - 1, [[1, DS], [STRIP - 1, DS]]),
                                     allow_slow_non_contiguous=True).then_inc(bT_in, 16)
            sp.dma_start(npool_s[:, 0:PAD - DS, :], state.rearrange("(b r) n -> b r n", b=DB)[:, DS:PAD, :]
                         ).then_inc(old_rows_out, 16)
            sp.wait_ge(x1_out[0], 16 * (SI + 1))
            sp.wait_ge(x1_out[1], 16 * SI)
            sp.wait_ge(k_out, 16 * (NT + 2))
            sp.wait_ge(v_out, 16 * (NT + 1))
            sp.wait_ge(new_rows_out, 16 * 2)
            sp.wait_ge(old_rows_out, 16)
            sp.wait_ge(pad_out, 16)
            for hp in range(2 * PH):
                if hp == 0:
                    sp.dma_start(keys_sb, keys_t.rearrange("h d k -> d h k")).then_inc(keys_in, 16)
                if hp >= 2:
                    sp.wait_ge(wk_ready[1], hp - 1)
                sp.dma_start(wq_st[:, hp % 2, :], wq_t[hp * T:(hp + 1) * T, :]).then_inc(wq_in[hp % 2], 16)
            sp.dma_start(xn_next[:, :], x1_d[0:T, :]).then_inc(xn_in, 16)
            for dst, src in ((g_ffn[:, :], norm_ffn_g.partition_broadcast(T)),
                             (g_fin[:, :], final_g.partition_broadcast(T)),
                             (g_pl[:, :], norm_pl_g), (iota[:, :], c_iota.partition_broadcast(T)),
                             (wpl[:, :, :], w_pl.rearrange("(k p) n -> p k n", p=T))):
                sp.dma_start(dst, src).then_inc(g_in, 16)
            sp.dma_start(x2[:, :], x1_d[0:T, :]).then_inc(x1_in, 16)
            for c in range(2):
                sp.dma_start(mid[:, :, c * W4:(c + 1) * W4],
                             w_gate[:, c * W4:(c + 1) * W4].rearrange("(k p) n -> p k n", p=T)
                             ).then_inc(gate_w_in, 16)
            sp.dma_start(p_sb[:, :, :], p_t[:, 0:T].rearrange("(k p) n -> p k n", p=T)).then_inc(p_in, 16)
            with sp.Fori(0, NT) as t:
                sp.wait_ge(xn_moved, t + 1)
                sp.dma_start(xn_next[:, :], x1_d[ds(t * T + T, T), :]).then_inc(xn_in, 16)
                sp.wait_ge(y_ready, t + 1)
                sp.dma_start(y_p[ds(t * T, T), :], x2[:, :]).then_inc(y_out, 16)
                sp.dma_start(p_sb[:, :, :], p_t[:, ds(t * T + T, T)].rearrange("(k p) n -> p k n", p=T)
                             ).then_inc(p_in, 16)
                sp.wait_ge(y_out, t * 16 + 16)
                sp.dma_start(x2[:, :], x1_d[ds(t * T + T, T), :]).then_inc(x1_in, 16)
            sp.wait_ge(y_ready, NT + 1)
            sp.dma_start(y_s, x2[0:NS, :]).then_inc(y_out, 16)
            sp.wait_ge(y_out, 16 * (NT + 1))

        @block.gpsimd
        def _(pool):
            pool.memset(avs[0:T - NS, :], 0.0).then_inc(pad_zero, 1)
            pool.wait_ge(pad_zero, 1)
            for c in range(2):
                pool.dma_start(x1_d[SEQ + NS:SEQ + T, c * W4:(c + 1) * W4], avs[0:T - NS, :]
                               ).then_inc(k_out if c == 0 else pad_out, 16)
            with pool.Fori(0, NT // 2) as i:
                for par in range(2):
                    rows = ds(i * (2 * T) + par * T, T)
                    b, m = proj(i, par, K_)
                    hold(pool, pb_free[b], m + 2)
                    pool.dma_start(nk_p[rows, :], k_sb).then_inc(k_out, 16)
                    b, m = proj(i, par, V_)
                    hold(pool, pb_free[b], m + 2)
                    pool.dma_start(nv_p[rows, :], vals[:, ds(i * 2 + par, 1), :].rearrange(
                        "p a b -> p (a b)")).then_inc(v_out, 16)
                    for c in range(2):
                        b, m = proj(i, par, WO + c)
                        hold(pool, pb_free[b], m + 2)
                    pool.dma_start(x1_d[rows, :], xt[:, par, :]).then_inc(x1_out[par], 16)
            pool.dma_start(npool_p, u_sb[T - PAD:T, 1, :]).then_inc(new_rows_out, 16)
            b, m = proj(SI, 0, K_)
            pool.wait_ge(pb_free[b], m + 2)
            pool.dma_start(nk_s, k_sb[0:NS, :]).then_inc(k_out, 16)
            b, m = proj(SI, 0, V_)
            pool.wait_ge(pb_free[b], m + 2)
            pool.dma_start(nv_s, q_sb[0:NS, :]).then_inc(v_out, 16)
            b, m = proj(SI, 0, U_)
            pool.wait_ge(pb_free[b], m + 2)
            pool.dma_start(npool_s[:, PAD - DS:PAD, :], u_sb[0:NS, 0, :]).then_inc(new_rows_out, 16)
            pool.wait_ge(page_idx, 1)
            pool.wait_ge(av_done, H * NT + H)
            for n in range(2 * DB * NPG):
                if n >= RING:
                    pool.wait_ge(page_read, n - RING + 1)
                src = cache_k if n < DB * NPG else cache_v
                m = n % (DB * NPG)
                pool.indirect_dma_start(pages[:, n % RING, :], None, src,
                                        bass.IndirectOffsetOnAxis(ap=pidx[:, m:m + 1], axis=0)
                                        ).then_inc(page_in[n % RING], 16)
            for c in range(2):
                b, m = proj(SI, 0, WO + c)
                pool.wait_ge(pb_free[b], m + 2)
            pool.dma_start(x1_d[SEQ:SEQ + NS, :], xt[0:NS, 0, :]).then_inc(x1_out[0], 16)

            def gather(n, par, P):
                hold(pool, idx_ready, n + 1)
                for j in range(TOPK):
                    hold(pool, slot_free, n * TOPK + j + 1)
                    pool.indirect_dma_start(ring[0:P, j % RING, :], None, uv,
                                            bass.IndirectOffsetOnAxis(ap=idx[0:P, par, j:j + 1], axis=0)
                                            ).then_inc(gathered[j % RING], 16)

            with pool.Fori(0, NT * PH // 2) as s:
                gather(s * 2, 0, T)
                gather(s * 2 + 1, 1, T)
            with pool.Fori(NT * PH // 2, (NT + 1) * PH // 2) as s:
                gather(s * 2, 0, NS)
                gather(s * 2 + 1, 1, NS)

        @block.tensor
        def _(pe):
            for b in range(2):
                pe.sem_inc(pb_free[b], 1)
                pe.sem_inc(tb_free[b], 1)
            pe.wait_ge(const_in, 16 * 14)
            pe.wait_ge(gain_ready, 1)
            pe.wait_ge(onehot_in, 16)
            for h in range(H):
                if h >= 1:
                    pe.wait_ge(strip_sb, h)
                oh = mid[0:BUCKETS + 1, 0:2, 0:768]
                for c in range(4):
                    mm = pe.matmul(sc[:, c, 0:384], AT[0:BUCKETS + 1, h, :], oh[:, c // 2, (c % 2) * 384:(c % 2) * 384 + 384],
                                   start=True, stop=True)
                mm.then_inc(strip_ps, 1)

            def project(i, par, o, P=T):
                b, m = proj(i, par, o)
                pe.wait_ge(pb_free[b], m + 1)
                for k in range(KD):
                    mm = pe.matmul(pb[b][0:P, :], xT[:, k, 0:P], big[:, k, o * W4:(o + 1) * W4],
                                   start=(k == 0), stop=(k == KD - 1))
                mm.then_inc(pb_ready[b], 1)

            def turn4(bm, ins, rows=T, cols=T, P=T):
                b, m = bm
                pe.wait_ge(tb_free[b], m + 1)
                for c, v in enumerate(ins):
                    mm = pe.transpose(tb[b][0:rows, c * cols:(c + 1) * cols], v, ident[0:P, 0:P])
                mm.then_inc(tb_ready[b], 1)

            def w_out_(i, par, P=T):
                for c in range(2):
                    b, m = proj(i, par, WO + c)
                    pe.wait_ge(pb_free[b], m + 1)
                    for k in range(KD):
                        mm = pe.matmul(pb[b][0:P, :], xT[:, k, 0:P], mid[:, k, c * W4:(c + 1) * W4],
                                       start=(k == 0), stop=(k == KD - 1))
                    mm.then_inc(pb_ready[b], 1)

            def pool_out(i, par, P=T):
                b, m = proj(i, par, BAND)
                pe.wait_ge(pb_free[b], m + 2)
                b, m = proj(i, par, POOL)
                pe.wait_ge(pb_free[b], m + 1)
                for g in range(H):
                    mm = pe.matmul(pb[b][:, g * P:(g + 1) * P], pw[:, g, :], dT[:, g, 0:P],
                                   start=True, stop=True)
                mm.then_inc(pb_ready[b], 1)

            def tile(R, i, par):
                t = i * 2 + par
                nb = R.nb
                pe.wait_ge(x_in[par], i * 16 + 16)
                for c in range(2):
                    turn4(R.turn(i, par, c), [xt[:, par, (4 * c + k) * T:(4 * c + k + 1) * T] for k in range(4)])
                for c in range(2):
                    b, m = R.turn(i, par, c)
                    pe.wait_ge(tb_free[b], m + 2)
                for o in (Q_, K_, V_):
                    project(i, par, o)
                for o, src in ((Q_, q_sb), (K_, k_sb)):
                    b, m = proj(i, par, o)
                    pe.wait_ge(pb_free[b], m + 2)
                    turn4(R.turn(i, par, 2 + o), [src[:, h * T:(h + 1) * T] for h in range(H)])
                project(i, par, U_)
                for o in (2, 3):
                    b, m = R.turn(i, par, o)
                    pe.wait_ge(tb_free[b], m + 2)

                def scores(h):
                    for a in range(2):
                        pe.wait_ge(s_read[a], t * H + h + 1)
                        for c in range(nb):
                            mm = pe.matmul(sc[:, 2 * a + c, :], qT[a * QK:(a + 1) * QK, h, :],
                                           kT[a * QK:(a + 1) * QK, h, c * 512:(c + 1) * 512],
                                           start=True, stop=True)
                        mm.then_inc(s_ready[a], 1)

                def values(h):
                    pe.wait_ge(a_ready, t * H + h + 1)
                    for c in range(nb):
                        turn4(R.a_turn(i, par, h, c),
                              [S[:, h % 2, 0, (4 * c + k) * T:(4 * c + k + 1) * T] for k in range(4)])
                    bo, mo = proj(i, par, AV)
                    if h == 0:
                        pe.wait_ge(pb_free[bo], mo + 1)
                    for c in range(nb):
                        b, m = R.a_turn(i, par, h, c)
                        pe.wait_ge(tb_free[b], m + 2)
                        for k in range(4 * c, 4 * c + 4):
                            mm = pe.matmul(pb[bo][:, h * HV:(h + 1) * HV], AT[:, k, :],
                                           vals[:, k, h * HV:(h + 1) * HV],
                                           start=(k == 0), stop=(k == 4 * nb - 1))
                            if h == 0 and k == 0:
                                mm.then_inc(pb_ready[bo], 1)
                    mm.then_inc(av_done, 1)

                scores(0)
                b, m = proj(i, par, U_)
                pe.wait_ge(pb_free[b], m + 2)
                pe.wait_ge(band_in, t * 16 + 16)
                b, m = proj(i, par, BAND)
                pe.wait_ge(pb_free[b], m + 1)
                for g in range(H):
                    pe.matmul(pb[b][:, g * T:(g + 1) * T], u_sb[:, par, g * T:(g + 1) * T],
                              bandc[:, g, :], start=True, stop=False)
                    mm = pe.matmul(pb[b][:, g * T:(g + 1) * T], u_sb[:, 1 - par, g * T:(g + 1) * T],
                                   bandp[:, g, :], start=False, stop=True)
                mm.then_inc(pb_ready[b], 1)
                scores(1)
                pool_out(i, par)
                values(0)
                scores(2)
                values(1)
                scores(3)
                values(2)
                values(3)
                pe.wait_ge(o_norm, t + 1)
                turn4(R.o_turn(i, par), [avs[:, h * T:(h + 1) * T] for h in range(H)])
                b, m = proj(i, par, POOL)
                pe.wait_ge(pb_free[b], m + 2)
                b, m = R.o_turn(i, par)
                pe.wait_ge(tb_free[b], m + 2)
                w_out_(i, par)

            pe.wait_ge(w_in_in, 16 * 4)
            pe.wait_ge(w_out_in, 16 * 2)
            for R in REGIONS:
                with pe.Fori(R.first, R.last) as i:
                    for par in range(2):
                        tile(R, i, par)

            pe.wait_ge(x_in[0], 16 * (SI + 1))
            for c in range(2):
                turn4(s_turn(c), [xt[0:NS, 0, (4 * c + k) * T:(4 * c + k + 1) * T] for k in range(4)],
                      cols=NS, P=NS)
            for c in range(2):
                b, m = s_turn(c)
                pe.wait_ge(tb_free[b], m + 2)
            for o in (Q_, K_, V_, U_):
                project(SI, 0, o, NS)
            for o, src in ((Q_, q_sb), (K_, k_sb)):
                b, m = proj(SI, 0, o)
                pe.wait_ge(pb_free[b], m + 2)
                turn4(s_turn(2 + o), [src[0:NS, h * T:(h + 1) * T] for h in range(H)], cols=NS, P=NS)
            b, m = proj(SI, 0, U_)
            pe.wait_ge(pb_free[b], m + 2)
            pe.wait_ge(st_in, 16)
            b, m = proj(SI, 0, BAND)
            pe.wait_ge(pb_free[b], m + 1)
            for g in range(H):
                pe.matmul(pb[b][:, g * NS:(g + 1) * NS], u_sb[0:NS, 0, g * T:(g + 1) * T],
                          bs_c[:, g * NS:(g + 1) * NS], start=True, stop=False)
                mm = pe.matmul(pb[b][:, g * NS:(g + 1) * NS], st_sb[0:DB * PAD, g * T:(g + 1) * T],
                               bs_p[:, g * NS:(g + 1) * NS], start=False, stop=True)
            mm.then_inc(pb_ready[b], 1)
            pool_out(SI, 0, NS)
            for o in (2, 3):
                b, m = s_turn(o)
                pe.wait_ge(tb_free[b], m + 2)
            qs = qTs.rearrange("p (h n) -> p h n", h=H)
            ks = kTs.rearrange("p (h n) -> p h n", h=H)
            pe.wait_ge(s_read[0], H * NT + 1)
            pe.wait_ge(s_read[1], H * NT + 1)
            pq = pages.rearrange("p r (h n) -> p r h n", h=H)
            pk = pkT.rearrange("p r (h n) -> p r h n", h=H)

            def page_turn(n):
                pe.wait_ge(page_in[n % RING], 16 * (n // RING + 1))
                b, m = s_turn(S_PAGE + n)
                pe.wait_ge(tb_free[b], m + 1)
                for h in range(H):
                    mm = pe.transpose(tb[b][:, h * T:(h + 1) * T], pq[:, n % RING, h, :], ident[:, :])
                mm.then_inc(tb_ready[b], 1)

            def page_scores(n):
                bi, pg = n // NPG, n % NPG
                b, m = s_turn(S_PAGE + n)
                pe.wait_ge(tb_free[b], m + 2)
                for h in range(H):
                    for a in range(2):
                        at = pg * T + bi * 16 + h * DS
                        mm = pe.matmul(sc[:, a, at:at + DS], pk[a * QK:(a + 1) * QK, n % 2, h, :],
                                       qs[a * QK:(a + 1) * QK, h, bi * DS:(bi + 1) * DS],
                                       start=True, stop=True)
                mm.then_inc(page_read, 1)

            for n in range(DB * NPG):
                page_turn(n)
                if n >= 1:
                    page_scores(n - 1)
            page_scores(DB * NPG - 1)
            new = sc[0:NS, 2:4, 0:T].rearrange("p a (b h i) -> p a b h i", b=DB, h=H)
            for h in range(H):
                for a in range(2):
                    mm = pe.matmul(new[:, a, :, h, :], ks[a * QK:(a + 1) * QK, h, :],
                                   qs[a * QK:(a + 1) * QK, h, :].rearrange("p (b i) -> p b i", b=DB),
                                   start=True, stop=True)
            mm.then_inc(ss_ready, 1)
            pe.wait_ge(sT_ready, 1)
            for g in range(2):
                turn4(s_turn(S_ROW + g), [s_T[:, pg * 256 + g * T:pg * 256 + (g + 1) * T] for pg in range(NPG)])
            turn4(s_turn(S_ROW + 2), [s_Tn[0:NS, g * T:(g + 1) * T] for g in range(2)], cols=NS, P=NS)
            pe.wait_ge(sp_ready, 1)
            for g in range(2):
                turn4(s_turn(S_BACK + g), [s_row[:, g, pg * T:(pg + 1) * T] for pg in range(NPG)])
            turn4(s_turn(S_BACK + 2), [s_row[:, g, PAST:PAST + NS] for g in range(2)], rows=NS)
            for o in range(3):
                b, m = s_turn(S_BACK + o)
                pe.wait_ge(tb_free[b], m + 2)
            for bi in range(DB):
                for pg in range(NPG):
                    n = DB * NPG + bi * NPG + pg
                    pe.wait_ge(page_in[n % RING], 16 * (n // RING + 1))
                for h in range(H):
                    at = bi * 32 + h * 8
                    cols = lambda ap: ap.rearrange("p (b a h i) -> p b h a i", b=DB, a=2, h=H)[:, bi, h]
                    for pg in range(NPG):
                        n = DB * NPG + bi * NPG + pg
                        pe.matmul(sc[:, 3, at:at + 8], pq[:, n % RING, h, :],
                                  cols(pr_T[:, pg * 256:(pg + 1) * 256]), start=(pg == 0), stop=False)
                    mm = pe.matmul(sc[:, 3, at:at + 8], q_sb[0:NS, h * HV:(h + 1) * HV],
                                   cols(pr_Tn[0:NS, :]), start=False, stop=True)
                mm.then_inc(page_read, NPG)
            pe.wait_ge(o_sum, 1)
            b, m = proj(SI, 0, AV)
            pe.wait_ge(pb_free[b], m + 1)
            for h in range(H):
                mm = pe.transpose(pb[b][0:NS, h * T:(h + 1) * T], o_T[:, h * NS:(h + 1) * NS], ident[:, :])
                if h == 0:
                    mm.then_inc(pb_ready[b], 1)
            mm.then_inc(av_done, H)
            pe.wait_ge(o_norm, NT + 1)
            turn4(s_turn(S_O), [avs[0:NS, h * T:(h + 1) * T] for h in range(H)], cols=NS, P=NS)
            b, m = proj(SI, 0, POOL)
            pe.wait_ge(pb_free[b], m + 2)
            b, m = s_turn(S_O)
            pe.wait_ge(tb_free[b], m + 2)
            w_out_(SI, 0, NS)

            pe.wait_ge(keys_in, 16)
            for c in range(2):
                b, m = proj(SI, 0, WO + c)
                pe.wait_ge(pb_free[b], m + 2)
            for hp in range(2 * PH):
                pe.wait_ge(wq_in[hp % 2], 16 * (hp // 2 + 1))
                for c in range(2):
                    if hp >= 1:
                        pe.wait_ge(wk_kept[c], hp)
                    for k in range(4):
                        mm = pe.matmul(pb[c][:, k * NK:(k + 1) * NK],
                                       wq_st[:, hp % 2, (4 * c + k) * T:(4 * c + k + 1) * T],
                                       keys_sb[:, hp, :], start=True, stop=True)
                    mm.then_inc(wk_ready[c], 1)
            pe.sem_inc(slot_free, RING)
            pe.sem_inc(route_read, 1)

            def turn_xn(t):
                pe.wait_ge(xn_ready, t + 1)
                for c in range(2):
                    for k in range(4):
                        mm = pe.transpose(tb[c][:, k * T:(k + 1) * T],
                                          xn_next[:, (4 * c + k) * T:(4 * c + k + 1) * T], ident[:, :])
                    mm.then_inc(xn_turned, 1)
                pe.wait_ge(xnT_ready, t * 2 + 2)

            def route(n, h):
                pe.wait_ge(route_read, n + 1)
                for k in range(KD):
                    mm = pe.matmul(pb[0][:, 0:256], xnT[:, k, :], big[:, k, ds(h * 256, 256)],
                                   start=(k == 0), stop=(k == KD - 1))
                mm.then_inc(route_ready, 1)

            def add_values(n, P, first, last):
                for k in range(NB):
                    pe.wait_ge(diag_ready, n * NB + k + 1)
                    for j in range(k * B, (k + 1) * B):
                        end = last and j == TOPK - 1
                        for c in range(2):
                            mm = pe.matmul(sc[:, c, :], diag[0:P, j % RING, :],
                                           ring[0:P, j % RING, D + c * 512:D + (c + 1) * 512],
                                           start=first and j == 0, stop=end)
                        mm.then_inc(slot_free, 1)

            def gate(t):
                for c in range(2):
                    pe.wait_ge(x2_ready, t * 2 + c + 1)
                    for k in range(4):
                        mm = pe.transpose(tb[c][:, k * T:(k + 1) * T],
                                          x2[:, (4 * c + k) * T:(4 * c + k + 1) * T], ident[:, :])
                    mm.then_inc(x2_turned, 1)
                pe.wait_ge(p_in, t * 16 + 16)
                for c in range(2):
                    if c == 1:
                        pe.wait_ge(x2T_ready, t * 2 + 2)
                    for k in range(2):
                        mm = pe.matmul((pb[1], tb[1])[c][:, :], p_sb[:, k, :],
                                       wpl[:, k, c * W4:(c + 1) * W4], start=(k == 0), stop=(k == 1))
                    mm.then_inc(ple_ready, 1)
                for c in range(2):
                    for k in range(KD):
                        mm = pe.matmul(sc[:, 2 + c, :], x2T[:, k, :], mid[:, k, c * W4:(c + 1) * W4],
                                       start=(k == 0), stop=(k == KD - 1))
                    mm.then_inc(gate_ready, 1)

            def step(t, h, P, more=True):
                if h == PH - 1 and more:
                    turn_xn(t + 1)
                if h < PH - 1 or more:
                    route(t * PH + h + 1, (h + 1) % PH)
                add_values(t * PH + h, P, h == 0, h == PH - 1)

            def later_heads(t, P, more):
                with pe.Fori(1, PH // 2 - 1) as hh:
                    for par in range(2):
                        route(t * PH + hh * 2 + par + 1, hh * 2 + par + 1)
                        add_values(t * PH + hh * 2 + par, P, False, False)
                step(t, PH - 2, P)
                step(t, PH - 1, P, more)

            def turn_of_tile(t, P_next):
                later_heads(t, T, True)
                gate(t)
                for h in range(2):
                    step(t + 1, h, P_next)

            pe.wait_ge(wk_kept[0], 2 * PH)
            pe.wait_ge(wk_kept[1], 2 * PH)
            turn_xn(0)
            route(0, 0)
            for h in range(2):
                step(0, h, T)
            pe.wait_ge(gate_w_in, 32)
            pe.wait_ge(g_in, 16 * 5)
            with pe.Fori(0, NT - 1) as t:
                turn_of_tile(t, T)
            turn_of_tile(NT - 1, NS)
            later_heads(NT, NS, False)
            gate(NT)

        @block.scalar
        def _(act):
            act.wait_ge(lam_sum, 2)
            act.activation(st[:, LAME:LAME + 2], st[:, LAMS:LAMS + 2], ACT.Exp).then_inc(lam_exp, 1)
            for h in range(H):
                act.wait_ge(strip_ps, h + 1)
                if h >= 2:
                    act.wait_ge(strip_out[h % 2], 16 * (h // 2))
                act.activation(S[:, h % 2, :, :].rearrange("p a b -> p (a b)")[:, 0:STRIP].rearrange(
                    "p (a b) -> p a b", b=384), sc[:, :, 0:384], ACT.Copy).then_inc(strip_sb, 1)

            def tile(R, i, par):
                t = i * 2 + par
                nb = R.nb
                act.wait_ge(x_sq, t + 1)
                act.activation(st[:, XRT + par:XRT + par + 1], st[:, XSS + par:XSS + par + 1], ACT.Sqrt,
                               ).then_inc(x_root, 1)
                act.wait_ge(x_norm, t + 1)

                def evac(o, dst, stand_alone=False):
                    b, m = proj(i, par, o)
                    if stand_alone:
                        hold(act, pb_ready[b], m + 1)
                    else:
                        act.wait_ge(pb_ready[b], m + 1)
                    act.activation(dst, pb[b][:, :], ACT.Copy, scale=st[:, XR + par:XR + par + 1]
                                   ).then_inc(pb_free[b], 1)

                evac(Q_, q_sb)
                act.wait_ge(k_out, t * 16 + 16)
                evac(K_, k_sb)
                evac(V_, vals[:, ds(t, 1), :].rearrange("p a b -> p (a b)"), True)
                b, m = R.turn(i, par, 2)
                act.wait_ge(tb_ready[b], m + 1)
                act.activation(qT, tb[b][:, :].rearrange("p (a b) -> p a b", a=H), ACT.Copy
                               ).then_inc(tb_free[b], 1)
                b, m = R.turn(i, par, 3)
                hold(act, tb_ready[b], m + 1)
                act.activation(kT[:, :, ds(t * T, T)], tb[b][:, :].rearrange("p (a b) -> p a b", a=H),
                               ACT.Copy).then_inc(tb_free[b], 1)
                evac(U_, u_sb[:, par, :])

                def exps(h):
                    for a in range(2):
                        act.wait_ge(s_max[a], t * H + h + 1)
                        row_ = S[:, h % 2, a, 0:R.width]
                        col = 2 * (h % 2) + a
                        act.activation(row_, row_, ACT.Exp, bias=st[:, NMAX + col:NMAX + col + 1],
                                       accum_out=st[:, LSUM + col:LSUM + col + 1]).then_inc(s_exp[a], 1)

                def weights(h):
                    act.wait_ge(av_done, t * H + h + H)
                    for c in range(nb):
                        b, m = R.a_turn(i, par, h, c)
                        act.wait_ge(tb_ready[b], m + 1)
                        act.activation(AT[:, 4 * c:4 * c + 4, :], tb[b][:, :].rearrange("p (a b) -> p a b", a=4),
                                       ACT.Copy).then_inc(tb_free[b], 1)

                exps(0)
                b, m = proj(i, par, BAND)
                act.wait_ge(pb_ready[b], m + 1)
                act.activation(dT, pb[b][:, :].rearrange("p (a b) -> p a b", a=H), ACT.Copy
                               ).then_inc(pb_free[b], 1)
                exps(1)
                weights(0)
                exps(2)
                weights(1)
                exps(3)
                weights(2)
                weights(3)
                act.wait_ge(av_done, t * H + 2 * H)
                b, m = proj(i, par, AV)
                act.activation(avs[:, :], pb[b][:, :], ACT.Copy).then_inc(pb_free[b], 1)
                act.wait_ge(o_sq, t + 1)
                act.activation(st[:, ORT:ORT + H], st[:, OSS:OSS + H], ACT.Sqrt).then_inc(o_root, 1)

            act.wait_ge(zeroed, 1)
            act.wait_ge(pad_out, 16)
            act.wait_ge(k_out, 16)
            for R in REGIONS:
                with act.Fori(R.first, R.last) as i:
                    for par in range(2):
                        tile(R, i, par)

            act.wait_ge(x_sq, NT + 1)
            act.activation(st[0:NS, XRT:XRT + 1], st[0:NS, XSS:XSS + 1], ACT.Sqrt).then_inc(x_root, 1)
            act.wait_ge(x_norm, NT + 1)
            for o, dst in ((Q_, q_sb), (K_, k_sb), (V_, q_sb), (U_, u_sb[:, 0, :])):
                b, m = proj(SI, 0, o)
                act.wait_ge(pb_ready[b], m + 1)
                if o == K_:
                    act.wait_ge(k_out, 16 * NT + 16)
                if o == V_:
                    bt, mt = s_turn(2)
                    act.wait_ge(tb_ready[bt], mt + 1)
                act.activation(dst[0:NS, :], pb[b][0:NS, :], ACT.Copy, scale=st[0:NS, XR:XR + 1]
                               ).then_inc(pb_free[b], 1)
                if o == K_:
                    act.wait_ge(av_done, H * NT + H)
                    act.wait_ge(s_read[0], H * NT + 1)
                    for oo, dd in ((2, qTs),):
                        bt, mt = s_turn(oo)
                        act.wait_ge(tb_ready[bt], mt + 1)
                        act.activation(dd, tb[bt][:, 0:H * NS], ACT.Copy).then_inc(tb_free[bt], 1)
            bt, mt = s_turn(3)
            act.wait_ge(tb_ready[bt], mt + 1)
            act.activation(kTs, tb[bt][:, 0:H * NS], ACT.Copy).then_inc(tb_free[bt], 1)
            b, m = proj(SI, 0, BAND)
            act.wait_ge(pb_ready[b], m + 1)
            act.activation(dT[:, :, 0:NS], pb[b][:, 0:H * NS].rearrange("p (a b) -> p a b", a=H), ACT.Copy
                           ).then_inc(pb_free[b], 1)
            for n in range(DB * NPG):
                b, m = s_turn(S_PAGE + n)
                act.wait_ge(tb_ready[b], m + 1)
                if n >= 2:
                    act.wait_ge(page_read, n - 1)
                act.activation(pkT[:, n % 2, :], tb[b][:, :], ACT.Copy).then_inc(tb_free[b], 1)
            act.wait_ge(sx_ready, 2)
            for g in range(2):
                act.activation(s_row[:, g, :], s_row[:, g, :], ACT.Exp, bias=st[:, SMX + g:SMX + g + 1],
                               accum_out=st[:, SSUM + g:SSUM + g + 1]).then_inc(sx_exp, 1)
            for g in range(2):
                b, m = s_turn(S_BACK + g)
                act.wait_ge(tb_ready[b], m + 1)
                act.activation(pr_T.rearrange("p (a b) -> p a b", a=NPG)[:, :, g * T:(g + 1) * T],
                               tb[b][:, :].rearrange("p (a b) -> p a b", a=NPG), ACT.Copy
                               ).then_inc(tb_free[b], 1)
            b, m = s_turn(S_BACK + 2)
            act.wait_ge(tb_ready[b], m + 1)
            act.activation(pr_Tn[0:NS, :], tb[b][0:NS, 0:256], ACT.Copy).then_inc(tb_free[b], 1)
            act.wait_ge(av_done, H * NT + 2 * H)
            b, m = proj(SI, 0, AV)
            act.activation(avs[0:NS, :], pb[b][0:NS, :], ACT.Copy).then_inc(pb_free[b], 1)
            act.wait_ge(o_sq, NT + 1)
            act.activation(st[0:NS, ORT:ORT + H], st[0:NS, OSS:OSS + H], ACT.Sqrt).then_inc(o_root, 1)

            for hp in range(2 * PH):
                act.wait_ge(wk_ready[0], hp + 1)
                act.activation(big[:, 0:4, hp * NK:(hp + 1) * NK],
                               pb[0][:, :].rearrange("p (a b) -> p a b", a=4), ACT.Copy
                               ).then_inc(wk_kept[0], 1)

            def norm_next(t):
                act.wait_ge(xn_sq, t + 1)
                act.activation(gst[:, RT1:RT1 + 1], gst[:, NS1:NS1 + 1], ACT.Sqrt).then_inc(xn_root, 1)
                for c in range(2):
                    act.wait_ge(xn_turned, t * 2 + c + 1)
                    act.activation(xnT[:, 4 * c:4 * c + 4, :], tb[c][:, :].rearrange("p (a b) -> p a b", a=4),
                                   ACT.Copy).then_inc(xnT_ready, 1)

            def gates(n, par):
                act.wait_ge(top_ready, n + 1)
                act.activation(ex[:, par, :], top2[:, :], ACT.Exp, bias=gst[:, NTOP + par:NTOP + par + 1],
                               accum_out=gst[:, ESUM + par:ESUM + par + 1]).then_inc(top_exp, 1)

            def gelu(n, par, P, k):
                act.wait_ge(dots_done, n * NB + k + 1)
                act.activation(hgelu[0:P, par, k * B:(k + 1) * B], hdot[0:P, par, k * B:(k + 1) * B],
                               ACT.Gelu).then_inc(gelu_done, 1)

            def step(n, par, P, more=True, tile_next=None, tile_last=None):
                gelu(n, par, P, 0)
                if tile_next is not None:
                    norm_next(tile_next)
                if more:
                    gates(n + 1, 1 - par)
                for k in range(1, NB):
                    gelu(n, par, P, k)
                    if k == 5 and tile_last is not None:
                        gate(tile_last, n)

            def close_sum(t):
                act.wait_ge(x2_sq, t + 1)
                act.activation(gst[:, RT2:RT2 + 1], gst[:, NS2:NS2 + 1], ACT.Sqrt).then_inc(x2_root, 1)

            def gate(t, n=None):
                act.wait_ge(r2_ready, t + 1)
                if n is not None:
                    act.wait_ge(idx_ready, n + 2)
                for c in range(2):
                    hold(act, gate_ready, t * 2 + c + 1)
                    act.wait_ge(sig_read, t * 2 + c + 1)
                    act.activation(sg[:, :], sc[:, 2 + c, :], ACT.Sigmoid, scale=gst[:, R2:R2 + 1]
                                   ).then_inc(sig_ready, 1)
                act.wait_ge(y_sq, t + 1)
                act.activation(gst[:, RT3:RT3 + 1], gst[:, NS3:NS3 + 1], ACT.Sqrt).then_inc(y_root, 1)

            def later_heads(t, P, more):
                with act.Fori(1, PH // 2 - 1) as hh:
                    for par in range(2):
                        step(t * PH + hh * 2 + par, par, P)
                step(t * PH + PH - 2, 0, P)
                step(t * PH + PH - 1, 1, P, more, t + 1 if more else None)
                close_sum(t)

            def turn_of_tile(t, P_next):
                later_heads(t, T, True)
                step((t + 1) * PH, 0, P_next, tile_last=t)
                step((t + 1) * PH + 1, 1, P_next)

            norm_next(0)
            gates(0, 0)
            for h in range(2):
                step(h, h, T)
            with act.Fori(0, NT - 1) as t:
                turn_of_tile(t, T)
            turn_of_tile(NT - 1, NS)
            later_heads(NT, NS, False)
            gate(NT)

        @block.vector
        def _(dve):
            for a in range(2):
                dve.sem_inc(s_read[a], 1)
            dve.sem_inc(av_done, H)
            dve.sem_inc(sig_read, 1)
            dve.sem_inc(top_exp, 1)
            dve.memset(relb[BUCKETS:BUCKETS + 1, :], NEG)
            dve.memset(kT, 0.0)
            dve.memset(vals, 0.0)
            dve.memset(u_sb[:, 1, :], 0.0).then_inc(zeroed, 1)
            dve.drain()
            dve.wait_ge(const_in, 16 * 14)
            dve.tensor_copy(AT[0:BUCKETS, 0:H, :],
                            relb[0:BUCKETS, :].unsqueeze(2).to_broadcast([BUCKETS, H, T]))
            dve.tensor_copy(AT[BUCKETS:BUCKETS + 1, 0:H, :],
                            relb[BUCKETS:BUCKETS + 1, :].unsqueeze(2).to_broadcast([1, H, T])
                            ).then_inc(gain_ready, 1)
            for a in range(2):
                dve.tensor_tensor_reduce(lam_in[:, 2 * a, :], lam_in[:, 2 * a, :], lam_in[:, 2 * a + 1, :],
                                         1.0, 0.0, ALU.mult, ALU.add, st[:, LAMS + a:LAMS + a + 1]
                                         ).then_inc(lam_sum, 1)
            dve.tensor_scalar(g_sub[:, :], g_sub[:, :], 1.0 - LAM_INIT, None, ALU.mult)
            dve.tensor_copy(pagef, ptab[:, :])
            dve.drain()
            dve.tensor_scalar(pidx[:, :], pagef, float(PAGE), row[:, 0:1], ALU.mult, ALU.add
                              ).then_inc(page_idx, 1)
            dve.wait_ge(lam_exp, 1)
            dve.tensor_tensor(st[:, NLAM:NLAM + 1], st[:, LAME + 1:LAME + 2], st[:, LAME:LAME + 1],
                              ALU.subtract)
            dve.drain()
            dve.tensor_scalar(st[:, NLAM:NLAM + 1], st[:, NLAM:NLAM + 1], LAM_INIT, None, ALU.subtract)
            dve.wait_ge(bias_in, 16)
            dve.tensor_copy(far[:, :], biasw[:, :, 0])

            def mean_eps(cols, width):
                dve.drain()
                return dve.tensor_scalar(cols, cols, 1.0 / width, EPS, ALU.mult, ALU.add)

            def x_stats(i, par, P=T):
                dve.wait_ge(x_in[par], i * 16 + 16)
                dve.tensor_tensor_reduce(sq[0:P, :], xt[0:P, par, :], xt[0:P, par, :], 1.0, 0.0,
                                         ALU.mult, ALU.add, st[0:P, XSS + par:XSS + par + 1])
                mean_eps(st[0:P, XSS + par:XSS + par + 1], D).then_inc(x_sq, 1)

            def x_turned(turn, P=T):
                for c in range(2):
                    b, m = turn(c)
                    dve.wait_ge(tb_ready[b], m + 1)
                    dve.tensor_tensor(xT[:, 4 * c:4 * c + 4, 0:P],
                                      tb[b][:, 0:4 * P].rearrange("p (a b) -> p a b", a=4),
                                      g_attn[:, 4 * c:4 * c + 4].unsqueeze(2).to_broadcast([T, 4, P]),
                                      ALU.mult).then_inc(tb_free[b], 1)

            def x_factor(t, par, P=T):
                dve.wait_ge(x_root, t + 1)
                dve.reciprocal(st[0:P, XR + par:XR + par + 1], st[0:P, XRT + par:XRT + par + 1]
                               ).then_inc(x_norm, 1)

            def pooled(i, par, P=T):
                b, m = proj(i, par, POOL)
                dve.wait_ge(pb_ready[b], m + 1)
                dve.tensor_tensor(xT[:, H:2 * H, 0:P], pb[b][:, 0:H * P].rearrange("p (a b) -> p a b", a=H),
                                  psc[:, :].unsqueeze(2).to_broadcast([T, H, P]), ALU.mult
                                  ).then_inc(pb_free[b], 1)

            def normed_heads(i, par, t, P=T):
                b, m = proj(i, par, AV)
                dve.wait_ge(pb_free[b], m + 2)
                dve.tensor_tensor(sq[0:P, 0:W4], avs[0:P, :], avs[0:P, :], ALU.mult)
                dve.drain()
                dve.tensor_reduce(st[0:P, OSS:OSS + H], sq[0:P, 0:W4].rearrange("p (h d) -> p h d", h=H),
                                  AX.X, ALU.add)
                mean_eps(st[0:P, OSS:OSS + H], HV).then_inc(o_sq, 1)
                dve.wait_ge(o_root, t + 1)
                dve.reciprocal(st[0:P, OREC:OREC + H], st[0:P, ORT:ORT + H])
                dve.drain()
                av = avs[0:P, :].rearrange("p (h d) -> p h d", h=H)
                dve.tensor_tensor(av, av, st[0:P, OREC:OREC + H].unsqueeze(2).to_broadcast([P, H, HV]),
                                  ALU.mult).then_inc(o_norm, 1)

            def finish(i, par, turn, P=T):
                b, m = turn
                dve.wait_ge(tb_ready[b], m + 1)
                dve.tensor_scalar(xT[:, 0:H, 0:P], tb[b][:, 0:H * P].rearrange("p (a b) -> p a b", a=H),
                                  g_sub[:, 0:1], None, ALU.mult).then_inc(tb_free[b], 1)
                for c in range(2):
                    b, m = proj(i, par, WO + c)
                    dve.wait_ge(pb_ready[b], m + 1)
                    cols = slice(c * W4, (c + 1) * W4)
                    dve.tensor_tensor(xt[0:P, par, cols], pb[b][0:P, :], xt[0:P, par, cols], ALU.add
                                      ).then_inc(pb_free[b], 1)

            def tile(R, i, par):
                t = i * 2 + par
                W = R.width
                x_stats(i, par)
                x_turned(lambda c: R.turn(i, par, c))
                x_factor(t, par)

                def scores(h):
                    if h >= 2:
                        hold(dve, av_done, t * H + h - 1 + H)
                    for a in range(2):
                        hold(dve, s_ready[a], t * H + h + 1)
                        dve.scalar_tensor_tensor(
                            out=S[:, h % 2, a, 0:W],
                            in0=sc[:, 2 * a:2 * a + R.nb, :].rearrange("p a b -> p (a b)"), scalar=SCALE,
                            in1=biasw[:, h, ds((NT - 1) * T - t * T, W)],
                            op0=ALU.mult, op1=ALU.add).then_inc(s_read[a], 1)
                    dve.drain()
                    for a in range(2):
                        col = NMAX + 2 * (h % 2) + a
                        dve.tensor_reduce(st[:, col:col + 1], S[:, h % 2, a, 0:W], AX.X, ALU.max,
                                          negate=True).then_inc(s_max[a], 1)

                def combine(h):
                    q = h % 2
                    for a in range(2):
                        dve.wait_ge(s_exp[a], t * H + h + 1)
                    c = LREC + 2 * q
                    dve.reciprocal(st[:, c:c + 2], st[:, LSUM + 2 * q:LSUM + 2 * q + 2])
                    dve.drain()
                    dve.tensor_tensor(st[:, c + 1:c + 2], st[:, c + 1:c + 2], st[:, NLAM:NLAM + 1], ALU.mult)
                    dve.tensor_scalar(S[:, q, 0, 0:W], S[:, q, 0, 0:W], st[:, c:c + 1], None, ALU.mult)
                    dve.drain()
                    dve.scalar_tensor_tensor(out=S[:, q, 0, 0:W], in0=S[:, q, 1, 0:W],
                                             scalar=st[:, c + 1:c + 2], in1=S[:, q, 0, 0:W],
                                             op0=ALU.mult, op1=ALU.add).then_inc(a_ready, 1)

                scores(0)
                scores(1)
                combine(0)
                pooled(i, par)
                scores(2)
                combine(1)
                scores(3)
                combine(2)
                combine(3)
                normed_heads(i, par, t)
                finish(i, par, R.o_turn(i, par))

            for R in REGIONS:
                with dve.Fori(R.first, R.last) as i:
                    for par in range(2):
                        tile(R, i, par)

            x_stats(SI, 0, NS)
            x_turned(s_turn, NS)
            x_factor(NT, 0, NS)
            dve.wait_ge(bT_in, 16 * H * (DB + 1))
            dve.tensor_copy(bf_T.rearrange("p (h i) -> p h i", h=H),
                            far[:, :].unsqueeze(2).to_broadcast([T, H, DS]))
            pooled(SI, 0, NS)
            dve.drain()
            dve.wait_ge(ss_ready, 1)
            rows8 = lambda ap: ap.rearrange("p (b c) -> p b c", b=DB)
            per_b = lambda ap: ap.unsqueeze(1).to_broadcast([ap.shape[0], DB, H * DS])
            for a in range(2):
                half_a = slice(a * H * DS, (a + 1) * H * DS)
                for pg in range(NPG):
                    dve.scalar_tensor_tensor(
                        out=rows8(s_T[:, pg * 256:(pg + 1) * 256])[:, :, half_a],
                        in0=rows8(sc[:, a, pg * T:(pg + 1) * T]), scalar=SCALE,
                        in1=per_b(b_raw if pg == NPG - 1 else bf_T), op0=ALU.mult, op1=ALU.add)
                dve.scalar_tensor_tensor(
                    out=rows8(s_Tn[0:NS, :])[:, :, half_a], in0=rows8(sc[0:NS, 2 + a, 0:T]), scalar=SCALE,
                    in1=per_b(bx_raw[0:NS, :]), op0=ALU.mult, op1=ALU.add)
            dve.drain()
            dve.tensor_tensor(rows8(s_Tn[0:NS, :]), rows8(s_Tn[0:NS, :]),
                              mask_s[:, :].unsqueeze(2).to_broadcast([NS, DB, 32]), ALU.add
                              ).then_inc(sT_ready, 1)
            for g in range(2):
                b, m = s_turn(S_ROW + g)
                dve.wait_ge(tb_ready[b], m + 1)
                dve.tensor_copy(s_row[:, g, 0:PAST], tb[b][:, :]).then_inc(tb_free[b], 1)
            b, m = s_turn(S_ROW + 2)
            dve.wait_ge(tb_ready[b], m + 1)
            dve.tensor_copy(s_row[:, :, PAST:PAST + NS], tb[b][:, 0:2 * NS].rearrange("p (g n) -> p g n", g=2)
                            ).then_inc(tb_free[b], 1)
            dve.drain()
            for g in range(2):
                dve.tensor_reduce(st[:, SMX + g:SMX + g + 1], s_row[:, g, :], AX.X, ALU.max, negate=True
                                  ).then_inc(sx_ready, 1)
            dve.wait_ge(sx_exp, 2)
            dve.reciprocal(st[:, SREC:SREC + 2], st[:, SSUM:SSUM + 2])
            dve.tensor_scalar(st[:, SCO:SCO + 1], half[:, 1:2], st[:, NLAM:NLAM + 1], None, ALU.mult)
            dve.drain()
            dve.tensor_tensor(st[:, SCO:SCO + 1], st[:, SCO:SCO + 1], half[:, 0:1], ALU.add)
            dve.drain()
            dve.tensor_scalar(st[:, SREC:SREC + 2], st[:, SREC:SREC + 2], st[:, SCO:SCO + 1], None, ALU.mult)
            dve.drain()
            dve.tensor_tensor(s_row, s_row, st[:, SREC:SREC + 2].unsqueeze(2).to_broadcast([T, 2, 544]),
                              ALU.mult).then_inc(sp_ready, 1)
            dve.wait_ge(page_read, 2 * DB * NPG)
            dve.tensor_copy(o_ps, sc[:, 3, 0:256])
            dve.drain()
            ov = o_ps.rearrange("p (b h a i) -> p b h a i", b=DB, h=H, a=2)
            dve.tensor_tensor(o_T.rearrange("p (h b i) -> p b h i", h=H, b=DB), ov[:, :, :, 0, :],
                              ov[:, :, :, 1, :], ALU.add).then_inc(o_sum, 1)
            normed_heads(SI, 0, NT, NS)
            finish(SI, 0, s_turn(S_O), NS)

            for hp in range(2 * PH):
                dve.wait_ge(wk_ready[1], hp + 1)
                dve.tensor_copy(big[:, 4:8, hp * NK:(hp + 1) * NK],
                                pb[1][:, :].rearrange("p (a b) -> p a b", a=4)).then_inc(wk_kept[1], 1)

            def norm_next(t):
                dve.wait_ge(xn_in, t * 16 + 16)
                dve.tensor_tensor_reduce(junk, xn_next[:, :], xn_next[:, :], 1.0, 0.0, ALU.mult,
                                         ALU.add, gst[:, NS1:NS1 + 1])
                mean_eps(gst[:, NS1:NS1 + 1], D).then_inc(xn_sq, 1)
                dve.wait_ge(xn_root, t + 1)
                dve.reciprocal(gst[:, R1:R1 + 1], gst[:, RT1:RT1 + 1])
                dve.drain()
                dve.scalar_tensor_tensor(out=xn_next[:, :], in0=xn_next[:, :], scalar=gst[:, R1:R1 + 1],
                                         in1=g_ffn[:, :], op0=ALU.mult, op1=ALU.mult).then_inc(xn_ready, 1)

            def choose(n, par):
                dve.wait_ge(route_ready, n + 1)
                dve.tensor_copy(sc_sb[:, :], pb[0][:, 0:256]).then_inc(route_read, 1)
                dve.drain()
                seg = [slice(s * NK, (s + 1) * NK) for s in range(2)]
                for s in range(2):
                    dve.max(top1[:, s, 0:8], sc_sb[:, seg[s]])
                dve.drain()
                for s in range(2):
                    dve.match_replace(sc_lo[:, seg[s]], top1[:, s, 0:8], sc_sb[:, seg[s]], FMAX)
                    dve.max_index(ind1[:, s, 0:8], top1[:, s, 0:8], sc_sb[:, seg[s]])
                dve.drain()
                for s in range(2):
                    dve.max(top1[:, s, 8:16], sc_lo[:, seg[s]])
                dve.drain()
                pairs = lambda ap: ap.rearrange("p (i j) -> p i j", i=TOPK)
                over_j = lambda ap: ap.unsqueeze(2).to_broadcast([T, TOPK, TOPK])
                over_i = lambda ap: ap.unsqueeze(1).to_broadcast([T, TOPK, TOPK])
                dve.tensor_tensor(pairs(cand[:, :]), over_j(top1[:, 0, :]), over_i(top1[:, 1, :]), ALU.add)
                for s in range(2):
                    dve.max_index(ind1[:, s, 8:16], top1[:, s, 8:16], sc_lo[:, seg[s]])
                hold(dve, top_exp, n + 1)
                dve.drain()
                dve.max(top2[:, 0:8], cand[:, :])
                dve.drain()
                dve.match_replace(cand_lo[:, :], top2[:, 0:8], cand[:, :], FMAX)
                dve.max_index(ind2[:, 0:8], top2[:, 0:8], cand[:, :])
                dve.drain()
                dve.max(top2[:, 8:16], cand_lo[:, :])
                dve.tensor_scalar(gst[:, NTOP + par:NTOP + par + 1], top2[:, 0:1], -1.0, None, ALU.mult
                                  ).then_inc(top_ready, 1)
                dve.tensor_copy(ind1f[:, :, :], ind1[:, :, :])
                dve.drain()
                dve.max_index(ind2[:, 8:16], top2[:, 8:16], cand_lo[:, :])
                dve.drain()
                dve.tensor_scalar(ab[:, 0, :], ind2[:, :], 4, None, ALU.logical_shift_right)
                dve.tensor_scalar(ab[:, 1, :], ind2[:, :], 15, None, ALU.bitwise_and)
                dve.drain()
                dve.tensor_copy(abf[:, :, :], ab[:, :, :])
                dve.drain()
                tmp = (cand, cand_lo)
                for s in range(2):
                    dve.tensor_tensor(pairs(tmp[s][:, :]), over_j(abf[:, s, :]), over_i(iota[:, :]),
                                      ALU.is_equal)
                dve.drain()
                for s in range(2):
                    dve.tensor_tensor(pairs(tmp[s][:, :]), pairs(tmp[s][:, :]), over_i(ind1f[:, s, :]),
                                      ALU.mult)
                dve.drain()
                for s in range(2):
                    dve.tensor_reduce(pick[:, s, :], pairs(tmp[s][:, :]), AX.X, ALU.add)
                dve.drain()
                dve.scalar_tensor_tensor(out=idx[:, par, :], in0=pick[:, 0, :], scalar=float(NK),
                                         in1=pick[:, 1, :], op0=ALU.mult, op1=ALU.add).then_inc(idx_ready, 1)

            def gates(n, par):
                dve.wait_ge(top_exp, n + 2)
                dve.reciprocal(gst[:, EREC + par:EREC + par + 1], gst[:, ESUM + par:ESUM + par + 1])
                dve.drain()
                dve.tensor_scalar(gate[:, par, :], ex[:, par, :], gst[:, EREC + par:EREC + par + 1], None,
                                  ALU.mult)

            def dots(n, par, P, k):
                for j in range(k * B, (k + 1) * B):
                    r = j % RING
                    dve.wait_ge(gathered[r], n * 32 + (j // RING) * 16 + 16)
                    ins = dve.tensor_tensor_reduce(ring[0:P, r, 0:D], ring[0:P, r, 0:D], xn_cur[0:P, :],
                                                   1.0, 0.0, ALU.mult, ALU.add, hdot[0:P, par, j:j + 1])
                ins.then_inc(dots_done, 1)

            def coefficients(n, par, P, k):
                dve.wait_ge(gelu_done, n * NB + k + 1)
                hold(dve, slot_free, n * TOPK + (k + 1) * B)
                for j in range(k * B, (k + 1) * B):
                    ins = dve.tensor_scalar(diag[0:P, j % RING, :], ident[0:P, :],
                                            hgelu[0:P, par, j:j + 1], gate[0:P, par, j:j + 1],
                                            ALU.mult, ALU.mult)
                ins.then_inc(diag_ready, 1)

            def step(n, par, P, more=True, tile_next=None, tile_last=None):
                for k in range(NB):
                    dots(n, par, P, k)
                    coefficients(n, par, P, k)
                    if k == 0:
                        if tile_next is not None:
                            norm_next(tile_next)
                        if more:
                            choose(n + 1, 1 - par)
                    if k == 4 and more:
                        gates(n + 1, 1 - par)
                    if k == 5 and tile_last is not None:
                        gate_and_embed(tile_last)

            def close_sum(t):
                dve.wait_ge(x1_in, t * 16 + 16)
                hold(dve, slot_free, t * (PH * TOPK) + PH * TOPK + RING)
                for c in range(2):
                    half_c = slice(c * W4, (c + 1) * W4)
                    dve.tensor_tensor(x2[:, half_c], x2[:, half_c], sc[:, c, :], ALU.add).then_inc(x2_ready, 1)
                for c in range(2):
                    dve.wait_ge(x2_turned, t * 2 + c + 1)
                    dve.tensor_tensor(x2T[:, 4 * c:4 * c + 4, :],
                                      tb[c][:, :].rearrange("p (a b) -> p a b", a=4),
                                      g_pl[:, 4 * c:4 * c + 4].unsqueeze(2).to_broadcast([T, 4, T]),
                                      ALU.mult).then_inc(x2T_ready, 1)
                dve.tensor_tensor_reduce(junk, x2[:, :], x2[:, :], 1.0, 0.0, ALU.mult, ALU.add,
                                         gst[:, NS2:NS2 + 1])
                mean_eps(gst[:, NS2:NS2 + 1], D).then_inc(x2_sq, 1)
                dve.wait_ge(x2_root, t + 1)
                dve.reciprocal(gst[:, R2:R2 + 1], gst[:, RT2:RT2 + 1]).then_inc(r2_ready, 1)

            def open_tile():
                dve.tensor_copy(xn_cur[:, :], xn_next[:, :]).then_inc(xn_moved, 1)
                dve.drain()

            def gate_and_embed(t):
                for c in range(2):
                    half_c = slice(c * W4, (c + 1) * W4)
                    hold(dve, sig_ready, t * 2 + c + 1)
                    dve.wait_ge(ple_ready, t * 2 + c + 1)
                    dve.tensor_tensor(sg[:, :], sg[:, :], (pb[1], tb[1])[c][:, :], ALU.mult
                                      ).then_inc(ple_read, 1)
                    dve.drain()
                    dve.tensor_tensor(x2[:, half_c], x2[:, half_c], sg[:, :], ALU.add).then_inc(sig_read, 1)
                dve.drain()
                dve.tensor_tensor_reduce(junk, x2[:, :], x2[:, :], 1.0, 0.0, ALU.mult, ALU.add,
                                         gst[:, NS3:NS3 + 1])
                mean_eps(gst[:, NS3:NS3 + 1], D).then_inc(y_sq, 1)
                dve.wait_ge(y_root, t + 1)
                dve.reciprocal(gst[:, R3:R3 + 1], gst[:, RT3:RT3 + 1])
                dve.drain()
                dve.scalar_tensor_tensor(out=x2[:, :], in0=x2[:, :], scalar=gst[:, R3:R3 + 1],
                                         in1=g_fin[:, :], op0=ALU.mult, op1=ALU.mult).then_inc(y_ready, 1)

            def later_heads(t, P, more):
                with dve.Fori(1, PH // 2 - 1) as hh:
                    for par in range(2):
                        step(t * PH + hh * 2 + par, par, P)
                step(t * PH + PH - 2, 0, P)
                step(t * PH + PH - 1, 1, P, more, t + 1 if more else None)
                close_sum(t)

            def turn_of_tile(t, P_next):
                later_heads(t, T, True)
                open_tile()
                step((t + 1) * PH, 0, P_next, tile_last=t)
                step((t + 1) * PH + 1, 1, P_next)

            dve.wait_ge(g_in, 16 * 5)
            norm_next(0)
            choose(0, 0)
            gates(0, 0)
            dve.drain()
            open_tile()
            for h in range(2):
                step(h, h, T)
            with dve.Fori(0, NT - 1) as t:
                turn_of_tile(t, T)
            turn_of_tile(NT - 1, NS)
            later_heads(NT, NS, False)
            gate_and_embed(NT)


def onehot_buckets():
    n = SPAN + T - 1 - np.arange(STRIP)
    exact = BUCKETS // 2
    pos = np.maximum(n, 1).astype(np.float32) / np.float32(exact)
    large = exact + (np.log(pos) / np.float32(np.log(MAX_DIST / exact)) * np.float32(BUCKETS - exact)
                     ).astype(np.int32)
    bucket = np.where(n < exact, n, np.minimum(large, BUCKETS - 1))
    bucket = np.where(n < 0, BUCKETS, bucket)
    return (np.arange(BUCKETS + 1)[:, None] == bucket[None, :]).astype(np.float32)


def bands():
    cur = np.zeros((NT, T, H, T), np.float32)
    prev = np.zeros((T, H, T), np.float32)
    s, t = np.arange(T)[:, None], np.arange(T)[None, :]
    for g, w in enumerate(WINDOWS):
        inside = ((s <= t) & (s > t - w)).astype(np.float32)
        for k in range(NT):
            cur[k, :, g, :] = inside / np.minimum(k * T + t + 1, w) - (s == t)
        prev[:, g, :] = (s - T > t - w) / np.float32(w)
    return cur.reshape(NT * T, H * T), prev


def sample_bands():
    cur = np.zeros((NS, H, NS), np.float32)
    old = np.zeros((DB * PAD, H, NS), np.float32)
    for g, w in enumerate(WINDOWS):
        for b in range(DB):
            for i in range(DS):
                at = PAD + i
                for r in range(at - w + 1, at + 1):
                    if r < PAD:
                        old[b * PAD + r, g, b * DS + i] += 1.0 / w
                    else:
                        cur[b * DS + r - PAD, g, b * DS + i] += 1.0 / w
                cur[b * DS + i, g, b * DS + i] -= 1.0
    return cur.reshape(NS, H * NS), old.reshape(DB * PAD, H * NS)


_OUTS = [(SEQ, D), (NS, D), (SEQ, W4), (SEQ, W4), (PAD, W4), (NS, W4), (NS, W4), (DB, PAD, W4)]
_SHAPES = [(1, SEQ, D), (DB, DS, D), (1, 1, SEQ, H, 2 * QK), (1, 1, SEQ, H, HV), (1, 1, PAD, W4),
           (1, DB, DS, H, 2 * QK), (1, DB, DS, H, HV), (1, DB, PAD, W4)]


def kernel(**inputs):
    import concourse.bacc as bacc
    from concourse.bass_utils import run_bass_kernel_spmd

    a = {k: np.asarray(v) for k, v in inputs.items()}
    cur, prev = bands()
    s_cur, s_old = sample_bands()
    rows = np.arange(T)
    mask = np.where(np.arange(NS)[:, None] // DS == np.arange(DB)[None, :], 0.0, NEG).astype(np.float32)
    first_half = (rows // (H * DS)) % 2 == 0
    laid = [
        ("x", a["x_prompt"].reshape(SEQ, D)), ("xs", a["x_sample"].reshape(NS, D)),
        ("cache_k", a["cache_k"].reshape(-1, W4)), ("cache_v", a["cache_v"].reshape(-1, W4)),
        ("page_table", a["page_table"]), ("state", a["state_pool"].reshape(DB * PAD, W4)),
        ("p_t", np.concatenate([a["p_prompt"].reshape(SEQ, PLE), a["p_sample"].reshape(NS, PLE),
                                np.zeros((T - NS, PLE), np.float32)]).T),
        ("norm_attn_g", a["norm_attn_g"].reshape(KD, T).T), ("w_in", a["w_in"][0]),
        ("lams", np.concatenate([a["lambda_q1"], a["lambda_k1"], a["lambda_q2"], a["lambda_k2"]])),
        ("subln_g", a["subln_g"].reshape(HV, 1)), ("rel_bias", a["rel_bias"]),
        ("pool_w", a["pool_w"][0].transpose(1, 0, 2)), ("pool_scale", a["pool_scale"].reshape(H, T).T),
        ("w_out", a["w_out"][0]), ("norm_ffn_g", a["norm_ffn_g"].reshape(D)),
        ("wq_t", a["peer_wq"][0].T), ("keys_t", a["peer_keys"].reshape(2 * PH, NK, NK).transpose(0, 2, 1)),
        ("uv", np.concatenate([a["peer_u"][0], a["peer_v"][0]], axis=1)),
        ("norm_pl_g", a["norm_pl_g"].reshape(KD, T).T), ("w_pl", a["w_pl"][0]),
        ("w_gate", a["w_pl_gate"][0]), ("final_g", a["final_norm_g"]),
        ("c_ident", np.eye(T, dtype=np.float32)), ("c_onehot", onehot_buckets()),
        ("c_bands", cur), ("c_band_prev", prev), ("c_band_s", s_cur), ("c_band_sp", s_old),
        ("c_mask_s", mask), ("c_half", np.stack([first_half, ~first_half], 1).astype(np.float32)),
        ("c_row", rows.astype(np.float32)[:, None]), ("c_iota", np.arange(TOPK, dtype=np.float32)),
    ]
    nc = bacc.Bacc("TRN2", target_bir_lowering=False, num_devices=1)
    arrays, args = {}, []
    for name, v in laid:
        v = np.ascontiguousarray(v)
        arrays[f"in_{name}"] = v
        args.append(nc.dram_tensor(f"in_{name}", v.shape, mybir.dt.from_np(v.dtype), kind="ExternalInput").ap())
    outs = [nc.dram_tensor(f"out_{i}", s, mybir.dt.float32, kind="ExternalOutput").ap()
            for i, s in enumerate(_OUTS)]
    front_and_experts(nc, *args, outs)
    r = run_bass_kernel_spmd(nc, [arrays], core_ids=[0])
    return tuple(r.results[0][f"out_{i}"].reshape(s) for i, s in enumerate(_SHAPES))
```

```python
from contextlib import ExitStack

import numpy as np

import concourse.bass as bass
from concourse import mybir

D = 1024
T = 128
SEQ = 1024
NT = SEQ // T
DB, DS = 8, 4
NS = DB * DS
PAST, PAGE = 512, 128
NPG = PAST // PAGE
H = 4
QK = 64
HV = 128
W4 = 512
WINDOWS = (2, 4, 8, 16)
PAD = 15
KD = D // 128
GATE_AT = 6
BUCKETS, MAX_DIST = 32, 128
PH, NK, TOPK = 8, 128, 16
PLE = 256
EPS = 1e-6
NEG = -1e30
LAM_INIT = 0.2
SCALE = QK ** -0.5
FMAX = -3.0e38
RING = 8
B = 2
NB = TOPK // B
COPIES = T // NS
QS = TOPK // COPIES
N0 = NT * PH
SPAN = (NT - 1) * T
BW = 1408
STRIP = 1536
PT_P = 9


def front_and_experts(nc, x, xs, cache_k, cache_v, page_table, state, p_t, norm_attn_g, w_in,
                      lams, subln_g, rel_bias, pool_w, pool_scale, w_out, norm_ffn_g, wq_t,
                      keys_t, uv, norm_pl_g, w_pl, w_gate, final_g, c_ident, c_onehot, c_bands,
                      c_band_prev, c_band_s, c_band_sp, c_mask_s, c_half, c_row, c_iota,
                      c_fold, c_copy, outs):
    (y_p, y_s, nk_p, nv_p, npool_p, nk_s, nv_s, npool_s) = outs
    f32, i32, u32, bf16 = mybir.dt.float32, mybir.dt.int32, mybir.dt.uint32, mybir.dt.bfloat16
    ALU, ACT, AX = mybir.AluOpType, mybir.ActivationFunctionType, mybir.AxisListType
    ds = bass.ds

    x1_d = nc.dram_tensor("x1_scratch", ((NT + 1) * T, D), f32, kind="Internal").ap()
    strip_h = nc.dram_tensor("strip_scratch", (H * T * STRIP,), f32, kind="Internal")
    strip_d = strip_h.ap()

    def strip_view(offset, dims):
        return bass.AP(tensor=strip_d.tensor, offset=offset, ap=dims)

    with ExitStack() as whole:
        def sb(name, shape, dt=f32, stack=whole):
            return stack.enter_context(nc.sbuf_tensor(name, shape, dt))

        def sem(name):
            return whole.enter_context(nc.semaphore(name))

        big = sb("big", [T, KD, 2048])
        mid = sb("mid", [T, KD, D])
        ring = sb("ring", [T, RING, 2 * D])
        ident = sb("ident", [T, T])
        rf = ring[:, :, :].rearrange("p a b -> p (a b)")

        def part(at, *shape):
            n = int(np.prod(shape))
            v = rf[:, at:at + n]
            if len(shape) == 2:
                return v.rearrange("p (a b) -> p a b", b=shape[1])
            return v

        kT = part(0, H, SEQ)
        vals = part(4096, NT, W4)
        biasw = part(8192, H, BW)
        q_sb = part(13824, W4)
        k_sb = part(14336, W4)
        qT = part(14848, H, T)
        dT = part(15360, H, T)
        bandc = part(15872, H, T)
        pages = part(0, RING, W4)
        pkT = part(4096, 2, W4)
        s_T = part(5120, NPG * 256)
        s_Tn = part(6144, 256)
        s_row = part(6400, 2, 544)
        pr_T = part(7488, NPG * 256)
        pr_Tn = part(8512, 256)
        o_ps = part(8768, 256)
        o_T = part(9024, H * NS)
        st_sb = part(9152, W4)
        qTs = part(9664, H * NS)
        kTs = part(9792, H * NS)
        bf_T = part(9920, H * DS)
        b_raw = part(9936, H * DS)
        bx_raw = part(9952, H * DS)
        wq_st = part(0, 2, D)
        keys_sb = part(2048, 2 * PH, NK)

        with ExitStack() as first:
            def fb(name, shape, dt=f32):
                return sb(name, shape, dt, first)

            xt = fb("xt", [T, 2, D])
            xT = fb("xT", [T, KD, T])
            u_sb = fb("u_sb", [T, 2, W4])
            S = fb("S", [T, 2, 2, SEQ])
            AT = fb("AT", [T, KD, T])
            bandp = fb("bandp", [T, H, T])
            pw = fb("pw", [T, H, T])
            bs_c = fb("bs_c", [NS, H * NS])
            bs_p = fb("bs_p", [DB * PAD, H * NS])
            avs = fb("avs", [T, W4])
            g_attn = fb("g_attn", [T, KD])
            g_sub = fb("g_sub", [T, 1])
            psc = fb("psc", [T, H])
            lam_in = fb("lam_in", [T, 4, QK])
            relb = fb("relb", [BUCKETS + 1, H])
            ptab = fb("ptab", [T, DB * NPG], i32)
            pidx = fb("pidx", [T, DB * NPG], i32)
            mask_s = fb("mask_s", [NS, DB])
            half = fb("half", [T, 2])
            pagef = fb("pagef", [T, DB * NPG])[:, :]
            row = fb("row", [T, 1])
            far = fb("far", [T, H])
            st = fb("st", [T, 48])
            sq = AT[:, :, :].rearrange("p a b -> p (a b)")
        XSS, XRT, XR = 0, 2, 4
        LAMS, LAME, NLAM = 6, 8, 10
        NMAX, LSUM, LREC = 12, 16, 20
        OSS, ORT, OREC = 24, 28, 32
        SMX, SSUM, SREC, SCO = 36, 38, 40, 42

        with ExitStack() as second:
            def gb(name, shape, dt=f32):
                return sb(name, shape, dt, second)

            xn_next = gb("xn_next", [T, D])
            xn_cur = gb("xn_cur", [T, D])
            xnT = gb("xnT", [T, KD, T])
            x2 = gb("x2", [T, D])
            g_ffn = gb("g_ffn", [T, D])
            g_fin = gb("g_fin", [T, D])
            wpl = gb("wpl", [T, 2, D])
            p_sb = gb("p_sb", [T, 2, T])
            diag = gb("diag", [T, RING, T])
            x2T = gb("x2T", [T, KD, T])
            sg = gb("sg", [T, W4])
            junk = sg[:, :].bitcast(bf16)
            g_pl = gb("g_pl", [T, KD])
            iota = gb("iota", [T, TOPK])
            idx = gb("idx", [T, 2, TOPK], i32)
            gate = gb("gate", [T, 2, TOPK])
            ex = gb("ex", [T, 2, TOPK])
            hdot = gb("hdot", [T, 2, TOPK])
            hgelu = gb("hgelu", [T, 2, TOPK])
            sc_sb = gb("sc_sb", [T, 256])
            sc_lo = sg[:, 0:256]
            cand = sg[:, 256:512]
            cand_lo = sc_sb
            top1 = gb("top1", [T, 2, TOPK])
            ind1 = gb("ind1", [T, 2, TOPK], u32)
            ind1f = gb("ind1f", [T, 2, TOPK])
            top2 = gb("top2", [T, TOPK])
            ind2 = gb("ind2", [T, TOPK], u32)
            ab = gb("ab", [T, 2, TOPK], u32)
            abf = gb("abf", [T, 2, TOPK])
            pick = gb("pick", [T, 2, TOPK])
            fold = gb("fold", [T, T])
            copy = gb("copy", [T, COPIES])
            gst = gb("gst", [T, 16])
        NS1, RT1, R1 = 0, 1, 2
        NS2, RT2, R2 = 3, 4, 5
        NS3, RT3, R3 = 6, 7, 8
        NTOP, ESUM, EREC = 10, 12, 14

        sc = whole.enter_context(nc.psum_tensor("sc", [T, 4, 512], f32))
        pb = [whole.enter_context(nc.psum_tensor(f"proj{i}", [T, 512], f32)) for i in range(2)]
        tb = [whole.enter_context(nc.psum_tensor(f"turn{i}", [T, 512], f32)) for i in range(2)]

        const_in = sem("const_in")
        w_in_in = sem("w_in_in")
        w_out_in = sem("w_out_in")
        onehot_in = sem("onehot_in")
        strip_ps = sem("strip_ps")
        strip_sb = sem("strip_sb")
        strip_out = [sem(f"strip_out{i}") for i in range(2)]
        bias_in = sem("bias_in")
        gain_ready = sem("gain_ready")
        lam_sum = sem("lam_sum")
        lam_exp = sem("lam_exp")
        zeroed = sem("zeroed")
        x_in = [sem(f"x_in{i}") for i in range(2)]
        band_in = sem("band_in")
        x_sq = sem("x_sq")
        x_root = sem("x_root")
        x_norm = sem("x_norm")
        pb_ready = [sem(f"proj_ready{i}") for i in range(2)]
        pb_free = [sem(f"proj_free{i}") for i in range(2)]
        tb_ready = [sem(f"turn_ready{i}") for i in range(2)]
        tb_free = [sem(f"turn_free{i}") for i in range(2)]
        s_ready = [sem(f"score_ready{i}") for i in range(2)]
        s_read = [sem(f"score_read{i}") for i in range(2)]
        s_max = [sem(f"score_max{i}") for i in range(2)]
        s_exp = [sem(f"score_exp{i}") for i in range(2)]
        a_ready = sem("a_ready")
        av_done = sem("av_done")
        o_sq = sem("o_sq")
        o_root = sem("o_root")
        o_norm = sem("o_norm")
        k_out = sem("k_out")
        v_out = sem("v_out")
        new_rows_out = sem("new_rows_out")
        x1_out = [sem(f"x1_out{i}") for i in range(2)]
        turns = sem("turns")
        st_in = sem("st_in")
        page_idx = sem("page_idx")
        page_in = [sem(f"page_in{i}") for i in range(RING)]
        page_read = sem("page_read")
        kp_ready = sem("kp_ready")
        kp_read = sem("kp_read")
        ss_ready = sem("ss_ready")
        bT_in = sem("bT_in")
        bT_ready = sem("bT_ready")
        sT_ready = sem("sT_ready")
        sx_ready = sem("sx_ready")
        sx_exp = sem("sx_exp")
        sp_ready = sem("sp_ready")
        prT_ready = sem("prT_ready")
        o_sum = sem("o_sum")
        wq_in = [sem(f"wq_in{i}") for i in range(2)]
        keys_in = sem("keys_in")
        wk_ready = [sem(f"wk_ready{i}") for i in range(2)]
        wk_kept = [sem(f"wk_kept{i}") for i in range(2)]
        gate_w_in = sem("gate_w_in")
        g_in = sem("g_in")
        xn_in = sem("xn_in")
        xn_sq = sem("xn_sq")
        xn_root = sem("xn_root")
        xn_ready = sem("xn_ready")
        xn_turned = sem("xn_turned")
        xnT_ready = sem("xnT_ready")
        xn_moved = sem("xn_moved")
        x1_in = sem("x1_in")
        p_in = sem("p_in")
        route_ready = sem("route_ready")
        route_read = sem("route_read")
        top_ready = sem("top_ready")
        top_exp = sem("top_exp")
        idx_ready = sem("idx_ready")
        gathered = [sem(f"gathered{i}") for i in range(RING)]
        slot_free = sem("slot_free")
        dots_done = sem("dots_done")
        gelu_done = sem("gelu_done")
        diag_ready = sem("diag_ready")
        x2_ready = sem("x2_ready")
        x2_sq = sem("x2_sq")
        x2_root = sem("x2_root")
        r2_ready = sem("r2_ready")
        x2_turned = sem("x2_turned")
        x2T_ready = sem("x2T_ready")
        gate_ready = sem("gate_ready")
        ple_ready = sem("ple_ready")
        ple_read = sem("ple_read")
        sig_ready = sem("sig_ready")
        sig_read = sem("sig_read")
        y_sq = sem("y_sq")
        y_root = sem("y_root")
        y_ready = sem("y_ready")
        y_out = sem("y_out")

        block = whole.enter_context(nc.Block())

        def hold(eng, s, value):
            eng.wait_ge(s, value)
            eng.sem_inc(turns, 1)

        def proj(i, par, o):
            n = par * PT_P + o
            return n % 2, i * PT_P + n // 2
        Q_, K_, U_, V_, BAND, POOL, AV, WO = range(8)
        COLUMNS = {Q_: 0, K_: 1, V_: 2, U_: 3}

        class Region:
            def __init__(self, first, last, width, before):
                self.first, self.last, self.width = first, last, width
                self.nb = width // 512
                self.per = 5 + H * self.nb
                self.before = before
                self.after = before + (last - first) * self.per

            def turn(self, i, par, o):
                n = par * self.per + o
                return n % 2, (i - self.first) * self.per + self.before + n // 2

            def a_turn(self, i, par, h, c):
                return self.turn(i, par, 4 + h * self.nb + c)

            def o_turn(self, i, par):
                return self.turn(i, par, 4 + H * self.nb)

        RA = Region(0, 2, 512, 0)
        RB = Region(2, 4, 1024, RA.after)
        REGIONS = (RA, RB)
        ST0 = RB.after
        SI = NT // 2

        def s_turn(o):
            return o % 2, ST0 + o // 2
        S_PAGE, S_ROW, S_BACK, S_O = 4, 36, 39, 42
        ST_N = 44
        N_FIRST_LOADS = 15

        @block.sync
        def _(sp):
            for dst, src in (
                (ident[:, :], c_ident), (bandp[:, :, :], c_band_prev), (pw[:, :, :], pool_w),
                (bs_c[:, :], c_band_s), (bs_p[:, :], c_band_sp), (g_attn[:, :], norm_attn_g),
                (g_sub[:, :], subln_g), (psc[:, :], pool_scale),
                (relb[0:BUCKETS, :], rel_bias), (mask_s[:, :], c_mask_s), (half[:, :], c_half),
                (row[:, :], c_row),
                (ptab[:, :], page_table.rearrange("a b -> (a b)").partition_broadcast(T)),
                (lam_in[:, :, :], lams.partition_broadcast(T)),
            ):
                sp.dma_start(dst, src).then_inc(const_in, 16)
            sp.dma_start(mid[0:BUCKETS + 1, 0:2, 0:768],
                         c_onehot.rearrange("p (a b) -> p a b", b=768)).then_inc(onehot_in, 16)
            sp.dma_start(xt[:, 0, :], x[0:T, :]).then_inc(x_in[0], 16)
            for c in range(4):
                sp.dma_start(big[:, :, c * W4:(c + 1) * W4],
                             w_in[:, c * W4:(c + 1) * W4].rearrange("(k p) n -> p k n", p=T)
                             ).then_inc(w_in_in, 16)
                if c == 0:
                    sp.dma_start(xt[:, 1, :], x[T:2 * T, :]).then_inc(x_in[1], 16)
            sp.dma_start(bandc, c_bands[0:T, :].rearrange("p (g t) -> p g t", g=H)).then_inc(band_in, 16)
            for h in range(H):
                sp.wait_ge(strip_sb, h + 1)
                sp.dma_start(strip_view(h * T * STRIP, [[STRIP, T], [1, STRIP]]),
                             S[:, h % 2, :, :].rearrange("p a b -> p (a b)")[:, 0:STRIP]
                             ).then_inc(strip_out[h % 2], 16)
            for c in range(2):
                sp.dma_start(mid[:, :, c * W4:(c + 1) * W4],
                             w_out[:, c * W4:(c + 1) * W4].rearrange("(k p) n -> p k n", p=T)
                             ).then_inc(w_out_in, 16)
            sp.wait_ge(strip_out[0], 16 * H // 2)
            sp.wait_ge(strip_out[1], 16 * H // 2)
            sp.dma_start(biasw, strip_view(T - 1, [[STRIP - 1, T], [T * STRIP, H], [1, BW]])
                         ).then_inc(bias_in, 16)
            with sp.Fori(1, NT // 2) as i:
                for par in range(2):
                    b, m = proj(i - 1, par, BAND)
                    sp.wait_ge(pb_ready[b], m + 1)
                    sp.dma_start(bandc, c_bands[ds(i * (2 * T) + (par - 1) * T, T), :].rearrange(
                        "p (g t) -> p g t", g=H)).then_inc(band_in, 16)
                    sp.wait_ge(x1_out[par], i * 16)
                    sp.dma_start(xt[:, par, :], x[ds(i * (2 * T) + par * T, T), :]
                                 ).then_inc(x_in[par], 16)
            b, m = proj(SI - 1, 0, BAND)
            sp.wait_ge(pb_ready[b], m + 1)
            sp.dma_start(bandc, c_bands[SEQ - T:SEQ, :].rearrange("p (g t) -> p g t", g=H)
                         ).then_inc(band_in, 16)
            sp.wait_ge(x1_out[0], 16 * SI)
            sp.dma_start(xt[0:NS, 0, :], xs).then_inc(x_in[0], 16)
            sp.wait_ge(av_done, H * NT + H)
            sp.dma_start(st_sb[0:DB * PAD, :], state).then_inc(st_in, 16)
            near0 = SPAN + T - 1 - T
            with nc.allow_non_contiguous_dma(reason="small bias tables"):
                for h in range(H):
                    sp.dma_start(b_raw[:, h * DS:(h + 1) * DS],
                                 strip_view(h * T * STRIP + near0, [[1, T], [STRIP - 1, DS]]),
                                 allow_slow_non_contiguous=True).then_inc(bT_in, 16)
                    for b in range(DB):
                        sp.dma_start(bx_raw[b * DS:(b + 1) * DS, h * DS:(h + 1) * DS],
                                     strip_view(h * T * STRIP + SPAN + T - 1, [[1, DS], [STRIP - 1, DS]]),
                                     allow_slow_non_contiguous=True).then_inc(bT_in, 16)
            sp.wait_ge(x1_out[0], 16 * (SI + COPIES))
            sp.wait_ge(x1_out[1], 16 * SI)
            sp.wait_ge(k_out, 16 * (NT + 2))
            sp.wait_ge(v_out, 16 * (NT + 1))
            sp.wait_ge(new_rows_out, 16 * 2)
            for hp in range(2 * PH):
                if hp == 0:
                    sp.dma_start(keys_sb, keys_t.rearrange("h d k -> d h k")).then_inc(keys_in, 16)
                if hp >= 2:
                    sp.wait_ge(wk_ready[1], hp - 1)
                sp.dma_start(wq_st[:, hp % 2, :], wq_t[hp * T:(hp + 1) * T, :]).then_inc(wq_in[hp % 2], 16)
            sp.dma_start(xn_next[:, :], x1_d[0:T, :]).then_inc(xn_in, 16)
            for dst, src in ((g_ffn[:, :], norm_ffn_g.partition_broadcast(T)),
                             (g_fin[:, :], final_g.partition_broadcast(T)),
                             (g_pl[:, :], norm_pl_g), (iota[:, :], c_iota.partition_broadcast(T)),
                             (fold[:, :], c_fold), (copy[:, :], c_copy),
                             (wpl[:, :, :], w_pl.rearrange("(k p) n -> p k n", p=T))):
                sp.dma_start(dst, src).then_inc(g_in, 16)
            sp.dma_start(x2[:, :], x1_d[0:T, :]).then_inc(x1_in, 16)
            for c in range(2):
                sp.dma_start(mid[:, :, c * W4:(c + 1) * W4],
                             w_gate[:, c * W4:(c + 1) * W4].rearrange("(k p) n -> p k n", p=T)
                             ).then_inc(gate_w_in, 16)
            sp.dma_start(p_sb[:, :, :], p_t[:, 0:T].rearrange("(k p) n -> p k n", p=T)).then_inc(p_in, 16)
            with sp.Fori(0, NT) as t:
                sp.wait_ge(xn_moved, t + 1)
                sp.dma_start(xn_next[:, :], x1_d[ds(t * T + T, T), :]).then_inc(xn_in, 16)
                sp.wait_ge(y_ready, t + 1)
                sp.dma_start(y_p[ds(t * T, T), :], x2[:, :]).then_inc(y_out, 16)
                sp.dma_start(p_sb[:, :, :], p_t[:, ds(t * T + T, T)].rearrange("(k p) n -> p k n", p=T)
                             ).then_inc(p_in, 16)
                sp.wait_ge(y_out, t * 16 + 16)
                sp.dma_start(x2[:, :], x1_d[ds(t * T + T, T), :]).then_inc(x1_in, 16)
            sp.wait_ge(y_ready, NT + 1)
            sp.dma_start(y_s, x2[0:NS, :]).then_inc(y_out, 16)
            sp.wait_ge(y_out, 16 * (NT + 1))

        @block.gpsimd
        def _(pool):
            pool.dma_start(npool_s[:, 0:PAD - DS, :], state.rearrange("(b r) n -> b r n", b=DB)[:, DS:PAD, :]
                           ).then_inc(k_out, 16)
            with pool.Fori(0, NT // 2) as i:
                for par in range(2):
                    rows = ds(i * (2 * T) + par * T, T)
                    b, m = proj(i, par, K_)
                    hold(pool, pb_free[b], m + 2)
                    pool.dma_start(nk_p[rows, :], k_sb).then_inc(k_out, 16)
                    b, m = proj(i, par, V_)
                    hold(pool, pb_free[b], m + 2)
                    pool.dma_start(nv_p[rows, :], vals[:, ds(i * 2 + par, 1), :].rearrange(
                        "p a b -> p (a b)")).then_inc(v_out, 16)
                    for c in range(2):
                        b, m = proj(i, par, WO + c)
                        hold(pool, pb_free[b], m + 2)
                    pool.dma_start(x1_d[rows, :], xt[:, par, :]).then_inc(x1_out[par], 16)
            pool.dma_start(npool_p, u_sb[T - PAD:T, 1, :]).then_inc(new_rows_out, 16)
            b, m = proj(SI, 0, K_)
            pool.wait_ge(pb_free[b], m + 2)
            pool.dma_start(nk_s, k_sb[0:NS, :]).then_inc(k_out, 16)
            b, m = proj(SI, 0, V_)
            pool.wait_ge(pb_free[b], m + 2)
            pool.dma_start(nv_s, q_sb[0:NS, :]).then_inc(v_out, 16)
            b, m = proj(SI, 0, U_)
            pool.wait_ge(pb_free[b], m + 2)
            pool.dma_start(npool_s[:, PAD - DS:PAD, :], u_sb[0:NS, 0, :]).then_inc(new_rows_out, 16)
            pool.wait_ge(page_idx, 1)
            pool.wait_ge(av_done, H * NT + H)
            for n in range(2 * DB * NPG):
                if n >= RING:
                    pool.wait_ge(page_read, n - RING + 1)
                src = cache_k if n < DB * NPG else cache_v
                m = n % (DB * NPG)
                pool.indirect_dma_start(pages[:, n % RING, :], None, src,
                                        bass.IndirectOffsetOnAxis(ap=pidx[:, m:m + 1], axis=0)
                                        ).then_inc(page_in[n % RING], 16)
            for c in range(2):
                b, m = proj(SI, 0, WO + c)
                pool.wait_ge(pb_free[b], m + 2)
            for q in range(COPIES):
                pool.dma_start(x1_d[SEQ + q * NS:SEQ + (q + 1) * NS, :], xt[0:NS, 0, :]
                               ).then_inc(x1_out[0], 16)

            def gather(n, first, slots):
                hold(pool, idx_ready, n + 1)
                for j, (r, par) in enumerate(slots):
                    hold(pool, slot_free, first + j + 1)
                    pool.indirect_dma_start(ring[:, r, :], None, uv,
                                            bass.IndirectOffsetOnAxis(ap=idx[:, par, j:j + 1], axis=0)
                                            ).then_inc(gathered[r], 16)

            with pool.Fori(0, N0 // 2) as s:
                for par in range(2):
                    gather(s * 2 + par, (s * 2 + par) * TOPK, [(j % RING, par) for j in range(TOPK)])
            with pool.Fori(0, PH // 2) as s:
                for par in range(2):
                    gather(s * 2 + par + N0, (s * 2 + par) * QS + N0 * TOPK,
                           [(par * QS + j, par) for j in range(QS)])

        @block.tensor
        def _(pe):
            for b in range(2):
                pe.sem_inc(pb_free[b], 1)
                pe.sem_inc(tb_free[b], 1)
            pe.wait_ge(const_in, 16 * 14)
            pe.wait_ge(gain_ready, 1)
            pe.wait_ge(onehot_in, 16)
            for h in range(H):
                if h >= 1:
                    pe.wait_ge(strip_sb, h)
                oh = mid[0:BUCKETS + 1, 0:2, 0:768]
                for c in range(4):
                    mm = pe.matmul(sc[:, c, 0:384], AT[0:BUCKETS + 1, h, :], oh[:, c // 2, (c % 2) * 384:(c % 2) * 384 + 384],
                                   start=True, stop=True)
                mm.then_inc(strip_ps, 1)

            def project(i, par, o, P=T, halfway=None):
                b, m = proj(i, par, o)
                pe.wait_ge(pb_free[b], m + 1)
                at = COLUMNS[o] * W4
                for k in range(KD):
                    if halfway and k == KD // 2:
                        halfway()
                    mm = pe.matmul(pb[b][0:P, :], xT[:, k, 0:P], big[:, k, at:at + W4],
                                   start=(k == 0), stop=(k == KD - 1))
                mm.then_inc(pb_ready[b], 1)

            def turn4(bm, ins, rows=T, cols=T, P=T):
                b, m = bm
                pe.wait_ge(tb_free[b], m + 1)
                for c, v in enumerate(ins):
                    mm = pe.transpose(tb[b][0:rows, c * cols:(c + 1) * cols], v, ident[0:P, 0:P])
                mm.then_inc(tb_ready[b], 1)

            def w_out_part(i, par, c, pooled, P=T):
                b, m = proj(i, par, WO + c)
                if pooled:
                    pe.wait_ge(pb_free[b], m + 1)
                for k in range(H, 2 * H) if pooled else range(H):
                    mm = pe.matmul(pb[b][0:P, :], xT[:, k, 0:P], mid[:, k, c * W4:(c + 1) * W4],
                                   start=(k == H), stop=(k == H - 1))
                if not pooled:
                    mm.then_inc(pb_ready[b], 1)

            def w_out_(i, par, out_turn, P=T):
                b, m = proj(i, par, POOL)
                pe.wait_ge(pb_free[b], m + 2)
                w_out_part(i, par, 0, True, P)
                pe.wait_ge(o_norm, i * 2 + par + 1)
                turn4(out_turn, [avs[0:P, h * T:(h + 1) * T] for h in range(H)], cols=P, P=P)
                w_out_part(i, par, 1, True, P)
                b, m = out_turn
                pe.wait_ge(tb_free[b], m + 2)
                w_out_part(i, par, 0, False, P)
                w_out_part(i, par, 1, False, P)

            def pool_out(i, par, P=T):
                b, m = proj(i, par, BAND)
                pe.wait_ge(pb_free[b], m + 2)
                b, m = proj(i, par, POOL)
                pe.wait_ge(pb_free[b], m + 1)
                for g in range(H):
                    mm = pe.matmul(pb[b][:, g * P:(g + 1) * P], pw[:, g, :], dT[:, g, 0:P],
                                   start=True, stop=True)
                mm.then_inc(pb_ready[b], 1)

            def tile(R, i, par):
                t = i * 2 + par
                nb = R.nb
                pe.wait_ge(x_in[par], i * 16 + 16)
                for c in range(2):
                    turn4(R.turn(i, par, c), [xt[:, par, (4 * c + k) * T:(4 * c + k + 1) * T] for k in range(4)])
                for c in range(2):
                    b, m = R.turn(i, par, c)
                    pe.wait_ge(tb_free[b], m + 2)
                def turn_heads(o, src):
                    b, m = proj(i, par, o)
                    pe.wait_ge(pb_free[b], m + 2)
                    turn4(R.turn(i, par, 2 + o), [src[:, h * T:(h + 1) * T] for h in range(H)])

                for o in (Q_, K_):
                    project(i, par, o)
                turn_heads(Q_, q_sb)
                project(i, par, U_, halfway=lambda: turn_heads(K_, k_sb))
                for o in (2, 3):
                    b, m = R.turn(i, par, o)
                    pe.wait_ge(tb_free[b], m + 2)

                def scores(h):
                    for a in range(2):
                        pe.wait_ge(s_read[a], t * H + h + 1)
                        for c in range(nb):
                            mm = pe.matmul(sc[:, 2 * a + c, :], qT[a * QK:(a + 1) * QK, h, :],
                                           kT[a * QK:(a + 1) * QK, h, c * 512:(c + 1) * 512],
                                           start=True, stop=True)
                        mm.then_inc(s_ready[a], 1)

                def values(h):
                    pe.wait_ge(a_ready, t * H + h + 1)
                    for c in range(nb):
                        turn4(R.a_turn(i, par, h, c),
                              [S[:, h % 2, 0, (4 * c + k) * T:(4 * c + k + 1) * T] for k in range(4)])
                    bo, mo = proj(i, par, AV)
                    if h == 0:
                        pe.wait_ge(pb_free[bo], mo + 1)
                    for c in range(nb):
                        b, m = R.a_turn(i, par, h, c)
                        pe.wait_ge(tb_free[b], m + 2)
                        for k in range(4 * c, 4 * c + 4):
                            mm = pe.matmul(pb[bo][:, h * HV:(h + 1) * HV], AT[:, k, :],
                                           vals[:, k, h * HV:(h + 1) * HV],
                                           start=(k == 0), stop=(k == 4 * nb - 1))
                            if h == 0 and k == 0:
                                mm.then_inc(pb_ready[bo], 1)
                    mm.then_inc(av_done, 1)

                scores(0)
                scores(1)
                project(i, par, V_)
                b, m = proj(i, par, U_)
                pe.wait_ge(pb_free[b], m + 2)
                pe.wait_ge(band_in, t * 16 + 16)
                b, m = proj(i, par, BAND)
                pe.wait_ge(pb_free[b], m + 1)
                for g in range(H):
                    pe.matmul(pb[b][:, g * T:(g + 1) * T], u_sb[:, par, g * T:(g + 1) * T],
                              bandc[:, g, :], start=True, stop=False)
                    mm = pe.matmul(pb[b][:, g * T:(g + 1) * T], u_sb[:, 1 - par, g * T:(g + 1) * T],
                                   bandp[:, g, :], start=False, stop=True)
                mm.then_inc(pb_ready[b], 1)
                b, m = proj(i, par, V_)
                pe.wait_ge(pb_free[b], m + 2)
                values(0)
                pool_out(i, par)
                scores(2)
                values(1)
                scores(3)
                values(2)
                values(3)
                w_out_(i, par, R.o_turn(i, par))

            pe.wait_ge(w_in_in, 16 * 4)
            pe.wait_ge(w_out_in, 16 * 2)
            for R in REGIONS:
                with pe.Fori(R.first, R.last) as i:
                    for par in range(2):
                        tile(R, i, par)

            pe.wait_ge(x_in[0], 16 * (SI + 1))
            for c in range(2):
                turn4(s_turn(c), [xt[0:NS, 0, (4 * c + k) * T:(4 * c + k + 1) * T] for k in range(4)],
                      cols=NS, P=NS)
            for c in range(2):
                b, m = s_turn(c)
                pe.wait_ge(tb_free[b], m + 2)
            for o in (Q_, K_, U_, V_):
                project(SI, 0, o, NS)
            for o, src in ((Q_, q_sb), (K_, k_sb)):
                b, m = proj(SI, 0, o)
                pe.wait_ge(pb_free[b], m + 2)
                turn4(s_turn(2 + o), [src[0:NS, h * T:(h + 1) * T] for h in range(H)], cols=NS, P=NS)
            b, m = proj(SI, 0, U_)
            pe.wait_ge(pb_free[b], m + 2)
            pe.wait_ge(st_in, 16)
            b, m = proj(SI, 0, BAND)
            pe.wait_ge(pb_free[b], m + 1)
            for g in range(H):
                pe.matmul(pb[b][:, g * NS:(g + 1) * NS], u_sb[0:NS, 0, g * T:(g + 1) * T],
                          bs_c[:, g * NS:(g + 1) * NS], start=True, stop=False)
                mm = pe.matmul(pb[b][:, g * NS:(g + 1) * NS], st_sb[0:DB * PAD, g * T:(g + 1) * T],
                               bs_p[:, g * NS:(g + 1) * NS], start=False, stop=True)
            mm.then_inc(pb_ready[b], 1)
            pool_out(SI, 0, NS)
            for o in (2, 3):
                b, m = s_turn(o)
                pe.wait_ge(tb_free[b], m + 2)
            qs = qTs.rearrange("p (h n) -> p h n", h=H)
            ks = kTs.rearrange("p (h n) -> p h n", h=H)
            pe.wait_ge(s_read[0], H * NT + 1)
            pe.wait_ge(s_read[1], H * NT + 1)
            pq = pages.rearrange("p r (h n) -> p r h n", h=H)
            pk = pkT.rearrange("p r (h n) -> p r h n", h=H)

            def page_turn(n):
                pe.wait_ge(page_in[n % RING], 16 * (n // RING + 1))
                b, m = s_turn(S_PAGE + n)
                pe.wait_ge(tb_free[b], m + 1)
                for h in range(H):
                    mm = pe.transpose(tb[b][:, h * T:(h + 1) * T], pq[:, n % RING, h, :], ident[:, :])
                mm.then_inc(tb_ready[b], 1)

            def page_scores(n):
                bi, pg = n // NPG, n % NPG
                b, m = s_turn(S_PAGE + n)
                pe.wait_ge(tb_free[b], m + 2)
                for h in range(H):
                    for a in range(2):
                        at = pg * T + bi * 16 + h * DS
                        mm = pe.matmul(sc[:, a, at:at + DS], pk[a * QK:(a + 1) * QK, n % 2, h, :],
                                       qs[a * QK:(a + 1) * QK, h, bi * DS:(bi + 1) * DS],
                                       start=True, stop=True)
                mm.then_inc(page_read, 1)

            for n in range(DB * NPG):
                page_turn(n)
                if n >= 1:
                    page_scores(n - 1)
            page_scores(DB * NPG - 1)
            new = sc[0:NS, 2:4, 0:T].rearrange("p a (b h i) -> p a b h i", b=DB, h=H)
            for h in range(H):
                for a in range(2):
                    mm = pe.matmul(new[:, a, :, h, :], ks[a * QK:(a + 1) * QK, h, :],
                                   qs[a * QK:(a + 1) * QK, h, :].rearrange("p (b i) -> p b i", b=DB),
                                   start=True, stop=True)
            mm.then_inc(ss_ready, 1)
            pe.wait_ge(sT_ready, 1)
            for g in range(2):
                turn4(s_turn(S_ROW + g), [s_T[:, pg * 256 + g * T:pg * 256 + (g + 1) * T] for pg in range(NPG)])
            turn4(s_turn(S_ROW + 2), [s_Tn[0:NS, g * T:(g + 1) * T] for g in range(2)], cols=NS, P=NS)
            pe.wait_ge(sp_ready, 1)
            for g in range(2):
                turn4(s_turn(S_BACK + g), [s_row[:, g, pg * T:(pg + 1) * T] for pg in range(NPG)])
            turn4(s_turn(S_BACK + 2), [s_row[:, g, PAST:PAST + NS] for g in range(2)], rows=NS)
            for o in range(3):
                b, m = s_turn(S_BACK + o)
                pe.wait_ge(tb_free[b], m + 2)
            for bi in range(DB):
                for pg in range(NPG):
                    n = DB * NPG + bi * NPG + pg
                    pe.wait_ge(page_in[n % RING], 16 * (n // RING + 1))
                for h in range(H):
                    at = bi * 32 + h * 8
                    cols = lambda ap: ap.rearrange("p (b a h i) -> p b h a i", b=DB, a=2, h=H)[:, bi, h]
                    for pg in range(NPG):
                        n = DB * NPG + bi * NPG + pg
                        pe.matmul(sc[:, 3, at:at + 8], pq[:, n % RING, h, :],
                                  cols(pr_T[:, pg * 256:(pg + 1) * 256]), start=(pg == 0), stop=False)
                    mm = pe.matmul(sc[:, 3, at:at + 8], q_sb[0:NS, h * HV:(h + 1) * HV],
                                   cols(pr_Tn[0:NS, :]), start=False, stop=True)
                mm.then_inc(page_read, NPG)
            pe.wait_ge(o_sum, 1)
            b, m = proj(SI, 0, AV)
            pe.wait_ge(pb_free[b], m + 1)
            for h in range(H):
                mm = pe.transpose(pb[b][0:NS, h * T:(h + 1) * T], o_T[:, h * NS:(h + 1) * NS], ident[:, :])
                if h == 0:
                    mm.then_inc(pb_ready[b], 1)
            mm.then_inc(av_done, H)
            w_out_(SI, 0, s_turn(S_O), NS)

            pe.wait_ge(keys_in, 16)
            for c in range(2):
                b, m = proj(SI, 0, WO + c)
                pe.wait_ge(pb_free[b], m + 2)
            for hp in range(2 * PH):
                pe.wait_ge(wq_in[hp % 2], 16 * (hp // 2 + 1))
                for c in range(2):
                    if hp >= 1:
                        pe.wait_ge(wk_kept[c], hp)
                    for k in range(4):
                        mm = pe.matmul(pb[c][:, k * NK:(k + 1) * NK],
                                       wq_st[:, hp % 2, (4 * c + k) * T:(4 * c + k + 1) * T],
                                       keys_sb[:, hp, :], start=True, stop=True)
                    mm.then_inc(wk_ready[c], 1)
            pe.sem_inc(slot_free, RING)
            pe.sem_inc(route_read, 1)

            def turn_xn(t):
                pe.wait_ge(xn_ready, t + 1)
                for c in range(2):
                    for k in range(4):
                        mm = pe.transpose(tb[c][:, k * T:(k + 1) * T],
                                          xn_next[:, (4 * c + k) * T:(4 * c + k + 1) * T], ident[:, :])
                    mm.then_inc(xn_turned, 1)
                pe.wait_ge(xnT_ready, t * 2 + 2)

            def route(n, h):
                pe.wait_ge(route_read, n + 1)
                for k in range(KD):
                    mm = pe.matmul(pb[0][:, 0:256], xnT[:, k, :], big[:, k, ds(h * 256, 256)],
                                   start=(k == 0), stop=(k == KD - 1))
                mm.then_inc(route_ready, 1)

            def add_value(r, opens, closes):
                for c in range(2):
                    mm = pe.matmul(sc[:, c, :], diag[:, r, :], ring[:, r, D + c * 512:D + (c + 1) * 512],
                                   start=opens, stop=closes)
                mm.then_inc(slot_free, 1)

            def add_values(n, first=False, last=False, between={}):
                for k in range(NB):
                    pe.wait_ge(diag_ready, n * NB + k + 1)
                    for j in range(k * B, (k + 1) * B):
                        add_value(j % RING, first and j == 0, last and j == TOPK - 1)
                    if k in between:
                        between[k]()

            def turn_x2(t):
                for c in range(2):
                    pe.wait_ge(x2_ready, t * 2 + c + 1)
                    for k in range(4):
                        mm = pe.transpose(tb[c][:, k * T:(k + 1) * T],
                                          x2[:, (4 * c + k) * T:(4 * c + k + 1) * T], ident[:, :])
                    mm.then_inc(x2_turned, 1)

            def embed(t):
                pe.wait_ge(p_in, t * 16 + 16)
                for c in range(2):
                    if c == 1:
                        pe.wait_ge(x2T_ready, t * 2 + 2)
                    for k in range(2):
                        mm = pe.matmul((pb[1], tb[1])[c][:, :], p_sb[:, k, :],
                                       wpl[:, k, c * W4:(c + 1) * W4], start=(k == 0), stop=(k == 1))
                    mm.then_inc(ple_ready, 1)

            def gate_part(c, k0):
                for k in range(k0, k0 + KD // 2):
                    mm = pe.matmul(sc[:, 2 + c, :], x2T[:, k, :], mid[:, k, c * W4:(c + 1) * W4],
                                   start=(k == 0), stop=(k == KD - 1))
                if k0:
                    mm.then_inc(gate_ready, 1)

            def gate(t):
                embed(t)
                for c in range(2):
                    for k0 in (0, KD // 2):
                        gate_part(c, k0)

            def first_heads(t):
                turn_x2(t - 1)
                route(t * PH + 1, 1)
                add_values(t * PH, first=True, between={
                    0: lambda: embed(t - 1), 1: lambda: gate_part(0, 0), 2: lambda: gate_part(0, KD // 2),
                    3: lambda: gate_part(1, 0), 5: lambda: gate_part(1, KD // 2)})
                route(t * PH + 2, 2)
                add_values(t * PH + 1)

            def later_heads(t):
                with pe.Fori(1, PH // 2 - 1) as hh:
                    for par in range(2):
                        route(t * PH + hh * 2 + par + 1, hh * 2 + par + 1)
                        add_values(t * PH + hh * 2 + par)
                route(t * PH + PH - 1, PH - 1)
                add_values(t * PH + PH - 2)
                turn_xn(t + 1)
                route(t * PH + PH, 0)
                add_values(t * PH + PH - 1, last=True)

            pe.wait_ge(wk_kept[0], 2 * PH)
            pe.wait_ge(wk_kept[1], 2 * PH)
            turn_xn(0)
            route(0, 0)
            route(1, 1)
            add_values(0, first=True)
            route(2, 2)
            add_values(1)
            pe.wait_ge(gate_w_in, 32)
            pe.wait_ge(g_in, 16 * 7)
            with pe.Fori(0, NT - 1) as t:
                later_heads(t)
                first_heads(t + 1)
            later_heads(NT - 1)
            route(N0 + 1, 1)
            turn_x2(NT - 1)
            gate(NT - 1)

            def sample_step(s, par, opens=False, more=True, last=False):
                if more:
                    route(s * 2 + par + (N0 + 2), s * 2 + par + 2)
                pe.wait_ge(diag_ready, s * 2 + par + (N0 * NB + 1))
                for j in range(QS):
                    add_value(par * QS + j, opens and j == 0, last and j == QS - 1)

            for par in range(2):
                sample_step(0, par, opens=(par == 0))
            with pe.Fori(1, PH // 2 - 1) as s:
                for par in range(2):
                    sample_step(s, par)
            for par in range(2):
                sample_step(PH // 2 - 1, par, more=False, last=(par == 1))
            turn_x2(NT)
            gate(NT)

        @block.scalar
        def _(act):
            act.wait_ge(lam_sum, 2)
            act.activation(st[:, LAME:LAME + 2], st[:, LAMS:LAMS + 2], ACT.Exp).then_inc(lam_exp, 1)
            for h in range(H):
                act.wait_ge(strip_ps, h + 1)
                if h >= 2:
                    act.wait_ge(strip_out[h % 2], 16 * (h // 2))
                act.activation(S[:, h % 2, :, :].rearrange("p a b -> p (a b)")[:, 0:STRIP].rearrange(
                    "p (a b) -> p a b", b=384), sc[:, :, 0:384], ACT.Copy).then_inc(strip_sb, 1)

            def tile(R, i, par):
                t = i * 2 + par
                nb = R.nb
                act.wait_ge(x_sq, t + 1)
                act.activation(st[:, XRT + par:XRT + par + 1], st[:, XSS + par:XSS + par + 1], ACT.Sqrt,
                               ).then_inc(x_root, 1)
                act.wait_ge(x_norm, t + 1)

                def evac(o, dst, stand_alone=False):
                    b, m = proj(i, par, o)
                    if stand_alone:
                        hold(act, pb_ready[b], m + 1)
                    else:
                        act.wait_ge(pb_ready[b], m + 1)
                    act.activation(dst, pb[b][:, :], ACT.Copy, scale=st[:, XR + par:XR + par + 1]
                                   ).then_inc(pb_free[b], 1)

                evac(Q_, q_sb)
                act.wait_ge(k_out, t * 16 + 16)
                evac(K_, k_sb)
                b, m = R.turn(i, par, 2)
                act.wait_ge(tb_ready[b], m + 1)
                act.activation(qT, tb[b][:, :].rearrange("p (a b) -> p a b", a=H), ACT.Copy
                               ).then_inc(tb_free[b], 1)
                b, m = R.turn(i, par, 3)
                hold(act, tb_ready[b], m + 1)
                act.activation(kT[:, :, ds(t * T, T)], tb[b][:, :].rearrange("p (a b) -> p a b", a=H),
                               ACT.Copy).then_inc(tb_free[b], 1)
                evac(U_, u_sb[:, par, :])

                def exps(h):
                    for a in range(2):
                        act.wait_ge(s_max[a], t * H + h + 1)
                        row_ = S[:, h % 2, a, 0:R.width]
                        col = 2 * (h % 2) + a
                        act.activation(row_, row_, ACT.Exp, bias=st[:, NMAX + col:NMAX + col + 1],
                                       accum_out=st[:, LSUM + col:LSUM + col + 1]).then_inc(s_exp[a], 1)

                def weights(h):
                    act.wait_ge(av_done, t * H + h + H)
                    for c in range(nb):
                        b, m = R.a_turn(i, par, h, c)
                        act.wait_ge(tb_ready[b], m + 1)
                        act.activation(AT[:, 4 * c:4 * c + 4, :], tb[b][:, :].rearrange("p (a b) -> p a b", a=4),
                                       ACT.Copy).then_inc(tb_free[b], 1)

                exps(0)
                exps(1)
                evac(V_, vals[:, ds(t, 1), :].rearrange("p a b -> p (a b)"), True)
                b, m = proj(i, par, BAND)
                act.wait_ge(pb_ready[b], m + 1)
                act.activation(dT, pb[b][:, :].rearrange("p (a b) -> p a b", a=H), ACT.Copy
                               ).then_inc(pb_free[b], 1)
                weights(0)
                weights(1)
                exps(2)
                weights(2)
                exps(3)
                weights(3)
                act.wait_ge(av_done, t * H + 2 * H)
                b, m = proj(i, par, AV)
                act.activation(avs[:, :], pb[b][:, :], ACT.Copy).then_inc(pb_free[b], 1)
                act.wait_ge(o_sq, t + 1)
                act.activation(st[:, ORT:ORT + H], st[:, OSS:OSS + H], ACT.Sqrt).then_inc(o_root, 1)

            act.wait_ge(zeroed, 1)
            for R in REGIONS:
                with act.Fori(R.first, R.last) as i:
                    for par in range(2):
                        tile(R, i, par)

            act.wait_ge(x_sq, NT + 1)
            act.activation(st[0:NS, XRT:XRT + 1], st[0:NS, XSS:XSS + 1], ACT.Sqrt).then_inc(x_root, 1)
            act.wait_ge(x_norm, NT + 1)
            for o, dst in ((Q_, q_sb), (K_, k_sb), (U_, u_sb[:, 0, :]), (V_, q_sb)):
                b, m = proj(SI, 0, o)
                act.wait_ge(pb_ready[b], m + 1)
                if o == K_:
                    act.wait_ge(k_out, 16 * NT + 16)
                if o == V_:
                    bt, mt = s_turn(2)
                    act.wait_ge(tb_ready[bt], mt + 1)
                act.activation(dst[0:NS, :], pb[b][0:NS, :], ACT.Copy, scale=st[0:NS, XR:XR + 1]
                               ).then_inc(pb_free[b], 1)
                if o == K_:
                    act.wait_ge(av_done, H * NT + H)
                    act.wait_ge(s_read[0], H * NT + 1)
                    for oo, dd in ((2, qTs),):
                        bt, mt = s_turn(oo)
                        act.wait_ge(tb_ready[bt], mt + 1)
                        act.activation(dd, tb[bt][:, 0:H * NS], ACT.Copy).then_inc(tb_free[bt], 1)
            bt, mt = s_turn(3)
            act.wait_ge(tb_ready[bt], mt + 1)
            act.activation(kTs, tb[bt][:, 0:H * NS], ACT.Copy).then_inc(tb_free[bt], 1)
            b, m = proj(SI, 0, BAND)
            act.wait_ge(pb_ready[b], m + 1)
            act.activation(dT[:, :, 0:NS], pb[b][:, 0:H * NS].rearrange("p (a b) -> p a b", a=H), ACT.Copy
                           ).then_inc(pb_free[b], 1)
            for n in range(DB * NPG):
                b, m = s_turn(S_PAGE + n)
                act.wait_ge(tb_ready[b], m + 1)
                if n >= 2:
                    act.wait_ge(page_read, n - 1)
                act.activation(pkT[:, n % 2, :], tb[b][:, :], ACT.Copy).then_inc(tb_free[b], 1)
            act.wait_ge(sx_ready, 2)
            for g in range(2):
                act.activation(s_row[:, g, :], s_row[:, g, :], ACT.Exp, bias=st[:, SMX + g:SMX + g + 1],
                               accum_out=st[:, SSUM + g:SSUM + g + 1]).then_inc(sx_exp, 1)
            for g in range(2):
                b, m = s_turn(S_BACK + g)
                act.wait_ge(tb_ready[b], m + 1)
                act.activation(pr_T.rearrange("p (a b) -> p a b", a=NPG)[:, :, g * T:(g + 1) * T],
                               tb[b][:, :].rearrange("p (a b) -> p a b", a=NPG), ACT.Copy
                               ).then_inc(tb_free[b], 1)
            b, m = s_turn(S_BACK + 2)
            act.wait_ge(tb_ready[b], m + 1)
            act.activation(pr_Tn[0:NS, :], tb[b][0:NS, 0:256], ACT.Copy).then_inc(tb_free[b], 1)
            act.wait_ge(av_done, H * NT + 2 * H)
            b, m = proj(SI, 0, AV)
            act.activation(avs[0:NS, :], pb[b][0:NS, :], ACT.Copy).then_inc(pb_free[b], 1)
            act.wait_ge(o_sq, NT + 1)
            act.activation(st[0:NS, ORT:ORT + H], st[0:NS, OSS:OSS + H], ACT.Sqrt).then_inc(o_root, 1)

            for hp in range(2 * PH):
                act.wait_ge(wk_ready[0], hp + 1)
                act.activation(big[:, 0:4, hp * NK:(hp + 1) * NK],
                               pb[0][:, :].rearrange("p (a b) -> p a b", a=4), ACT.Copy
                               ).then_inc(wk_kept[0], 1)

            def norm_next(t):
                act.wait_ge(xn_sq, t + 1)
                act.activation(gst[:, RT1:RT1 + 1], gst[:, NS1:NS1 + 1], ACT.Sqrt).then_inc(xn_root, 1)

            def keep_turned(t):
                for c in range(2):
                    act.wait_ge(xn_turned, t * 2 + c + 1)
                    act.activation(xnT[:, 4 * c:4 * c + 4, :], tb[c][:, :].rearrange("p (a b) -> p a b", a=4),
                                   ACT.Copy).then_inc(xnT_ready, 1)

            def gates(n, par):
                act.wait_ge(top_ready, n + 1)
                act.activation(ex[:, par, :], top2[:, :], ACT.Exp, bias=gst[:, NTOP + par:NTOP + par + 1],
                               accum_out=gst[:, ESUM + par:ESUM + par + 1]).then_inc(top_exp, 1)

            def gelu(n, par, k):
                act.wait_ge(dots_done, n * NB + k + 1)
                act.activation(hgelu[:, par, k * B:(k + 1) * B], hdot[:, par, k * B:(k + 1) * B],
                               ACT.Gelu).then_inc(gelu_done, 1)

            def step(n, par, after={}):
                for k in range(NB):
                    gelu(n, par, k)
                    if k in after:
                        after[k]()

            def close_sum(t):
                act.wait_ge(x2_sq, t + 1)
                act.activation(gst[:, RT2:RT2 + 1], gst[:, NS2:NS2 + 1], ACT.Sqrt).then_inc(x2_root, 1)

            def gate(t, chosen=None):
                act.wait_ge(r2_ready, t + 1)
                if chosen is not None:
                    act.wait_ge(idx_ready, chosen)
                for c in range(2):
                    hold(act, gate_ready, t * 2 + c + 1)
                    act.wait_ge(sig_read, t * 2 + c + 1)
                    act.activation(sg[:, :], sc[:, 2 + c, :], ACT.Sigmoid, scale=gst[:, R2:R2 + 1]
                                   ).then_inc(sig_ready, 1)
                act.wait_ge(y_sq, t + 1)
                act.activation(gst[:, RT3:RT3 + 1], gst[:, NS3:NS3 + 1], ACT.Sqrt).then_inc(y_root, 1)

            def first_heads(t):
                n = t * PH
                step(n, 0, {0: lambda: (close_sum(t - 1), gates(n + 1, 1)),
                            GATE_AT: lambda: gate(t - 1, n + 2)})
                step(n + 1, 1, {0: lambda: gates(n + 2, 0)})

            def later_heads(t):
                with act.Fori(1, PH // 2 - 1) as hh:
                    for par in range(2):
                        n = t * PH + hh * 2 + par
                        step(n, par, {0: lambda: gates(n + 1, 1 - par)})
                n = t * PH + PH - 2
                step(n, 0, {0: lambda: gates(n + 1, 1), 2: lambda: norm_next(t + 1)})
                step(n + 1, 1, {0: lambda: keep_turned(t + 1), 2: lambda: gates(n + 2, 0)})

            norm_next(0)
            keep_turned(0)
            gates(0, 0)
            step(0, 0, {0: lambda: gates(1, 1)})
            step(1, 1, {0: lambda: gates(2, 0)})
            with act.Fori(0, NT - 1) as t:
                later_heads(t)
                first_heads(t + 1)
            later_heads(NT - 1)
            close_sum(NT - 1)
            gates(N0 + 1, 1)
            gate(NT - 1, N0 + 2)

            def sample_step(s, par, more=True):
                act.wait_ge(dots_done, s * 2 + par + (N0 * NB + 1))
                act.activation(hgelu[:, par, 0:QS], hdot[:, par, 0:QS], ACT.Gelu).then_inc(gelu_done, 1)
                if more:
                    gates(s * 2 + par + (N0 + 2), par)

            with act.Fori(0, PH // 2 - 1) as s:
                for par in range(2):
                    sample_step(s, par)
            for par in range(2):
                sample_step(PH // 2 - 1, par, more=False)
            close_sum(NT)
            gate(NT)

        @block.vector
        def _(dve):
            for a in range(2):
                dve.sem_inc(s_read[a], 1)
            dve.sem_inc(av_done, H)
            dve.sem_inc(sig_read, 1)
            dve.sem_inc(top_exp, 1)
            dve.memset(relb[BUCKETS:BUCKETS + 1, :], NEG)
            dve.memset(kT, 0.0)
            dve.memset(vals, 0.0)
            dve.memset(u_sb[:, 1, :], 0.0).then_inc(zeroed, 1)
            dve.drain()
            dve.wait_ge(const_in, 16 * 14)
            dve.tensor_copy(AT[0:BUCKETS, 0:H, :],
                            relb[0:BUCKETS, :].unsqueeze(2).to_broadcast([BUCKETS, H, T]))
            dve.tensor_copy(AT[BUCKETS:BUCKETS + 1, 0:H, :],
                            relb[BUCKETS:BUCKETS + 1, :].unsqueeze(2).to_broadcast([1, H, T])
                            ).then_inc(gain_ready, 1)
            for a in range(2):
                dve.tensor_tensor_reduce(lam_in[:, 2 * a, :], lam_in[:, 2 * a, :], lam_in[:, 2 * a + 1, :],
                                         1.0, 0.0, ALU.mult, ALU.add, st[:, LAMS + a:LAMS + a + 1]
                                         ).then_inc(lam_sum, 1)
            dve.tensor_scalar(g_sub[:, :], g_sub[:, :], 1.0 - LAM_INIT, None, ALU.mult)
            dve.tensor_copy(pagef, ptab[:, :])
            dve.drain()
            dve.tensor_scalar(pidx[:, :], pagef, float(PAGE), row[:, 0:1], ALU.mult, ALU.add
                              ).then_inc(page_idx, 1)
            dve.wait_ge(lam_exp, 1)
            dve.tensor_tensor(st[:, NLAM:NLAM + 1], st[:, LAME + 1:LAME + 2], st[:, LAME:LAME + 1],
                              ALU.subtract)
            dve.drain()
            dve.tensor_scalar(st[:, NLAM:NLAM + 1], st[:, NLAM:NLAM + 1], LAM_INIT, None, ALU.subtract)
            dve.wait_ge(bias_in, 16)
            dve.tensor_copy(far[:, :], biasw[:, :, 0])

            def mean_eps(cols, width):
                dve.drain()
                return dve.tensor_scalar(cols, cols, 1.0 / width, EPS, ALU.mult, ALU.add)

            def x_stats(i, par, P=T):
                dve.wait_ge(x_in[par], i * 16 + 16)
                dve.tensor_tensor_reduce(sq[0:P, :], xt[0:P, par, :], xt[0:P, par, :], 1.0, 0.0,
                                         ALU.mult, ALU.add, st[0:P, XSS + par:XSS + par + 1])
                mean_eps(st[0:P, XSS + par:XSS + par + 1], D).then_inc(x_sq, 1)

            def x_turned(turn, P=T):
                for c in range(2):
                    b, m = turn(c)
                    dve.wait_ge(tb_ready[b], m + 1)
                    dve.tensor_tensor(xT[:, 4 * c:4 * c + 4, 0:P],
                                      tb[b][:, 0:4 * P].rearrange("p (a b) -> p a b", a=4),
                                      g_attn[:, 4 * c:4 * c + 4].unsqueeze(2).to_broadcast([T, 4, P]),
                                      ALU.mult).then_inc(tb_free[b], 1)

            def x_factor(t, par, P=T):
                dve.wait_ge(x_root, t + 1)
                dve.reciprocal(st[0:P, XR + par:XR + par + 1], st[0:P, XRT + par:XRT + par + 1]
                               ).then_inc(x_norm, 1)

            def pooled(i, par, P=T):
                b, m = proj(i, par, POOL)
                dve.wait_ge(pb_ready[b], m + 1)
                dve.tensor_tensor(xT[:, H:2 * H, 0:P], pb[b][:, 0:H * P].rearrange("p (a b) -> p a b", a=H),
                                  psc[:, :].unsqueeze(2).to_broadcast([T, H, P]), ALU.mult
                                  ).then_inc(pb_free[b], 1)

            def normed_heads(i, par, t, P=T):
                b, m = proj(i, par, AV)
                dve.wait_ge(pb_free[b], m + 2)
                dve.tensor_tensor(sq[0:P, 0:W4], avs[0:P, :], avs[0:P, :], ALU.mult)
                dve.drain()
                dve.tensor_reduce(st[0:P, OSS:OSS + H], sq[0:P, 0:W4].rearrange("p (h d) -> p h d", h=H),
                                  AX.X, ALU.add)
                mean_eps(st[0:P, OSS:OSS + H], HV).then_inc(o_sq, 1)
                dve.wait_ge(o_root, t + 1)
                dve.reciprocal(st[0:P, OREC:OREC + H], st[0:P, ORT:ORT + H])
                dve.drain()
                av = avs[0:P, :].rearrange("p (h d) -> p h d", h=H)
                dve.tensor_tensor(av, av, st[0:P, OREC:OREC + H].unsqueeze(2).to_broadcast([P, H, HV]),
                                  ALU.mult).then_inc(o_norm, 1)

            def finish(i, par, turn, P=T):
                b, m = turn
                dve.wait_ge(tb_ready[b], m + 1)
                dve.tensor_scalar(xT[:, 0:H, 0:P], tb[b][:, 0:H * P].rearrange("p (a b) -> p a b", a=H),
                                  g_sub[:, 0:1], None, ALU.mult).then_inc(tb_free[b], 1)
                for c in range(2):
                    b, m = proj(i, par, WO + c)
                    dve.wait_ge(pb_ready[b], m + 1)
                    cols = slice(c * W4, (c + 1) * W4)
                    dve.tensor_tensor(xt[0:P, par, cols], pb[b][0:P, :], xt[0:P, par, cols], ALU.add
                                      ).then_inc(pb_free[b], 1)

            def tile(R, i, par):
                t = i * 2 + par
                W = R.width
                x_turned(lambda c: R.turn(i, par, c))
                x_stats(i, par)
                x_factor(t, par)

                def scores(h):
                    if h >= 2:
                        hold(dve, av_done, t * H + h - 1 + H)
                    for a in range(2):
                        hold(dve, s_ready[a], t * H + h + 1)
                        dve.scalar_tensor_tensor(
                            out=S[:, h % 2, a, 0:W],
                            in0=sc[:, 2 * a:2 * a + R.nb, :].rearrange("p a b -> p (a b)"), scalar=SCALE,
                            in1=biasw[:, h, ds((NT - 1) * T - t * T, W)],
                            op0=ALU.mult, op1=ALU.add).then_inc(s_read[a], 1)
                    dve.drain()
                    for a in range(2):
                        col = NMAX + 2 * (h % 2) + a
                        dve.tensor_reduce(st[:, col:col + 1], S[:, h % 2, a, 0:W], AX.X, ALU.max,
                                          negate=True).then_inc(s_max[a], 1)

                def combine(h):
                    q = h % 2
                    for a in range(2):
                        dve.wait_ge(s_exp[a], t * H + h + 1)
                    c = LREC + 2 * q
                    dve.reciprocal(st[:, c:c + 2], st[:, LSUM + 2 * q:LSUM + 2 * q + 2])
                    dve.drain()
                    dve.tensor_tensor(st[:, c + 1:c + 2], st[:, c + 1:c + 2], st[:, NLAM:NLAM + 1], ALU.mult)
                    dve.tensor_scalar(S[:, q, 0, 0:W], S[:, q, 0, 0:W], st[:, c:c + 1], None, ALU.mult)
                    dve.drain()
                    dve.scalar_tensor_tensor(out=S[:, q, 0, 0:W], in0=S[:, q, 1, 0:W],
                                             scalar=st[:, c + 1:c + 2], in1=S[:, q, 0, 0:W],
                                             op0=ALU.mult, op1=ALU.add).then_inc(a_ready, 1)

                scores(0)
                scores(1)
                combine(0)
                combine(1)
                pooled(i, par)
                for h in (2, 3):
                    scores(h)
                    combine(h)
                normed_heads(i, par, t)
                finish(i, par, R.o_turn(i, par))

            for R in REGIONS:
                with dve.Fori(R.first, R.last) as i:
                    for par in range(2):
                        tile(R, i, par)

            x_stats(SI, 0, NS)
            x_turned(s_turn, NS)
            x_factor(NT, 0, NS)
            dve.wait_ge(bT_in, 16 * H * (DB + 1))
            dve.tensor_copy(bf_T.rearrange("p (h i) -> p h i", h=H),
                            far[:, :].unsqueeze(2).to_broadcast([T, H, DS]))
            pooled(SI, 0, NS)
            dve.drain()
            dve.wait_ge(ss_ready, 1)
            rows8 = lambda ap: ap.rearrange("p (b c) -> p b c", b=DB)
            per_b = lambda ap: ap.unsqueeze(1).to_broadcast([ap.shape[0], DB, H * DS])
            for a in range(2):
                half_a = slice(a * H * DS, (a + 1) * H * DS)
                for pg in range(NPG):
                    dve.scalar_tensor_tensor(
                        out=rows8(s_T[:, pg * 256:(pg + 1) * 256])[:, :, half_a],
                        in0=rows8(sc[:, a, pg * T:(pg + 1) * T]), scalar=SCALE,
                        in1=per_b(b_raw if pg == NPG - 1 else bf_T), op0=ALU.mult, op1=ALU.add)
                dve.scalar_tensor_tensor(
                    out=rows8(s_Tn[0:NS, :])[:, :, half_a], in0=rows8(sc[0:NS, 2 + a, 0:T]), scalar=SCALE,
                    in1=per_b(bx_raw[0:NS, :]), op0=ALU.mult, op1=ALU.add)
            dve.drain()
            dve.tensor_tensor(rows8(s_Tn[0:NS, :]), rows8(s_Tn[0:NS, :]),
                              mask_s[:, :].unsqueeze(2).to_broadcast([NS, DB, 32]), ALU.add
                              ).then_inc(sT_ready, 1)
            for g in range(2):
                b, m = s_turn(S_ROW + g)
                dve.wait_ge(tb_ready[b], m + 1)
                dve.tensor_copy(s_row[:, g, 0:PAST], tb[b][:, :]).then_inc(tb_free[b], 1)
            b, m = s_turn(S_ROW + 2)
            dve.wait_ge(tb_ready[b], m + 1)
            dve.tensor_copy(s_row[:, :, PAST:PAST + NS], tb[b][:, 0:2 * NS].rearrange("p (g n) -> p g n", g=2)
                            ).then_inc(tb_free[b], 1)
            dve.drain()
            for g in range(2):
                dve.tensor_reduce(st[:, SMX + g:SMX + g + 1], s_row[:, g, :], AX.X, ALU.max, negate=True
                                  ).then_inc(sx_ready, 1)
            dve.wait_ge(sx_exp, 2)
            dve.reciprocal(st[:, SREC:SREC + 2], st[:, SSUM:SSUM + 2])
            dve.tensor_scalar(st[:, SCO:SCO + 1], half[:, 1:2], st[:, NLAM:NLAM + 1], None, ALU.mult)
            dve.drain()
            dve.tensor_tensor(st[:, SCO:SCO + 1], st[:, SCO:SCO + 1], half[:, 0:1], ALU.add)
            dve.drain()
            dve.tensor_scalar(st[:, SREC:SREC + 2], st[:, SREC:SREC + 2], st[:, SCO:SCO + 1], None, ALU.mult)
            dve.drain()
            dve.tensor_tensor(s_row, s_row, st[:, SREC:SREC + 2].unsqueeze(2).to_broadcast([T, 2, 544]),
                              ALU.mult).then_inc(sp_ready, 1)
            dve.wait_ge(page_read, 2 * DB * NPG)
            dve.tensor_copy(o_ps, sc[:, 3, 0:256])
            dve.drain()
            ov = o_ps.rearrange("p (b h a i) -> p b h a i", b=DB, h=H, a=2)
            dve.tensor_tensor(o_T.rearrange("p (h b i) -> p b h i", h=H, b=DB), ov[:, :, :, 0, :],
                              ov[:, :, :, 1, :], ALU.add).then_inc(o_sum, 1)
            normed_heads(SI, 0, NT, NS)
            finish(SI, 0, s_turn(S_O), NS)

            for hp in range(2 * PH):
                dve.wait_ge(wk_ready[1], hp + 1)
                dve.tensor_copy(big[:, 4:8, hp * NK:(hp + 1) * NK],
                                pb[1][:, :].rearrange("p (a b) -> p a b", a=4)).then_inc(wk_kept[1], 1)

            def norm_next(t):
                dve.wait_ge(xn_in, t * 16 + 16)
                dve.tensor_tensor_reduce(junk, xn_next[:, :], xn_next[:, :], 1.0, 0.0, ALU.mult,
                                         ALU.add, gst[:, NS1:NS1 + 1])
                mean_eps(gst[:, NS1:NS1 + 1], D).then_inc(xn_sq, 1)
                dve.wait_ge(xn_root, t + 1)
                dve.reciprocal(gst[:, R1:R1 + 1], gst[:, RT1:RT1 + 1])
                dve.drain()
                dve.scalar_tensor_tensor(out=xn_next[:, :], in0=xn_next[:, :], scalar=gst[:, R1:R1 + 1],
                                         in1=g_ffn[:, :], op0=ALU.mult, op1=ALU.mult).then_inc(xn_ready, 1)

            def own_quarter(dst, src):
                own = cand_lo[:, TOPK:2 * TOPK].rearrange("p (j q) -> p j q", q=COPIES)
                dve.tensor_tensor(own,
                                  src.rearrange("p (j q) -> p j q", q=COPIES),
                                  copy[:, :].unsqueeze(1).to_broadcast([T, QS, COPIES]), ALU.mult)
                dve.drain()
                dve.tensor_reduce(pick[:, 0, 0:QS], own, AX.X, ALU.add)
                dve.drain()
                return dve.tensor_copy(dst, pick[:, 0, 0:QS])

            def choose(n, par, copies=False):
                dve.wait_ge(route_ready, n + 1)
                dve.tensor_copy(sc_sb[:, :], pb[0][:, 0:256]).then_inc(route_read, 1)
                dve.drain()
                seg = [slice(s * NK, (s + 1) * NK) for s in range(2)]
                for s in range(2):
                    dve.max(top1[:, s, 0:8], sc_sb[:, seg[s]])
                dve.drain()
                for s in range(2):
                    dve.match_replace(sc_lo[:, seg[s]], top1[:, s, 0:8], sc_sb[:, seg[s]], FMAX)
                    dve.max_index(ind1[:, s, 0:8], top1[:, s, 0:8], sc_sb[:, seg[s]])
                dve.drain()
                for s in range(2):
                    dve.max(top1[:, s, 8:16], sc_lo[:, seg[s]])
                dve.drain()
                pairs = lambda ap: ap.rearrange("p (i j) -> p i j", i=TOPK)
                over_j = lambda ap: ap.unsqueeze(2).to_broadcast([T, TOPK, TOPK])
                over_i = lambda ap: ap.unsqueeze(1).to_broadcast([T, TOPK, TOPK])
                dve.tensor_tensor(pairs(cand[:, :]), over_j(top1[:, 0, :]), over_i(top1[:, 1, :]), ALU.add)
                for s in range(2):
                    dve.max_index(ind1[:, s, 8:16], top1[:, s, 8:16], sc_lo[:, seg[s]])
                hold(dve, top_exp, n + 1)
                dve.drain()
                dve.max(top2[:, 0:8], cand[:, :])
                dve.drain()
                dve.match_replace(cand_lo[:, :], top2[:, 0:8], cand[:, :], FMAX)
                dve.max_index(ind2[:, 0:8], top2[:, 0:8], cand[:, :])
                dve.drain()
                dve.max(top2[:, 8:16], cand_lo[:, :])
                dve.tensor_scalar(gst[:, NTOP + par:NTOP + par + 1], top2[:, 0:1], -1.0, None, ALU.mult
                                  ).then_inc(top_ready, 1)
                dve.tensor_copy(ind1f[:, :, :], ind1[:, :, :])
                dve.drain()
                dve.max_index(ind2[:, 8:16], top2[:, 8:16], cand_lo[:, :])
                dve.drain()
                dve.tensor_scalar(ab[:, 0, :], ind2[:, :], 4, None, ALU.logical_shift_right)
                dve.tensor_scalar(ab[:, 1, :], ind2[:, :], 15, None, ALU.bitwise_and)
                dve.drain()
                dve.tensor_copy(abf[:, :, :], ab[:, :, :])
                dve.drain()
                tmp = (cand, cand_lo)
                for s in range(2):
                    dve.tensor_tensor(pairs(tmp[s][:, :]), over_j(abf[:, s, :]), over_i(iota[:, :]),
                                      ALU.is_equal)
                dve.drain()
                for s in range(2):
                    dve.tensor_tensor(pairs(tmp[s][:, :]), pairs(tmp[s][:, :]), over_i(ind1f[:, s, :]),
                                      ALU.mult)
                dve.drain()
                for s in range(2):
                    dve.tensor_reduce(pick[:, s, :], pairs(tmp[s][:, :]), AX.X, ALU.add)
                dve.drain()
                if copies:
                    dve.scalar_tensor_tensor(out=cand_lo[:, 0:TOPK], in0=pick[:, 0, :], scalar=float(NK),
                                             in1=pick[:, 1, :], op0=ALU.mult, op1=ALU.add)
                    dve.drain()
                    own_quarter(idx[:, par, 0:QS], cand_lo[:, 0:TOPK]).then_inc(idx_ready, 1)
                else:
                    dve.scalar_tensor_tensor(out=idx[:, par, :], in0=pick[:, 0, :], scalar=float(NK),
                                             in1=pick[:, 1, :], op0=ALU.mult, op1=ALU.add
                                             ).then_inc(idx_ready, 1)

            def gates(n, par):
                dve.wait_ge(top_exp, n + 2)
                dve.reciprocal(gst[:, EREC + par:EREC + par + 1], gst[:, ESUM + par:ESUM + par + 1])
                dve.drain()
                dve.tensor_scalar(gate[:, par, :], ex[:, par, :], gst[:, EREC + par:EREC + par + 1], None,
                                  ALU.mult)

            def sample_gates(n, par):
                gates(n, par)
                dve.drain()
                own_quarter(gate[:, par, 0:QS], gate[:, par, :])

            def dot(r, par, j, use):
                dve.wait_ge(gathered[r], use)
                return dve.tensor_tensor_reduce(ring[:, r, 0:D], ring[:, r, 0:D], xn_cur[:, :],
                                                1.0, 0.0, ALU.mult, ALU.add, hdot[:, par, j:j + 1])

            def dots(n, par, k):
                for j in range(k * B, (k + 1) * B):
                    ins = dot(j % RING, par, j, n * 32 + (j // RING) * 16 + 16)
                ins.then_inc(dots_done, 1)

            def coefficients(n, par, k):
                dve.wait_ge(gelu_done, n * NB + k + 1)
                hold(dve, slot_free, n * TOPK + (k + 1) * B)
                for j in range(k * B, (k + 1) * B):
                    ins = dve.tensor_scalar(diag[:, j % RING, :], ident[:, :], hgelu[:, par, j:j + 1],
                                            gate[:, par, j:j + 1], ALU.mult, ALU.mult)
                ins.then_inc(diag_ready, 1)

            def step(n, par, after={}, dotted={}):
                for k in range(NB):
                    dots(n, par, k)
                    if k in dotted:
                        dotted[k]()
                    coefficients(n, par, k)
                    if k in after:
                        after[k]()

            def close_sum(t, slots=PH * TOPK):
                dve.wait_ge(x1_in, t * 16 + 16)
                hold(dve, slot_free, t * (PH * TOPK) + slots + RING)
                for c in range(2):
                    half_c = slice(c * W4, (c + 1) * W4)
                    dve.tensor_tensor(x2[:, half_c], x2[:, half_c], sc[:, c, :], ALU.add).then_inc(x2_ready, 1)
                for c in range(2):
                    dve.wait_ge(x2_turned, t * 2 + c + 1)
                    dve.tensor_tensor(x2T[:, 4 * c:4 * c + 4, :],
                                      tb[c][:, :].rearrange("p (a b) -> p a b", a=4),
                                      g_pl[:, 4 * c:4 * c + 4].unsqueeze(2).to_broadcast([T, 4, T]),
                                      ALU.mult).then_inc(x2T_ready, 1)
                dve.tensor_tensor_reduce(junk, x2[:, :], x2[:, :], 1.0, 0.0, ALU.mult, ALU.add,
                                         gst[:, NS2:NS2 + 1])
                mean_eps(gst[:, NS2:NS2 + 1], D).then_inc(x2_sq, 1)
                dve.wait_ge(x2_root, t + 1)
                dve.reciprocal(gst[:, R2:R2 + 1], gst[:, RT2:RT2 + 1]).then_inc(r2_ready, 1)

            def open_tile():
                dve.tensor_copy(xn_cur[:, :], xn_next[:, :]).then_inc(xn_moved, 1)
                dve.drain()

            def gate_and_embed(t):
                for c in range(2):
                    half_c = slice(c * W4, (c + 1) * W4)
                    hold(dve, sig_ready, t * 2 + c + 1)
                    dve.wait_ge(ple_ready, t * 2 + c + 1)
                    dve.tensor_tensor(sg[:, :], sg[:, :], (pb[1], tb[1])[c][:, :], ALU.mult
                                      ).then_inc(ple_read, 1)
                    dve.drain()
                    dve.tensor_tensor(x2[:, half_c], x2[:, half_c], sg[:, :], ALU.add).then_inc(sig_read, 1)
                dve.drain()
                dve.tensor_tensor_reduce(junk, x2[:, :], x2[:, :], 1.0, 0.0, ALU.mult, ALU.add,
                                         gst[:, NS3:NS3 + 1])
                mean_eps(gst[:, NS3:NS3 + 1], D).then_inc(y_sq, 1)
                dve.wait_ge(y_root, t + 1)
                dve.reciprocal(gst[:, R3:R3 + 1], gst[:, RT3:RT3 + 1])
                dve.drain()
                dve.scalar_tensor_tensor(out=x2[:, :], in0=x2[:, :], scalar=gst[:, R3:R3 + 1],
                                         in1=g_fin[:, :], op0=ALU.mult, op1=ALU.mult).then_inc(y_ready, 1)

            def first_heads(t):
                n = t * PH
                open_tile()
                step(n, 0, {0: lambda: choose(n + 1, 1), 4: lambda: gates(n + 1, 1),
                            GATE_AT: lambda: gate_and_embed(t - 1)},
                     {0: lambda: close_sum(t - 1)})
                step(n + 1, 1, {0: lambda: choose(n + 2, 0), 4: lambda: gates(n + 2, 0)})

            def later_heads(t, copies=False):
                with dve.Fori(1, PH // 2 - 1) as hh:
                    for par in range(2):
                        n = t * PH + hh * 2 + par
                        step(n, par, {0: lambda: choose(n + 1, 1 - par), 4: lambda: gates(n + 1, 1 - par)})
                n = t * PH + PH - 2
                step(n, 0, {0: lambda: choose(n + 1, 1), 2: lambda: norm_next(t + 1),
                            4: lambda: gates(n + 1, 1)})
                step(n + 1, 1, {2: lambda: choose(n + 2, 0, copies),
                                5: lambda: (sample_gates if copies else gates)(n + 2, 0)})

            dve.wait_ge(g_in, 16 * 7)
            norm_next(0)
            choose(0, 0)
            gates(0, 0)
            dve.drain()
            open_tile()
            step(0, 0, {0: lambda: choose(1, 1), 4: lambda: gates(1, 1)})
            step(1, 1, {0: lambda: choose(2, 0), 4: lambda: gates(2, 0)})
            with dve.Fori(0, NT - 1) as t:
                later_heads(t)
                first_heads(t + 1)
            later_heads(NT - 1, copies=True)
            open_tile()
            close_sum(NT - 1)
            choose(N0 + 1, 1, True)
            sample_gates(N0 + 1, 1)
            gate_and_embed(NT - 1)

            def sample_step(s, par, more=True):
                for j in range(QS):
                    ins = dot(par * QS + j, par, j, s * 16 + (N0 * 32 + 16))
                ins.then_inc(dots_done, 1)
                if more:
                    choose(s * 2 + par + (N0 + 2), par, True)
                dve.wait_ge(gelu_done, s * 2 + par + (N0 * NB + 1))
                hold(dve, slot_free, (s * 2 + par) * QS + (N0 * TOPK + QS))
                for j in range(QS):
                    ins = dve.tensor_scalar(diag[:, par * QS + j, :], fold[:, :], hgelu[:, par, j:j + 1],
                                            gate[:, par, j:j + 1], ALU.mult, ALU.mult)
                ins.then_inc(diag_ready, 1)
                if more:
                    sample_gates(s * 2 + par + (N0 + 2), par)

            with dve.Fori(0, PH // 2 - 1) as s:
                for par in range(2):
                    sample_step(s, par)
            for par in range(2):
                sample_step(PH // 2 - 1, par, more=False)
            close_sum(NT, PH * QS)
            gate_and_embed(NT)


def onehot_buckets():
    n = SPAN + T - 1 - np.arange(STRIP)
    exact = BUCKETS // 2
    pos = np.maximum(n, 1).astype(np.float32) / np.float32(exact)
    large = exact + (np.log(pos) / np.float32(np.log(MAX_DIST / exact)) * np.float32(BUCKETS - exact)
                     ).astype(np.int32)
    bucket = np.where(n < exact, n, np.minimum(large, BUCKETS - 1))
    bucket = np.where(n < 0, BUCKETS, bucket)
    return (np.arange(BUCKETS + 1)[:, None] == bucket[None, :]).astype(np.float32)


def bands():
    cur = np.zeros((NT, T, H, T), np.float32)
    prev = np.zeros((T, H, T), np.float32)
    s, t = np.arange(T)[:, None], np.arange(T)[None, :]
    for g, w in enumerate(WINDOWS):
        inside = ((s <= t) & (s > t - w)).astype(np.float32)
        for k in range(NT):
            cur[k, :, g, :] = inside / np.minimum(k * T + t + 1, w) - (s == t)
        prev[:, g, :] = (s - T > t - w) / np.float32(w)
    return cur.reshape(NT * T, H * T), prev


def sample_bands():
    cur = np.zeros((NS, H, NS), np.float32)
    old = np.zeros((DB * PAD, H, NS), np.float32)
    for g, w in enumerate(WINDOWS):
        for b in range(DB):
            for i in range(DS):
                at = PAD + i
                for r in range(at - w + 1, at + 1):
                    if r < PAD:
                        old[b * PAD + r, g, b * DS + i] += 1.0 / w
                    else:
                        cur[b * DS + r - PAD, g, b * DS + i] += 1.0 / w
                cur[b * DS + i, g, b * DS + i] -= 1.0
    return cur.reshape(NS, H * NS), old.reshape(DB * PAD, H * NS)


_OUTS = [(SEQ, D), (NS, D), (SEQ, W4), (SEQ, W4), (PAD, W4), (NS, W4), (NS, W4), (DB, PAD, W4)]
_SHAPES = [(1, SEQ, D), (DB, DS, D), (1, 1, SEQ, H, 2 * QK), (1, 1, SEQ, H, HV), (1, 1, PAD, W4),
           (1, DB, DS, H, 2 * QK), (1, DB, DS, H, HV), (1, DB, PAD, W4)]


def kernel(**inputs):
    import concourse.bacc as bacc
    from concourse.bass_utils import run_bass_kernel_spmd

    a = {k: np.asarray(v) for k, v in inputs.items()}
    cur, prev = bands()
    s_cur, s_old = sample_bands()
    rows = np.arange(T)
    mask = np.where(np.arange(NS)[:, None] // DS == np.arange(DB)[None, :], 0.0, NEG).astype(np.float32)
    first_half = (rows // (H * DS)) % 2 == 0
    laid = [
        ("x", a["x_prompt"].reshape(SEQ, D)), ("xs", a["x_sample"].reshape(NS, D)),
        ("cache_k", a["cache_k"].reshape(-1, W4)), ("cache_v", a["cache_v"].reshape(-1, W4)),
        ("page_table", a["page_table"]), ("state", a["state_pool"].reshape(DB * PAD, W4)),
        ("p_t", np.concatenate([a["p_prompt"].reshape(SEQ, PLE), a["p_sample"].reshape(NS, PLE),
                                np.zeros((T - NS, PLE), np.float32)]).T),
        ("norm_attn_g", a["norm_attn_g"].reshape(KD, T).T), ("w_in", a["w_in"][0]),
        ("lams", np.concatenate([a["lambda_q1"], a["lambda_k1"], a["lambda_q2"], a["lambda_k2"]])),
        ("subln_g", a["subln_g"].reshape(HV, 1)), ("rel_bias", a["rel_bias"]),
        ("pool_w", a["pool_w"][0].transpose(1, 0, 2)), ("pool_scale", a["pool_scale"].reshape(H, T).T),
        ("w_out", a["w_out"][0]), ("norm_ffn_g", a["norm_ffn_g"].reshape(D)),
        ("wq_t", a["peer_wq"][0].T), ("keys_t", a["peer_keys"].reshape(2 * PH, NK, NK).transpose(0, 2, 1)),
        ("uv", np.concatenate([a["peer_u"][0], a["peer_v"][0]], axis=1)),
        ("norm_pl_g", a["norm_pl_g"].reshape(KD, T).T), ("w_pl", a["w_pl"][0]),
        ("w_gate", a["w_pl_gate"][0]), ("final_g", a["final_norm_g"]),
        ("c_ident", np.eye(T, dtype=np.float32)), ("c_onehot", onehot_buckets()),
        ("c_bands", cur), ("c_band_prev", prev), ("c_band_s", s_cur), ("c_band_sp", s_old),
        ("c_mask_s", mask), ("c_half", np.stack([first_half, ~first_half], 1).astype(np.float32)),
        ("c_row", rows.astype(np.float32)[:, None]), ("c_iota", np.arange(TOPK, dtype=np.float32)),
        ("c_fold", (rows[:, None] % NS == rows[None, :] % NS).astype(np.float32)),
        ("c_copy", (rows[:, None] // NS == np.arange(COPIES)[None, :]).astype(np.float32)),
    ]
    nc = bacc.Bacc("TRN2", target_bir_lowering=False, num_devices=1)
    arrays, args = {}, []
    for name, v in laid:
        v = np.ascontiguousarray(v)
        arrays[f"in_{name}"] = v
        args.append(nc.dram_tensor(f"in_{name}", v.shape, mybir.dt.from_np(v.dtype), kind="ExternalInput").ap())
    outs = [nc.dram_tensor(f"out_{i}", s, mybir.dt.float32, kind="ExternalOutput").ap()
            for i, s in enumerate(_OUTS)]
    front_and_experts(nc, *args, outs)
    r = run_bass_kernel_spmd(nc, [arrays], core_ids=[0])
    return tuple(r.results[0][f"out_{i}"].reshape(s) for i, s in enumerate(_SHAPES))
```

```python
from contextlib import ExitStack

import numpy as np

import concourse.bass as bass
from concourse import mybir

D = 1024
T = 128
SEQ = 1024
NT = SEQ // T
DB, DS = 8, 4
NS = DB * DS
PAST, PAGE = 512, 128
NPG = PAST // PAGE
H = 4
QK = 64
HV = 128
W4 = 512
WINDOWS = (2, 4, 8, 16)
PAD = 15
KD = D // 128
GATE_AT = 6
BUCKETS, MAX_DIST = 32, 128
PH, NK, TOPK = 8, 128, 16
PLE = 256
EPS = 1e-6
NEG = -1e30
LAM_INIT = 0.2
SCALE = QK ** -0.5
FMAX = -3.0e38
RING = 8
PAGES = 16
B = 2
NB = TOPK // B
COPIES = T // NS
SG = PH // COPIES
N0 = NT * PH
SPAN = (NT - 1) * T
BW = 1408
STRIP = 1536
PT_P = 9


def front_and_experts(nc, x, xs, cache_k, cache_v, page_table, state, p_t, norm_attn_g, w_in,
                      lams, subln_g, rel_bias, pool_w, pool_scale, w_out, norm_ffn_g, wq_t,
                      keys_t, uv, norm_pl_g, w_pl, w_gate, final_g, c_ident, c_onehot, c_bands,
                      c_band_prev, c_band_s, c_band_sp, c_mask_s, c_half, c_row, c_iota,
                      c_fold, c_pick_h, outs):
    (y_p, y_s, nk_p, nv_p, npool_p, nk_s, nv_s, npool_s) = outs
    f32, i32, u32, bf16 = mybir.dt.float32, mybir.dt.int32, mybir.dt.uint32, mybir.dt.bfloat16
    ALU, ACT, AX = mybir.AluOpType, mybir.ActivationFunctionType, mybir.AxisListType
    ds = bass.ds

    x1_d = nc.dram_tensor("x1_scratch", ((NT + 1) * T, D), f32, kind="Internal").ap()
    strip_h = nc.dram_tensor("strip_scratch", (H * T * STRIP,), f32, kind="Internal")
    strip_d = strip_h.ap()

    def strip_view(offset, dims):
        return bass.AP(tensor=strip_d.tensor, offset=offset, ap=dims)

    with ExitStack() as whole:
        def sb(name, shape, dt=f32, stack=whole):
            return stack.enter_context(nc.sbuf_tensor(name, shape, dt))

        def sem(name):
            return whole.enter_context(nc.semaphore(name))

        big = sb("big", [T, KD, 2048])
        mid = sb("mid", [T, KD, D])
        ring = sb("ring", [T, RING, 2 * D])
        ident = sb("ident", [T, T])
        rf = ring[:, :, :].rearrange("p a b -> p (a b)")

        def part(at, *shape):
            n = int(np.prod(shape))
            v = rf[:, at:at + n]
            if len(shape) == 2:
                return v.rearrange("p (a b) -> p a b", b=shape[1])
            return v

        kT = part(0, H, SEQ)
        vals = part(4096, NT, W4)
        biasw = part(8192, H, BW)
        q_sb = part(13824, W4)
        k_sb = part(14336, W4)
        qT = part(14848, H, T)
        dT = part(15360, H, T)
        bandc = part(15872, H, T)
        pages_a = part(0, PAGES // 2, W4)
        pkT = part(4096, 2, W4)
        s_T = part(5120, NPG * 256)
        o_rows = part(5120, 2, W4)
        s_Tn = part(6144, 256)
        s_row = part(6400, 2, 544)
        pr_T = part(7488, NPG * 256)
        pr_Tn = part(8512, 256)
        st_sb = part(9152, W4)
        kTs = part(9792, H * NS)
        bf_T = part(9920, H * DS)
        b_raw = part(9936, H * DS)
        bx_raw = part(9952, H * DS)
        q_bd = part(9984, 2 * H * NS)
        pick_h = part(10240, 2, H * NS)
        wq_b = part(10496, D)
        keys_sb = part(11520, 2 * PH, NK)

        with ExitStack() as first:
            def fb(name, shape, dt=f32):
                return sb(name, shape, dt, first)

            S = fb("S", [T, 2, 2, SEQ])
            bandp = fb("bandp", [T, H, T])
            xt = fb("xt", [T, 2, D])
            xT = fb("xT", [T, KD, T])
            u_sb = fb("u_sb", [T, 2, W4])
            AT = fb("AT", [T, KD, T])
            pw = fb("pw", [T, H, T])
            bs_c = fb("bs_c", [NS, H * NS])
            bs_p = fb("bs_p", [DB * PAD, H * NS])
            avs = fb("avs", [T, W4])
            g_attn = fb("g_attn", [T, KD])
            g_sub = fb("g_sub", [T, 1])
            psc = fb("psc", [T, H])
            lam_in = fb("lam_in", [T, 4, QK])
            relb = fb("relb", [BUCKETS + 1, H])
            ptab = fb("ptab", [T, DB * NPG], i32)
            pidx = fb("pidx", [T, DB * NPG], i32)
            mask_s = fb("mask_s", [NS, DB])
            half = fb("half", [T, 2])
            pagef = fb("pagef", [T, DB * NPG])[:, :]
            row = fb("row", [T, 1])
            far = fb("far", [T, H])
            st = fb("st", [T, 48])
            sq = AT[:, :, :].rearrange("p a b -> p (a b)")
        wq_st = (xt[:, 1, :], wq_b)
        pages_b = S[:, :, :, :].rearrange("p a b c -> p (a b c)").rearrange("p (r n) -> p r n", n=W4)
        XSS, XRT, XR = 0, 2, 4
        LAMS, LAME, NLAM = 6, 8, 10
        NMAX, LSUM, LREC = 12, 16, 20
        OSS, ORT, OREC = 24, 28, 32
        SMX, SSUM, SREC, SCO = 36, 38, 40, 42

        with ExitStack() as second:
            def gb(name, shape, dt=f32):
                return sb(name, shape, dt, second)

            xn_next = gb("xn_next", [T, D])
            g_ffn = gb("g_ffn", [T, D])
            xnT = gb("xnT", [T, KD, T])
            sg = gb("sg", [T, W4])
            junk = sg[:, :].bitcast(bf16)
            gst = gb("gst", [T, 16])
            sc_sb = gb("sc_sb", [T, 256])
            sc_lo = sg[:, 0:256]
            cand = sg[:, 256:512]
            cand_lo = sc_sb
            iota = gb("iota", [T, TOPK])
            top1 = gb("top1", [T, 2, TOPK])
            ind1 = gb("ind1", [T, 2, TOPK], u32)
            ind1f = gb("ind1f", [T, 2, TOPK])
            top2 = gb("top2", [T, TOPK])
            ind2 = gb("ind2", [T, TOPK], u32)
            ab = gb("ab", [T, 2, TOPK], u32)
            abf = gb("abf", [T, 2, TOPK])
            pick = gb("pick", [T, 2, TOPK])
            idx = gb("idx", [T, 2, TOPK], i32)
            gate = gb("gate", [T, 2, TOPK])
            ex = gb("ex", [T, 2, TOPK])
            xn_cur = gb("xn_cur", [T, D])
            x2 = gb("x2", [T, D])
            g_fin = gb("g_fin", [T, D])
            wpl = gb("wpl", [T, 2, D])
            p_sb = gb("p_sb", [T, 2, T])
            diag = gb("diag", [T, RING, T])
            x2T = gb("x2T", [T, KD, T])
            g_pl = gb("g_pl", [T, KD])
            hdot = gb("hdot", [T, 2, TOPK])
            hgelu = gb("hgelu", [T, 2, TOPK])
            fold = gb("fold", [T, T])
        NS1, RT1, R1 = 0, 1, 2
        NS2, RT2, R2 = 3, 4, 5
        NS3, RT3, R3 = 6, 7, 8
        NTOP, ESUM, EREC = 10, 12, 14

        sc = whole.enter_context(nc.psum_tensor("sc", [T, 4, 512], f32))
        pb = [whole.enter_context(nc.psum_tensor(f"proj{i}", [T, 512], f32)) for i in range(2)]
        tb = [whole.enter_context(nc.psum_tensor(f"turn{i}", [T, 512], f32)) for i in range(2)]

        const_in = sem("const_in")
        w_in_in = [sem(f"w_in_in{c}") for c in range(4)]
        w_out_in = sem("w_out_in")
        onehot_in = sem("onehot_in")
        strip_ps = sem("strip_ps")
        strip_sb = sem("strip_sb")
        strip_out = [sem(f"strip_out{i}") for i in range(2)]
        bias_in = sem("bias_in")
        gain_ready = sem("gain_ready")
        lam_sum = sem("lam_sum")
        lam_exp = sem("lam_exp")
        zeroed = sem("zeroed")
        x_in = [sem(f"x_in{i}") for i in range(2)]
        band_in = sem("band_in")
        x_sq = sem("x_sq")
        x_root = sem("x_root")
        x_norm = sem("x_norm")
        pb_ready = [sem(f"proj_ready{i}") for i in range(2)]
        pb_free = [sem(f"proj_free{i}") for i in range(2)]
        tb_ready = [sem(f"turn_ready{i}") for i in range(2)]
        tb_free = [sem(f"turn_free{i}") for i in range(2)]
        s_ready = [sem(f"score_ready{i}") for i in range(2)]
        s_read = [sem(f"score_read{i}") for i in range(2)]
        s_max = [sem(f"score_max{i}") for i in range(2)]
        s_exp = [sem(f"score_exp{i}") for i in range(2)]
        a_ready = sem("a_ready")
        av_done = sem("av_done")
        o_sq = sem("o_sq")
        o_root = sem("o_root")
        o_norm = sem("o_norm")
        k_out = sem("k_out")
        v_out = sem("v_out")
        new_rows_out = sem("new_rows_out")
        x1_out = [sem(f"x1_out{i}") for i in range(2)]
        turns = sem("turns")
        st_in = sem("st_in")
        page_idx = sem("page_idx")
        page_in = [sem(f"page_in{i}") for i in range(PAGES)]
        page_read = sem("page_read")
        ss_ready = sem("ss_ready")
        bT_in = sem("bT_in")
        sT_ready = sem("sT_ready")
        sx_ready = sem("sx_ready")
        sx_exp = sem("sx_exp")
        sp_ready = sem("sp_ready")
        q_zero = sem("q_zero")
        o_kept = sem("o_kept")
        wq_in = [sem(f"wq_in{i}") for i in range(2)]
        keys_in = sem("keys_in")
        wk_ready = [sem(f"wk_ready{i}") for i in range(2)]
        wk_kept = [sem(f"wk_kept{i}") for i in range(2)]
        gate_w_in = sem("gate_w_in")
        g_in = sem("g_in")
        early_in = sem("early_in")
        xn_in = sem("xn_in")
        xn_sq = sem("xn_sq")
        xn_root = sem("xn_root")
        xn_ready = sem("xn_ready")
        xn_turned = sem("xn_turned")
        xnT_ready = sem("xnT_ready")
        xn_moved = sem("xn_moved")
        x1_in = sem("x1_in")
        p_in = sem("p_in")
        route_ready = sem("route_ready")
        route_read = sem("route_read")
        top_ready = sem("top_ready")
        top_exp = sem("top_exp")
        idx_ready = sem("idx_ready")
        gathered = [sem(f"gathered{i}") for i in range(RING)]
        slot_free = sem("slot_free")
        dots_done = sem("dots_done")
        gelu_done = sem("gelu_done")
        diag_ready = sem("diag_ready")
        x2_ready = sem("x2_ready")
        x2_sq = sem("x2_sq")
        x2_root = sem("x2_root")
        r2_ready = sem("r2_ready")
        x2_turned = sem("x2_turned")
        x2T_ready = sem("x2T_ready")
        gate_ready = sem("gate_ready")
        ple_ready = sem("ple_ready")
        ple_read = sem("ple_read")
        sig_ready = sem("sig_ready")
        sig_read = sem("sig_read")
        y_sq = sem("y_sq")
        y_root = sem("y_root")
        y_ready = sem("y_ready")
        y_out = sem("y_out")

        block = whole.enter_context(nc.Block())

        def hold(eng, s, value):
            eng.wait_ge(s, value)
            eng.sem_inc(turns, 1)

        def page(n):
            r = n % PAGES
            return pages_a[:, r, :] if r < PAGES // 2 else pages_b[:, r - PAGES // 2, :]

        def proj(i, par, o):
            n = par * PT_P + o
            return n % 2, i * PT_P + n // 2
        Q_, K_, U_, V_, BAND, POOL, AV, WO = range(8)
        COLUMNS = {Q_: 0, K_: 1, V_: 2, U_: 3}

        class Region:
            def __init__(self, first, last, width, before):
                self.first, self.last, self.width = first, last, width
                self.nb = width // 512
                self.per = 5 + H * self.nb
                self.before = before
                self.after = before + (last - first) * self.per

            def turn(self, i, par, o):
                n = par * self.per + o
                return n % 2, (i - self.first) * self.per + self.before + n // 2

            def a_turn(self, i, par, h, c):
                return self.turn(i, par, 4 + h * self.nb + c)

            def o_turn(self, i, par):
                return self.turn(i, par, 4 + H * self.nb)

        RA = Region(0, 2, 512, 0)
        RB = Region(2, 4, 1024, RA.after)
        REGIONS = (RA, RB)
        ST0 = RB.after
        SI = NT // 2

        def s_turn(o):
            return o % 2, ST0 + o // 2
        S_PAGE, S_ROW, S_BACK, S_O = 4, 36, 39, 42

        @block.sync
        def _(sp):
            for dst, src in (
                (ident[:, :], c_ident), (bandp[:, :, :], c_band_prev), (pw[:, :, :], pool_w),
                (bs_c[:, :], c_band_s), (bs_p[:, :], c_band_sp), (g_attn[:, :], norm_attn_g),
                (g_sub[:, :], subln_g), (psc[:, :], pool_scale),
                (relb[0:BUCKETS, :], rel_bias), (mask_s[:, :], c_mask_s), (half[:, :], c_half),
                (row[:, :], c_row),
                (ptab[:, :], page_table.rearrange("a b -> (a b)").partition_broadcast(T)),
                (lam_in[:, :, :], lams.partition_broadcast(T)),
            ):
                sp.dma_start(dst, src).then_inc(const_in, 16)
            sp.dma_start(mid[0:BUCKETS + 1, 0:2, 0:768],
                         c_onehot.rearrange("p (a b) -> p a b", b=768)).then_inc(onehot_in, 16)
            sp.dma_start(xt[:, 0, :], x[0:T, :]).then_inc(x_in[0], 16)
            for h, o in enumerate((Q_, K_, U_, V_)):
                c = COLUMNS[o]
                sp.dma_start(big[:, :, c * W4:(c + 1) * W4],
                             w_in[:, c * W4:(c + 1) * W4].rearrange("(k p) n -> p k n", p=T)
                             ).then_inc(w_in_in[c], 16)
                if h == 0:
                    sp.dma_start(bandc, c_bands[0:T, :].rearrange("p (g t) -> p g t", g=H)
                                 ).then_inc(band_in, 16)
                if h == 1:
                    sp.dma_start(xt[:, 1, :], x[T:2 * T, :]).then_inc(x_in[1], 16)
                sp.wait_ge(strip_sb, h + 1)
                sp.dma_start(strip_view(h * T * STRIP, [[STRIP, T], [1, STRIP]]),
                             S[:, h % 2, :, :].rearrange("p a b -> p (a b)")[:, 0:STRIP]
                             ).then_inc(strip_out[h % 2], 16)
            sp.wait_ge(strip_out[0], 16 * H // 2)
            sp.wait_ge(strip_out[1], 16 * H // 2)
            sp.dma_start(biasw, strip_view(T - 1, [[STRIP - 1, T], [T * STRIP, H], [1, BW]])
                         ).then_inc(bias_in, 16)
            for c in range(2):
                sp.dma_start(mid[:, :, c * W4:(c + 1) * W4],
                             w_out[:, c * W4:(c + 1) * W4].rearrange("(k p) n -> p k n", p=T)
                             ).then_inc(w_out_in, 16)
            with sp.Fori(1, NT // 2) as i:
                for par in range(2):
                    b, m = proj(i - 1, par, BAND)
                    sp.wait_ge(pb_ready[b], m + 1)
                    sp.dma_start(bandc, c_bands[ds(i * (2 * T) + (par - 1) * T, T), :].rearrange(
                        "p (g t) -> p g t", g=H)).then_inc(band_in, 16)
                    sp.wait_ge(x1_out[par], i * 16)
                    sp.dma_start(xt[:, par, :], x[ds(i * (2 * T) + par * T, T), :]
                                 ).then_inc(x_in[par], 16)
            b, m = proj(SI - 1, 0, BAND)
            sp.wait_ge(pb_ready[b], m + 1)
            sp.dma_start(bandc, c_bands[SEQ - T:SEQ, :].rearrange("p (g t) -> p g t", g=H)
                         ).then_inc(band_in, 16)
            sp.wait_ge(x1_out[0], 16 * SI)
            sp.dma_start(xt[0:NS, 0, :], xs).then_inc(x_in[0], 16)
            sp.wait_ge(av_done, H * NT + H)
            sp.dma_start(st_sb[0:DB * PAD, :], state).then_inc(st_in, 16)
            sp.dma_start(pick_h, c_pick_h.rearrange("p (g n) -> p g n", g=2)).then_inc(st_in, 16)
            near0 = SPAN + T - 1 - T
            with nc.allow_non_contiguous_dma(reason="small bias tables"):
                for h in range(H):
                    sp.dma_start(b_raw[:, h * DS:(h + 1) * DS],
                                 strip_view(h * T * STRIP + near0, [[1, T], [STRIP - 1, DS]]),
                                 allow_slow_non_contiguous=True).then_inc(bT_in, 16)
                    for b in range(DB):
                        sp.dma_start(bx_raw[b * DS:(b + 1) * DS, h * DS:(h + 1) * DS],
                                     strip_view(h * T * STRIP + SPAN + T - 1, [[1, DS], [STRIP - 1, DS]]),
                                     allow_slow_non_contiguous=True).then_inc(bT_in, 16)
            sp.dma_start(keys_sb, keys_t.rearrange("h d k -> d h k")).then_inc(keys_in, 16)
            sp.wait_ge(x1_out[1], 16 * SI)
            for hp in range(2 * PH):
                if hp >= 2:
                    sp.wait_ge(wk_ready[1], hp - 1)
                sp.dma_start(wq_st[hp % 2], wq_t[hp * T:(hp + 1) * T, :]).then_inc(wq_in[hp % 2], 16)
            sp.wait_ge(page_read, 2 * DB * NPG)
            sp.dma_start(xn_next[:, :], x1_d[0:T, :]).then_inc(xn_in, 16)
            sp.dma_start(g_ffn[:, :], norm_ffn_g.partition_broadcast(T)).then_inc(early_in, 16)
            sp.dma_start(iota[:, :], c_iota.partition_broadcast(T)).then_inc(early_in, 16)
            for c in range(2):
                b, m = proj(SI, 0, WO + c)
                sp.wait_ge(pb_ready[b], m + 1)
            for c in range(2):
                sp.dma_start(mid[:, :, c * W4:(c + 1) * W4],
                             w_gate[:, c * W4:(c + 1) * W4].rearrange("(k p) n -> p k n", p=T)
                             ).then_inc(gate_w_in, 16)
            sp.wait_ge(x1_out[0], 16 * (SI + COPIES))
            sp.wait_ge(x1_out[1], 16 * SI)
            sp.wait_ge(k_out, 16 * (NT + 2))
            sp.wait_ge(v_out, 16 * (NT + 1))
            sp.wait_ge(new_rows_out, 16 * 2)
            for dst, src in ((g_fin[:, :], final_g.partition_broadcast(T)), (g_pl[:, :], norm_pl_g),
                             (fold[:, :], c_fold),
                             (wpl[:, :, :], w_pl.rearrange("(k p) n -> p k n", p=T))):
                sp.dma_start(dst, src).then_inc(g_in, 16)
            sp.dma_start(x2[:, :], x1_d[0:T, :]).then_inc(x1_in, 16)
            sp.dma_start(p_sb[:, :, :], p_t[:, 0:T].rearrange("(k p) n -> p k n", p=T)).then_inc(p_in, 16)
            with sp.Fori(0, NT) as t:
                sp.wait_ge(xn_moved, t + 1)
                sp.dma_start(xn_next[:, :], x1_d[ds(t * T + T, T), :]).then_inc(xn_in, 16)
                sp.wait_ge(y_ready, t + 1)
                sp.dma_start(y_p[ds(t * T, T), :], x2[:, :]).then_inc(y_out, 16)
                sp.dma_start(p_sb[:, :, :], p_t[:, ds(t * T + T, T)].rearrange("(k p) n -> p k n", p=T)
                             ).then_inc(p_in, 16)
                sp.wait_ge(y_out, t * 16 + 16)
                sp.dma_start(x2[:, :], x1_d[ds(t * T + T, T), :]).then_inc(x1_in, 16)
            sp.wait_ge(y_ready, NT + 1)
            sp.dma_start(y_s, x2[0:NS, :]).then_inc(y_out, 16)
            sp.wait_ge(y_out, 16 * (NT + 1))

        @block.gpsimd
        def _(pool):
            pool.dma_start(npool_s[:, 0:PAD - DS, :], state.rearrange("(b r) n -> b r n", b=DB)[:, DS:PAD, :]
                           ).then_inc(k_out, 16)
            with pool.Fori(0, NT // 2) as i:
                for par in range(2):
                    rows = ds(i * (2 * T) + par * T, T)
                    b, m = proj(i, par, K_)
                    hold(pool, pb_free[b], m + 2)
                    pool.dma_start(nk_p[rows, :], k_sb).then_inc(k_out, 16)
                    b, m = proj(i, par, V_)
                    hold(pool, pb_free[b], m + 2)
                    pool.dma_start(nv_p[rows, :], vals[:, ds(i * 2 + par, 1), :].rearrange(
                        "p a b -> p (a b)")).then_inc(v_out, 16)
                    for c in range(2):
                        b, m = proj(i, par, WO + c)
                        hold(pool, pb_free[b], m + 2)
                    pool.dma_start(x1_d[rows, :], xt[:, par, :]).then_inc(x1_out[par], 16)
            pool.dma_start(npool_p, u_sb[T - PAD:T, 1, :]).then_inc(new_rows_out, 16)
            b, m = proj(SI, 0, K_)
            pool.wait_ge(pb_free[b], m + 2)
            pool.dma_start(nk_s, k_sb[0:NS, :]).then_inc(k_out, 16)
            b, m = proj(SI, 0, V_)
            pool.wait_ge(pb_free[b], m + 2)
            pool.dma_start(nv_s, q_sb[0:NS, :]).then_inc(v_out, 16)
            b, m = proj(SI, 0, U_)
            pool.wait_ge(pb_free[b], m + 2)
            pool.dma_start(npool_s[:, PAD - DS:PAD, :], u_sb[0:NS, 0, :]).then_inc(new_rows_out, 16)
            pool.wait_ge(page_idx, 1)
            pool.wait_ge(av_done, H * NT + H)
            for n in range(2 * DB * NPG):
                if n >= PAGES:
                    pool.wait_ge(page_read, n - PAGES + 1)
                src = cache_k if n < DB * NPG else cache_v
                m = n % (DB * NPG)
                pool.indirect_dma_start(page(n), None, src,
                                        bass.IndirectOffsetOnAxis(ap=pidx[:, m:m + 1], axis=0)
                                        ).then_inc(page_in[n % PAGES], 16)
            for c in range(2):
                b, m = proj(SI, 0, WO + c)
                pool.wait_ge(pb_free[b], m + 2)
            for q in range(COPIES):
                pool.dma_start(x1_d[SEQ + q * NS:SEQ + (q + 1) * NS, :], xt[0:NS, 0, :]
                               ).then_inc(x1_out[0], 16)

            with pool.Fori(0, (N0 + SG) // 2) as s:
                for par in range(2):
                    n = s * 2 + par
                    hold(pool, idx_ready, n + 1)
                    for j in range(TOPK):
                        hold(pool, slot_free, n * TOPK + j + 1)
                        pool.indirect_dma_start(ring[:, j % RING, :], None, uv,
                                                bass.IndirectOffsetOnAxis(ap=idx[:, par, j:j + 1], axis=0)
                                                ).then_inc(gathered[j % RING], 16)

        @block.tensor
        def _(pe):
            for b in range(2):
                pe.sem_inc(pb_free[b], 1)
                pe.sem_inc(tb_free[b], 1)
            pe.wait_ge(const_in, 16 * 14)
            pe.wait_ge(gain_ready, 1)
            pe.wait_ge(onehot_in, 16)
            for h in range(H):
                if h >= 1:
                    pe.wait_ge(strip_sb, h)
                oh = mid[0:BUCKETS + 1, 0:2, 0:768]
                for c in range(4):
                    mm = pe.matmul(sc[:, c, 0:384], AT[0:BUCKETS + 1, h, :], oh[:, c // 2, (c % 2) * 384:(c % 2) * 384 + 384],
                                   start=True, stop=True)
                mm.then_inc(strip_ps, 1)

            def project(i, par, o, P=T, halfway=None):
                b, m = proj(i, par, o)
                pe.wait_ge(pb_free[b], m + 1)
                pe.wait_ge(w_in_in[COLUMNS[o]], 16)
                at = COLUMNS[o] * W4
                for k in range(KD):
                    if halfway and k == KD // 2:
                        halfway()
                    mm = pe.matmul(pb[b][0:P, :], xT[:, k, 0:P], big[:, k, at:at + W4],
                                   start=(k == 0), stop=(k == KD - 1))
                mm.then_inc(pb_ready[b], 1)

            def turn4(bm, ins, rows=T, cols=T, P=T):
                b, m = bm
                pe.wait_ge(tb_free[b], m + 1)
                for c, v in enumerate(ins):
                    mm = pe.transpose(tb[b][0:rows, c * cols:(c + 1) * cols], v, ident[0:P, 0:P])
                mm.then_inc(tb_ready[b], 1)

            def w_out_pooled(i, par, c, P=T):
                b, m = proj(i, par, POOL)
                pe.wait_ge(pb_free[b], m + 2)
                pe.wait_ge(w_out_in, 16 * 2)
                b, m = proj(i, par, WO + c)
                pe.wait_ge(pb_free[b], m + 1)
                for k in range(H, 2 * H):
                    pe.matmul(pb[b][0:P, :], xT[:, k, 0:P], mid[:, k, c * W4:(c + 1) * W4],
                              start=(k == H), stop=False)

            def w_out_heads(i, par, out_turn, P=T):
                pe.wait_ge(o_norm, i * 2 + par + 1)
                turn4(out_turn, [avs[0:P, h * T:(h + 1) * T] for h in range(H)], cols=P, P=P)
                b, m = out_turn
                pe.wait_ge(tb_free[b], m + 2)
                for c in range(2):
                    b, m = proj(i, par, WO + c)
                    for k in range(H):
                        mm = pe.matmul(pb[b][0:P, :], xT[:, k, 0:P], mid[:, k, c * W4:(c + 1) * W4],
                                       start=False, stop=(k == H - 1))
                    mm.then_inc(pb_ready[b], 1)

            def pool_out(i, par, P=T):
                b, m = proj(i, par, BAND)
                pe.wait_ge(pb_free[b], m + 2)
                b, m = proj(i, par, POOL)
                pe.wait_ge(pb_free[b], m + 1)
                for g in range(H):
                    mm = pe.matmul(pb[b][:, g * P:(g + 1) * P], pw[:, g, :], dT[:, g, 0:P],
                                   start=True, stop=True)
                mm.then_inc(pb_ready[b], 1)

            def tile(R, i, par):
                t = i * 2 + par
                nb = R.nb
                pe.wait_ge(x_in[par], i * 16 + 16)
                for c in range(2):
                    turn4(R.turn(i, par, c), [xt[:, par, (4 * c + k) * T:(4 * c + k + 1) * T] for k in range(4)])
                for c in range(2):
                    b, m = R.turn(i, par, c)
                    pe.wait_ge(tb_free[b], m + 2)
                def turn_heads(o, src):
                    b, m = proj(i, par, o)
                    pe.wait_ge(pb_free[b], m + 2)
                    turn4(R.turn(i, par, 2 + o), [src[:, h * T:(h + 1) * T] for h in range(H)])

                for o in (Q_, K_):
                    project(i, par, o)
                turn_heads(Q_, q_sb)
                project(i, par, U_, halfway=lambda: turn_heads(K_, k_sb))
                for o in (2, 3):
                    b, m = R.turn(i, par, o)
                    pe.wait_ge(tb_free[b], m + 2)

                def scores(h):
                    for a in range(2):
                        pe.wait_ge(s_read[a], t * H + h + 1)
                        for c in range(nb):
                            mm = pe.matmul(sc[:, 2 * a + c, :], qT[a * QK:(a + 1) * QK, h, :],
                                           kT[a * QK:(a + 1) * QK, h, c * 512:(c + 1) * 512],
                                           start=True, stop=True)
                        mm.then_inc(s_ready[a], 1)

                def values(h):
                    pe.wait_ge(a_ready, t * H + h + 1)
                    for c in range(nb):
                        turn4(R.a_turn(i, par, h, c),
                              [S[:, h % 2, 0, (4 * c + k) * T:(4 * c + k + 1) * T] for k in range(4)])
                    bo, mo = proj(i, par, AV)
                    if h == 0:
                        pe.wait_ge(pb_free[bo], mo + 1)
                    for c in range(nb):
                        b, m = R.a_turn(i, par, h, c)
                        pe.wait_ge(tb_free[b], m + 2)
                        for k in range(4 * c, 4 * c + 4):
                            mm = pe.matmul(pb[bo][:, h * HV:(h + 1) * HV], AT[:, k, :],
                                           vals[:, k, h * HV:(h + 1) * HV],
                                           start=(k == 0), stop=(k == 4 * nb - 1))
                            if h == 0 and k == 0:
                                mm.then_inc(pb_ready[bo], 1)
                    mm.then_inc(av_done, 1)

                scores(0)
                scores(1)
                project(i, par, V_)
                b, m = proj(i, par, U_)
                pe.wait_ge(pb_free[b], m + 2)
                pe.wait_ge(band_in, t * 16 + 16)
                b, m = proj(i, par, BAND)
                pe.wait_ge(pb_free[b], m + 1)
                for g in range(H):
                    pe.matmul(pb[b][:, g * T:(g + 1) * T], u_sb[:, par, g * T:(g + 1) * T],
                              bandc[:, g, :], start=True, stop=False)
                    mm = pe.matmul(pb[b][:, g * T:(g + 1) * T], u_sb[:, 1 - par, g * T:(g + 1) * T],
                                   bandp[:, g, :], start=False, stop=True)
                mm.then_inc(pb_ready[b], 1)
                b, m = proj(i, par, V_)
                pe.wait_ge(pb_free[b], m + 2)
                values(0)
                pool_out(i, par)
                scores(2)
                values(1)
                scores(3)
                values(2)
                w_out_pooled(i, par, 0)
                values(3)
                w_out_pooled(i, par, 1)
                w_out_heads(i, par, R.o_turn(i, par))

            for R in REGIONS:
                with pe.Fori(R.first, R.last) as i:
                    for par in range(2):
                        tile(R, i, par)

            pe.wait_ge(x_in[0], 16 * (SI + 1))
            for c in range(2):
                turn4(s_turn(c), [xt[0:NS, 0, (4 * c + k) * T:(4 * c + k + 1) * T] for k in range(4)],
                      cols=NS, P=NS)
            for c in range(2):
                b, m = s_turn(c)
                pe.wait_ge(tb_free[b], m + 2)
            for o in (Q_, K_, U_, V_):
                project(SI, 0, o, NS)
            for o, src in ((Q_, q_sb), (K_, k_sb)):
                b, m = proj(SI, 0, o)
                pe.wait_ge(pb_free[b], m + 2)
                turn4(s_turn(2 + o), [src[0:NS, h * T:(h + 1) * T] for h in range(H)], cols=NS, P=NS)
            b, m = proj(SI, 0, U_)
            pe.wait_ge(pb_free[b], m + 2)
            pe.wait_ge(st_in, 32)
            b, m = proj(SI, 0, BAND)
            pe.wait_ge(pb_free[b], m + 1)
            for g in range(H):
                pe.matmul(pb[b][:, g * NS:(g + 1) * NS], u_sb[0:NS, 0, g * T:(g + 1) * T],
                          bs_c[:, g * NS:(g + 1) * NS], start=True, stop=False)
                mm = pe.matmul(pb[b][:, g * NS:(g + 1) * NS], st_sb[0:DB * PAD, g * T:(g + 1) * T],
                               bs_p[:, g * NS:(g + 1) * NS], start=False, stop=True)
            mm.then_inc(pb_ready[b], 1)
            pool_out(SI, 0, NS)
            for o in (2, 3):
                b, m = s_turn(o)
                pe.wait_ge(tb_free[b], m + 2)
            qs = q_bd.rearrange("p (h n) -> p h n", h=H)
            ks = kTs.rearrange("p (h n) -> p h n", h=H)
            pe.wait_ge(s_read[0], H * NT + 1)
            pe.wait_ge(s_read[1], H * NT + 1)
            pk = pkT.rearrange("p r (h n) -> p r h n", h=H)

            def by_row(ap):
                return ap.rearrange("p (b a h i) -> p b a h i", b=DB, a=2, h=H)

            def page_turn(n):
                pe.wait_ge(page_in[n % PAGES], 16 * (n // PAGES + 1))
                b, m = s_turn(S_PAGE + n)
                pe.wait_ge(tb_free[b], m + 1)
                for h in range(H):
                    mm = pe.transpose(tb[b][:, h * T:(h + 1) * T], page(n)[:, h * HV:(h + 1) * HV], ident[:, :])
                mm.then_inc(tb_ready[b], 1)

            def page_scores(n):
                bi, pg = n // NPG, n % NPG
                b, m = s_turn(S_PAGE + n)
                pe.wait_ge(tb_free[b], m + 2)
                out = by_row(sc[:, pg // 2, (pg % 2) * 256:(pg % 2 + 1) * 256])
                for h in range(H):
                    mm = pe.matmul(out[:, bi, :, h, :], pk[:, n % 2, h, :],
                                   qs[:, h, bi * 2 * DS:(bi + 1) * 2 * DS], start=True, stop=True)
                mm.then_inc(page_read, 1)

            def key_half(hp):
                pe.wait_ge(wq_in[hp % 2], 16 * (hp // 2 + 1))
                for c in range(2):
                    if hp >= 1:
                        pe.wait_ge(wk_kept[c], hp)
                    for k in range(4):
                        mm = pe.matmul(pb[c][:, k * NK:(k + 1) * NK],
                                       wq_st[hp % 2][:, (4 * c + k) * T:(4 * c + k + 1) * T],
                                       keys_sb[:, hp, :], start=True, stop=True)
                    mm.then_inc(wk_ready[c], 1)

            for n in range(DB * NPG):
                page_turn(n)
                if n >= 1:
                    page_scores(n - 1)
                if n == 0:
                    for o in (BAND, POOL):
                        b, m = proj(SI, 0, o)
                        pe.wait_ge(pb_free[b], m + 2)
                    pe.wait_ge(keys_in, 16)
                if n % 2:
                    key_half(n // 2)
            page_scores(DB * NPG - 1)
            new = by_row(sc[0:NS, 2, 0:256])
            for h in range(H):
                mm = pe.matmul(new[:, :, :, h, :], ks[:, h, :], qs[:, h, :], start=True, stop=True)
            mm.then_inc(ss_ready, 1)
            pe.wait_ge(sT_ready, 1)
            for g in range(2):
                turn4(s_turn(S_ROW + g), [s_T[:, pg * 256 + g * T:pg * 256 + (g + 1) * T] for pg in range(NPG)])
            turn4(s_turn(S_ROW + 2), [s_Tn[0:NS, g * T:(g + 1) * T] for g in range(2)], cols=NS, P=NS)
            pe.wait_ge(sp_ready, 1)
            for g in range(2):
                turn4(s_turn(S_BACK + g), [s_row[:, g, pg * T:(pg + 1) * T] for pg in range(NPG)])
            turn4(s_turn(S_BACK + 2), [s_row[:, g, PAST:PAST + NS] for g in range(2)], rows=NS)
            for o in range(3):
                b, m = s_turn(S_BACK + o)
                pe.wait_ge(tb_free[b], m + 2)
            for bi in range(DB):
                for pg in range(NPG):
                    n = DB * NPG + bi * NPG + pg
                    pe.wait_ge(page_in[n % PAGES], 16 * (n // PAGES + 1))
                g, rows_b = bi // 4, slice((bi % 4) * 32, (bi % 4 + 1) * 32)
                for pg in range(NPG):
                    n = DB * NPG + bi * NPG + pg
                    at = pg * 256 + bi * 32
                    pe.matmul(sc[rows_b, g, :], pr_T[:, at:at + 32], page(n),
                              start=(pg == 0), stop=False)
                mm = pe.matmul(sc[rows_b, g, :], pr_Tn[0:NS, bi * 32:(bi + 1) * 32], q_sb[0:NS, :],
                               start=False, stop=True)
                mm.then_inc(page_read, NPG)
            for c in range(2):
                pe.wait_ge(wk_kept[c], 2 * PH)
            w_out_pooled(SI, 0, 0, NS)
            pe.wait_ge(o_kept, 2)
            b, m = proj(SI, 0, AV)
            for h in range(H):
                for g in range(2):
                    mm = pe.matmul(pb[b][0:NS, h * HV:(h + 1) * HV], pick_h[:, g, h * NS:(h + 1) * NS],
                                   o_rows[:, g, h * HV:(h + 1) * HV], start=(g == 0), stop=(g == 1))
                if h == 0:
                    mm.then_inc(pb_ready[b], 1)
            mm.then_inc(av_done, H)
            w_out_pooled(SI, 0, 1, NS)
            w_out_heads(SI, 0, s_turn(S_O), NS)

            for c in range(2):
                b, m = proj(SI, 0, WO + c)
                pe.wait_ge(pb_free[b], m + 2)
            pe.sem_inc(slot_free, RING)
            pe.sem_inc(route_read, 1)

            def turn_xn(t):
                pe.wait_ge(xn_ready, t + 1)
                for c in range(2):
                    for k in range(4):
                        mm = pe.transpose(tb[c][:, k * T:(k + 1) * T],
                                          xn_next[:, (4 * c + k) * T:(4 * c + k + 1) * T], ident[:, :])
                    mm.then_inc(xn_turned, 1)
                pe.wait_ge(xnT_ready, t * 2 + 2)

            def route(n, h):
                pe.wait_ge(route_read, n + 1)
                for k in range(KD):
                    mm = pe.matmul(pb[0][:, 0:256], xnT[:, k, :], big[:, k, ds(h * 256, 256)],
                                   start=(k == 0), stop=(k == KD - 1))
                mm.then_inc(route_ready, 1)

            def route_samples(g):
                pe.wait_ge(route_read, N0 + g + 1)
                for q in range(COPIES):
                    tokens, head = slice(q * NS, (q + 1) * NS), g * COPIES + q
                    for k in range(KD):
                        mm = pe.matmul(pb[0][tokens, 0:256], xnT[:, k, tokens],
                                       big[:, k, head * 256:(head + 1) * 256],
                                       start=(k == 0), stop=(k == KD - 1))
                mm.then_inc(route_ready, 1)

            def add_value(r, opens, closes):
                for c in range(2):
                    mm = pe.matmul(sc[:, c, :], diag[:, r, :], ring[:, r, D + c * 512:D + (c + 1) * 512],
                                   start=opens, stop=closes)
                mm.then_inc(slot_free, 1)

            def add_values(n, first=False, last=False, between={}):
                for k in range(NB):
                    pe.wait_ge(diag_ready, n * NB + k + 1)
                    for j in range(k * B, (k + 1) * B):
                        add_value(j % RING, first and j == 0, last and j == TOPK - 1)
                    if k in between:
                        between[k]()

            def turn_x2(t):
                for c in range(2):
                    pe.wait_ge(x2_ready, t * 2 + c + 1)
                    for k in range(4):
                        mm = pe.transpose(tb[c][:, k * T:(k + 1) * T],
                                          x2[:, (4 * c + k) * T:(4 * c + k + 1) * T], ident[:, :])
                    mm.then_inc(x2_turned, 1)

            def embed(t):
                pe.wait_ge(p_in, t * 16 + 16)
                for c in range(2):
                    if c == 1:
                        pe.wait_ge(x2T_ready, t * 2 + 2)
                    for k in range(2):
                        mm = pe.matmul((pb[1], tb[1])[c][:, :], p_sb[:, k, :],
                                       wpl[:, k, c * W4:(c + 1) * W4], start=(k == 0), stop=(k == 1))
                    mm.then_inc(ple_ready, 1)

            def gate_part(c, k0):
                for k in range(k0, k0 + KD // 2):
                    mm = pe.matmul(sc[:, 2 + c, :], x2T[:, k, :], mid[:, k, c * W4:(c + 1) * W4],
                                   start=(k == 0), stop=(k == KD - 1))
                if k0:
                    mm.then_inc(gate_ready, 1)

            def gate(t):
                embed(t)
                for c in range(2):
                    for k0 in (0, KD // 2):
                        gate_part(c, k0)

            def first_step(t):
                add_values(t * PH, first=True, between={
                    0: lambda: embed(t - 1), 1: lambda: gate_part(0, 0), 2: lambda: gate_part(0, KD // 2),
                    3: lambda: gate_part(1, 0), 5: lambda: gate_part(1, KD // 2)})

            def first_heads(t):
                turn_x2(t - 1)
                route(t * PH + 1, 1)
                first_step(t)
                route(t * PH + 2, 2)
                add_values(t * PH + 1)

            def later_heads(t, samples_next=False):
                with pe.Fori(1, PH // 2 - 1) as hh:
                    for par in range(2):
                        route(t * PH + hh * 2 + par + 1, hh * 2 + par + 1)
                        add_values(t * PH + hh * 2 + par)
                route(t * PH + PH - 1, PH - 1)
                add_values(t * PH + PH - 2)
                turn_xn(t + 1)
                if samples_next:
                    route_samples(0)
                else:
                    route(t * PH + PH, 0)
                add_values(t * PH + PH - 1, last=True)

            pe.wait_ge(wk_kept[0], 2 * PH)
            pe.wait_ge(wk_kept[1], 2 * PH)
            turn_xn(0)
            route(0, 0)
            route(1, 1)
            add_values(0, first=True)
            route(2, 2)
            add_values(1)
            pe.wait_ge(gate_w_in, 32)
            pe.wait_ge(g_in, 16 * 4)
            with pe.Fori(0, NT - 1) as t:
                later_heads(t)
                first_heads(t + 1)
            later_heads(NT - 1, samples_next=True)
            turn_x2(NT - 1)
            route_samples(1)
            first_step(NT)
            add_values(N0 + 1, last=True)
            turn_x2(NT)
            gate(NT)

        @block.scalar
        def _(act):
            act.wait_ge(lam_sum, 2)
            act.activation(st[:, LAME:LAME + 2], st[:, LAMS:LAMS + 2], ACT.Exp).then_inc(lam_exp, 1)
            for h in range(H):
                act.wait_ge(strip_ps, h + 1)
                if h >= 2:
                    act.wait_ge(strip_out[h % 2], 16 * (h // 2))
                act.activation(S[:, h % 2, :, :].rearrange("p a b -> p (a b)")[:, 0:STRIP].rearrange(
                    "p (a b) -> p a b", b=384), sc[:, :, 0:384], ACT.Copy).then_inc(strip_sb, 1)

            def tile(R, i, par):
                t = i * 2 + par
                nb = R.nb
                act.wait_ge(x_sq, t + 1)
                act.activation(st[:, XRT + par:XRT + par + 1], st[:, XSS + par:XSS + par + 1], ACT.Sqrt,
                               ).then_inc(x_root, 1)
                act.wait_ge(x_norm, t + 1)

                def evac(o, dst, stand_alone=False):
                    b, m = proj(i, par, o)
                    if stand_alone:
                        hold(act, pb_ready[b], m + 1)
                    else:
                        act.wait_ge(pb_ready[b], m + 1)
                    act.activation(dst, pb[b][:, :], ACT.Copy, scale=st[:, XR + par:XR + par + 1]
                                   ).then_inc(pb_free[b], 1)

                evac(Q_, q_sb)
                act.wait_ge(k_out, t * 16 + 16)
                evac(K_, k_sb)
                b, m = R.turn(i, par, 2)
                act.wait_ge(tb_ready[b], m + 1)
                act.activation(qT, tb[b][:, :].rearrange("p (a b) -> p a b", a=H), ACT.Copy
                               ).then_inc(tb_free[b], 1)
                b, m = R.turn(i, par, 3)
                hold(act, tb_ready[b], m + 1)
                act.activation(kT[:, :, ds(t * T, T)], tb[b][:, :].rearrange("p (a b) -> p a b", a=H),
                               ACT.Copy).then_inc(tb_free[b], 1)
                evac(U_, u_sb[:, par, :])

                def exps(h):
                    for a in range(2):
                        act.wait_ge(s_max[a], t * H + h + 1)
                        row_ = S[:, h % 2, a, 0:R.width]
                        col = 2 * (h % 2) + a
                        act.activation(row_, row_, ACT.Exp, bias=st[:, NMAX + col:NMAX + col + 1],
                                       accum_out=st[:, LSUM + col:LSUM + col + 1]).then_inc(s_exp[a], 1)

                def weights(h):
                    act.wait_ge(av_done, t * H + h + H)
                    for c in range(nb):
                        b, m = R.a_turn(i, par, h, c)
                        act.wait_ge(tb_ready[b], m + 1)
                        act.activation(AT[:, 4 * c:4 * c + 4, :], tb[b][:, :].rearrange("p (a b) -> p a b", a=4),
                                       ACT.Copy).then_inc(tb_free[b], 1)

                exps(0)
                exps(1)
                evac(V_, vals[:, ds(t, 1), :].rearrange("p a b -> p (a b)"), True)
                b, m = proj(i, par, BAND)
                act.wait_ge(pb_ready[b], m + 1)
                act.activation(dT, pb[b][:, :].rearrange("p (a b) -> p a b", a=H), ACT.Copy
                               ).then_inc(pb_free[b], 1)
                weights(0)
                weights(1)
                exps(2)
                weights(2)
                exps(3)
                weights(3)
                act.wait_ge(av_done, t * H + 2 * H)
                b, m = proj(i, par, AV)
                act.activation(avs[:, :], pb[b][:, :], ACT.Copy).then_inc(pb_free[b], 1)
                act.wait_ge(o_sq, t + 1)
                act.activation(st[:, ORT:ORT + H], st[:, OSS:OSS + H], ACT.Sqrt).then_inc(o_root, 1)

            act.wait_ge(zeroed, 1)
            for R in REGIONS:
                with act.Fori(R.first, R.last) as i:
                    for par in range(2):
                        tile(R, i, par)

            act.wait_ge(x_sq, NT + 1)
            act.activation(st[0:NS, XRT:XRT + 1], st[0:NS, XSS:XSS + 1], ACT.Sqrt).then_inc(x_root, 1)
            act.wait_ge(x_norm, NT + 1)
            for o, dst in ((Q_, q_sb), (K_, k_sb), (U_, u_sb[:, 0, :]), (V_, q_sb)):
                b, m = proj(SI, 0, o)
                act.wait_ge(pb_ready[b], m + 1)
                if o == K_:
                    act.wait_ge(k_out, 16 * NT + 16)
                if o == V_:
                    bt, mt = s_turn(2)
                    act.wait_ge(tb_ready[bt], mt + 1)
                act.activation(dst[0:NS, :], pb[b][0:NS, :], ACT.Copy, scale=st[0:NS, XR:XR + 1]
                               ).then_inc(pb_free[b], 1)
                if o == K_:
                    act.wait_ge(av_done, H * NT + H)
                    act.wait_ge(s_read[0], H * NT + 1)
                    act.wait_ge(q_zero, 1)
                    bt, mt = s_turn(2)
                    act.wait_ge(tb_ready[bt], mt + 1)
                    for a in range(2):
                        dims = slice(a * QK, (a + 1) * QK)
                        ins = act.activation(
                            q_bd[dims, :].rearrange("p (m a i) -> p m a i", a=2, i=DS)[:, :, a, :],
                            tb[bt][dims, 0:H * NS].rearrange("p (m i) -> p m i", i=DS), ACT.Copy)
                    ins.then_inc(tb_free[bt], 1)
            bt, mt = s_turn(3)
            act.wait_ge(tb_ready[bt], mt + 1)
            act.activation(kTs, tb[bt][:, 0:H * NS], ACT.Copy).then_inc(tb_free[bt], 1)
            b, m = proj(SI, 0, BAND)
            act.wait_ge(pb_ready[b], m + 1)
            act.activation(dT[:, :, 0:NS], pb[b][:, 0:H * NS].rearrange("p (a b) -> p a b", a=H), ACT.Copy
                           ).then_inc(pb_free[b], 1)
            for n in range(DB * NPG):
                b, m = s_turn(S_PAGE + n)
                act.wait_ge(tb_ready[b], m + 1)
                if n >= 2:
                    act.wait_ge(page_read, n - 1)
                act.activation(pkT[:, n % 2, :], tb[b][:, :], ACT.Copy).then_inc(tb_free[b], 1)
            act.wait_ge(sx_ready, 2)
            for g in range(2):
                act.activation(s_row[:, g, :], s_row[:, g, :], ACT.Exp, bias=st[:, SMX + g:SMX + g + 1],
                               accum_out=st[:, SSUM + g:SSUM + g + 1]).then_inc(sx_exp, 1)
            for g in range(2):
                b, m = s_turn(S_BACK + g)
                act.wait_ge(tb_ready[b], m + 1)
                act.activation(pr_T.rearrange("p (a b) -> p a b", a=NPG)[:, :, g * T:(g + 1) * T],
                               tb[b][:, :].rearrange("p (a b) -> p a b", a=NPG), ACT.Copy
                               ).then_inc(tb_free[b], 1)
            b, m = s_turn(S_BACK + 2)
            act.wait_ge(tb_ready[b], m + 1)
            act.activation(pr_Tn[0:NS, :], tb[b][0:NS, 0:256], ACT.Copy).then_inc(tb_free[b], 1)
            for g in range(2):
                act.wait_ge(page_read, DB * NPG + (g + 1) * DB * NPG // 2)
                act.activation(o_rows[:, g, :], sc[:, g, :], ACT.Copy).then_inc(o_kept, 1)
            act.wait_ge(av_done, H * NT + 2 * H)
            b, m = proj(SI, 0, AV)
            act.activation(avs[0:NS, :], pb[b][0:NS, :], ACT.Copy).then_inc(pb_free[b], 1)
            act.wait_ge(o_sq, NT + 1)
            act.activation(st[0:NS, ORT:ORT + H], st[0:NS, OSS:OSS + H], ACT.Sqrt).then_inc(o_root, 1)

            def norm_next(t):
                act.wait_ge(xn_sq, t + 1)
                act.activation(gst[:, RT1:RT1 + 1], gst[:, NS1:NS1 + 1], ACT.Sqrt).then_inc(xn_root, 1)

            def keep_turned(t):
                for c in range(2):
                    act.wait_ge(xn_turned, t * 2 + c + 1)
                    act.activation(xnT[:, 4 * c:4 * c + 4, :], tb[c][:, :].rearrange("p (a b) -> p a b", a=4),
                                   ACT.Copy).then_inc(xnT_ready, 1)

            def gates(n, par):
                act.wait_ge(top_ready, n + 1)
                act.activation(ex[:, par, :], top2[:, :], ACT.Exp, bias=gst[:, NTOP + par:NTOP + par + 1],
                               accum_out=gst[:, ESUM + par:ESUM + par + 1]).then_inc(top_exp, 1)

            def gelu(n, par, k):
                act.wait_ge(dots_done, n * NB + k + 1)
                act.activation(hgelu[:, par, k * B:(k + 1) * B], hdot[:, par, k * B:(k + 1) * B],
                               ACT.Gelu).then_inc(gelu_done, 1)

            def step(n, par, after={}):
                for k in range(NB):
                    gelu(n, par, k)
                    if k in after:
                        after[k]()

            def close_sum(t):
                act.wait_ge(x2_sq, t + 1)
                act.activation(gst[:, RT2:RT2 + 1], gst[:, NS2:NS2 + 1], ACT.Sqrt).then_inc(x2_root, 1)

            def gate(t, chosen=None):
                act.wait_ge(r2_ready, t + 1)
                if chosen is not None:
                    act.wait_ge(idx_ready, chosen)
                for c in range(2):
                    hold(act, gate_ready, t * 2 + c + 1)
                    act.wait_ge(sig_read, t * 2 + c + 1)
                    act.activation(sg[:, :], sc[:, 2 + c, :], ACT.Sigmoid, scale=gst[:, R2:R2 + 1]
                                   ).then_inc(sig_ready, 1)
                act.wait_ge(y_sq, t + 1)
                act.activation(gst[:, RT3:RT3 + 1], gst[:, NS3:NS3 + 1], ACT.Sqrt).then_inc(y_root, 1)

            def first_step(t):
                n = t * PH
                step(n, 0, {0: lambda: close_sum(t - 1), 1: lambda: gates(n + 1, 1),
                            GATE_AT: lambda: gate(t - 1, n + 2)})

            def first_heads(t):
                n = t * PH
                first_step(t)
                step(n + 1, 1, {2: lambda: gates(n + 2, 0)})

            def later_heads(t):
                with act.Fori(1, PH // 2 - 1) as hh:
                    for par in range(2):
                        n = t * PH + hh * 2 + par
                        step(n, par, {1: lambda: gates(n + 1, 1 - par)})
                n = t * PH + PH - 2
                step(n, 0, {1: lambda: gates(n + 1, 1), 2: lambda: norm_next(t + 1)})
                step(n + 1, 1, {0: lambda: keep_turned(t + 1), 3: lambda: gates(n + 2, 0)})

            norm_next(0)
            keep_turned(0)
            gates(0, 0)
            step(0, 0, {1: lambda: gates(1, 1)})
            step(1, 1, {1: lambda: gates(2, 0)})
            with act.Fori(0, NT - 1) as t:
                later_heads(t)
                first_heads(t + 1)
            later_heads(NT - 1)
            first_step(NT)
            step(N0 + 1, 1)
            close_sum(NT)
            gate(NT)

        @block.vector
        def _(dve):
            for a in range(2):
                dve.sem_inc(s_read[a], 1)
            dve.sem_inc(av_done, H)
            dve.sem_inc(sig_read, 1)
            dve.sem_inc(top_exp, 1)
            dve.memset(relb[BUCKETS:BUCKETS + 1, :], NEG)
            dve.memset(kT, 0.0)
            dve.memset(vals, 0.0)
            dve.memset(u_sb[:, 1, :], 0.0).then_inc(zeroed, 1)
            dve.drain()
            dve.wait_ge(const_in, 16 * 14)
            dve.tensor_copy(AT[0:BUCKETS, 0:H, :],
                            relb[0:BUCKETS, :].unsqueeze(2).to_broadcast([BUCKETS, H, T]))
            dve.tensor_copy(AT[BUCKETS:BUCKETS + 1, 0:H, :],
                            relb[BUCKETS:BUCKETS + 1, :].unsqueeze(2).to_broadcast([1, H, T])
                            ).then_inc(gain_ready, 1)
            for a in range(2):
                dve.tensor_tensor_reduce(lam_in[:, 2 * a, :], lam_in[:, 2 * a, :], lam_in[:, 2 * a + 1, :],
                                         1.0, 0.0, ALU.mult, ALU.add, st[:, LAMS + a:LAMS + a + 1]
                                         ).then_inc(lam_sum, 1)
            dve.tensor_scalar(g_sub[:, :], g_sub[:, :], 1.0 - LAM_INIT, None, ALU.mult)
            dve.tensor_copy(pagef, ptab[:, :])
            dve.drain()
            dve.tensor_scalar(pidx[:, :], pagef, float(PAGE), row[:, 0:1], ALU.mult, ALU.add
                              ).then_inc(page_idx, 1)
            dve.wait_ge(lam_exp, 1)
            dve.tensor_tensor(st[:, NLAM:NLAM + 1], st[:, LAME + 1:LAME + 2], st[:, LAME:LAME + 1],
                              ALU.subtract)
            dve.drain()
            dve.tensor_scalar(st[:, NLAM:NLAM + 1], st[:, NLAM:NLAM + 1], LAM_INIT, None, ALU.subtract)

            def mean_eps(cols, width):
                dve.drain()
                return dve.tensor_scalar(cols, cols, 1.0 / width, EPS, ALU.mult, ALU.add)

            def x_stats(i, par, P=T):
                dve.wait_ge(x_in[par], i * 16 + 16)
                dve.tensor_tensor_reduce(sq[0:P, :], xt[0:P, par, :], xt[0:P, par, :], 1.0, 0.0,
                                         ALU.mult, ALU.add, st[0:P, XSS + par:XSS + par + 1])
                mean_eps(st[0:P, XSS + par:XSS + par + 1], D).then_inc(x_sq, 1)

            def x_turned(turn, P=T):
                for c in range(2):
                    b, m = turn(c)
                    dve.wait_ge(tb_ready[b], m + 1)
                    dve.tensor_tensor(xT[:, 4 * c:4 * c + 4, 0:P],
                                      tb[b][:, 0:4 * P].rearrange("p (a b) -> p a b", a=4),
                                      g_attn[:, 4 * c:4 * c + 4].unsqueeze(2).to_broadcast([T, 4, P]),
                                      ALU.mult).then_inc(tb_free[b], 1)

            def x_factor(t, par, P=T):
                dve.wait_ge(x_root, t + 1)
                dve.reciprocal(st[0:P, XR + par:XR + par + 1], st[0:P, XRT + par:XRT + par + 1]
                               ).then_inc(x_norm, 1)

            def pooled(i, par, P=T):
                b, m = proj(i, par, POOL)
                dve.wait_ge(pb_ready[b], m + 1)
                dve.tensor_tensor(xT[:, H:2 * H, 0:P], pb[b][:, 0:H * P].rearrange("p (a b) -> p a b", a=H),
                                  psc[:, :].unsqueeze(2).to_broadcast([T, H, P]), ALU.mult
                                  ).then_inc(pb_free[b], 1)

            def normed_heads(i, par, t, P=T):
                b, m = proj(i, par, AV)
                dve.wait_ge(pb_free[b], m + 2)
                dve.tensor_tensor(sq[0:P, 0:W4], avs[0:P, :], avs[0:P, :], ALU.mult)
                dve.drain()
                dve.tensor_reduce(st[0:P, OSS:OSS + H], sq[0:P, 0:W4].rearrange("p (h d) -> p h d", h=H),
                                  AX.X, ALU.add)
                mean_eps(st[0:P, OSS:OSS + H], HV).then_inc(o_sq, 1)
                dve.wait_ge(o_root, t + 1)
                dve.reciprocal(st[0:P, OREC:OREC + H], st[0:P, ORT:ORT + H])
                dve.drain()
                av = avs[0:P, :].rearrange("p (h d) -> p h d", h=H)
                dve.tensor_tensor(av, av, st[0:P, OREC:OREC + H].unsqueeze(2).to_broadcast([P, H, HV]),
                                  ALU.mult).then_inc(o_norm, 1)

            def heads_turned(turn, P=T):
                b, m = turn
                dve.wait_ge(tb_ready[b], m + 1)
                dve.tensor_scalar(xT[:, 0:H, 0:P], tb[b][:, 0:H * P].rearrange("p (a b) -> p a b", a=H),
                                  g_sub[:, 0:1], None, ALU.mult).then_inc(tb_free[b], 1)

            def finish(i, par, P=T):
                for c in range(2):
                    b, m = proj(i, par, WO + c)
                    dve.wait_ge(pb_ready[b], m + 1)
                    cols = slice(c * W4, (c + 1) * W4)
                    dve.tensor_tensor(xt[0:P, par, cols], pb[b][0:P, :], xt[0:P, par, cols], ALU.add
                                      ).then_inc(pb_free[b], 1)

            def tile(R, i, par):
                t = i * 2 + par
                W = R.width
                x_turned(lambda c: R.turn(i, par, c))
                x_stats(i, par)
                x_factor(t, par)

                def scores(h):
                    if h >= 2:
                        hold(dve, av_done, t * H + h - 1 + H)
                    for a in range(2):
                        hold(dve, s_ready[a], t * H + h + 1)
                        dve.scalar_tensor_tensor(
                            out=S[:, h % 2, a, 0:W],
                            in0=sc[:, 2 * a:2 * a + R.nb, :].rearrange("p a b -> p (a b)"), scalar=SCALE,
                            in1=biasw[:, h, ds((NT - 1) * T - t * T, W)],
                            op0=ALU.mult, op1=ALU.add).then_inc(s_read[a], 1)
                    dve.drain()
                    for a in range(2):
                        col = NMAX + 2 * (h % 2) + a
                        dve.tensor_reduce(st[:, col:col + 1], S[:, h % 2, a, 0:W], AX.X, ALU.max,
                                          negate=True).then_inc(s_max[a], 1)

                def combine(h):
                    q = h % 2
                    for a in range(2):
                        dve.wait_ge(s_exp[a], t * H + h + 1)
                    c = LREC + 2 * q
                    dve.reciprocal(st[:, c:c + 2], st[:, LSUM + 2 * q:LSUM + 2 * q + 2])
                    dve.drain()
                    dve.tensor_tensor(st[:, c + 1:c + 2], st[:, c + 1:c + 2], st[:, NLAM:NLAM + 1], ALU.mult)
                    dve.tensor_scalar(S[:, q, 0, 0:W], S[:, q, 0, 0:W], st[:, c:c + 1], None, ALU.mult)
                    dve.drain()
                    dve.scalar_tensor_tensor(out=S[:, q, 0, 0:W], in0=S[:, q, 1, 0:W],
                                             scalar=st[:, c + 1:c + 2], in1=S[:, q, 0, 0:W],
                                             op0=ALU.mult, op1=ALU.add).then_inc(a_ready, 1)

                dve.wait_ge(bias_in, 16)
                dve.tensor_copy(far[:, :], biasw[:, :, 0])
                scores(0)
                scores(1)
                combine(0)
                combine(1)
                pooled(i, par)
                for h in (2, 3):
                    scores(h)
                    combine(h)
                normed_heads(i, par, t)
                heads_turned(R.o_turn(i, par))
                finish(i, par)

            for R in REGIONS:
                with dve.Fori(R.first, R.last) as i:
                    for par in range(2):
                        tile(R, i, par)

            dve.memset(q_bd, 0.0).then_inc(q_zero, 1)
            x_stats(SI, 0, NS)
            x_turned(s_turn, NS)
            x_factor(NT, 0, NS)
            dve.wait_ge(bT_in, 16 * H * (DB + 1))
            dve.tensor_copy(bf_T.rearrange("p (h i) -> p h i", h=H),
                            far[:, :].unsqueeze(2).to_broadcast([T, H, DS]))
            pooled(SI, 0, NS)
            dve.drain()
            for hp in range(2 * PH):
                for c in range(2):
                    dve.wait_ge(wk_ready[c], hp + 1)
                    dve.tensor_copy(big[:, 4 * c:4 * c + 4, hp * NK:(hp + 1) * NK],
                                    pb[c][:, :].rearrange("p (a b) -> p a b", a=4)).then_inc(wk_kept[c], 1)
            dve.wait_ge(ss_ready, 1)
            rows8 = lambda ap: ap.rearrange("p (b c) -> p b c", b=DB)
            rows16 = lambda ap: ap.rearrange("p (b c) -> p b c", b=2 * DB)
            per_row = lambda ap: ap.unsqueeze(1).to_broadcast([ap.shape[0], 2 * DB, H * DS])
            for pg in range(NPG):
                dve.scalar_tensor_tensor(
                    out=rows16(s_T[:, pg * 256:(pg + 1) * 256]),
                    in0=rows16(sc[:, pg // 2, (pg % 2) * 256:(pg % 2 + 1) * 256]), scalar=SCALE,
                    in1=per_row(b_raw if pg == NPG - 1 else bf_T), op0=ALU.mult, op1=ALU.add)
            dve.scalar_tensor_tensor(
                out=rows16(s_Tn[0:NS, :]), in0=rows16(sc[0:NS, 2, 0:256]), scalar=SCALE,
                in1=per_row(bx_raw[0:NS, :]), op0=ALU.mult, op1=ALU.add)
            dve.drain()
            dve.tensor_tensor(rows8(s_Tn[0:NS, :]), rows8(s_Tn[0:NS, :]),
                              mask_s[:, :].unsqueeze(2).to_broadcast([NS, DB, 32]), ALU.add
                              ).then_inc(sT_ready, 1)
            for g in range(2):
                b, m = s_turn(S_ROW + g)
                dve.wait_ge(tb_ready[b], m + 1)
                dve.tensor_copy(s_row[:, g, 0:PAST], tb[b][:, :]).then_inc(tb_free[b], 1)
            b, m = s_turn(S_ROW + 2)
            dve.wait_ge(tb_ready[b], m + 1)
            dve.tensor_copy(s_row[:, :, PAST:PAST + NS], tb[b][:, 0:2 * NS].rearrange("p (g n) -> p g n", g=2)
                            ).then_inc(tb_free[b], 1)
            dve.drain()
            for g in range(2):
                dve.tensor_reduce(st[:, SMX + g:SMX + g + 1], s_row[:, g, :], AX.X, ALU.max, negate=True
                                  ).then_inc(sx_ready, 1)
            dve.wait_ge(sx_exp, 2)
            dve.reciprocal(st[:, SREC:SREC + 2], st[:, SSUM:SSUM + 2])
            dve.tensor_scalar(st[:, SCO:SCO + 1], half[:, 1:2], st[:, NLAM:NLAM + 1], None, ALU.mult)
            dve.drain()
            dve.tensor_tensor(st[:, SCO:SCO + 1], st[:, SCO:SCO + 1], half[:, 0:1], ALU.add)
            dve.drain()
            dve.tensor_scalar(st[:, SREC:SREC + 2], st[:, SREC:SREC + 2], st[:, SCO:SCO + 1], None, ALU.mult)
            dve.drain()
            dve.tensor_tensor(s_row, s_row, st[:, SREC:SREC + 2].unsqueeze(2).to_broadcast([T, 2, 544]),
                              ALU.mult).then_inc(sp_ready, 1)
            normed_heads(SI, 0, NT, NS)
            heads_turned(s_turn(S_O), NS)

            def norm_next(t):
                dve.wait_ge(xn_in, t * 16 + 16)
                dve.tensor_tensor_reduce(junk, xn_next[:, :], xn_next[:, :], 1.0, 0.0, ALU.mult,
                                         ALU.add, gst[:, NS1:NS1 + 1])
                mean_eps(gst[:, NS1:NS1 + 1], D).then_inc(xn_sq, 1)
                dve.wait_ge(xn_root, t + 1)
                dve.reciprocal(gst[:, R1:R1 + 1], gst[:, RT1:RT1 + 1])
                dve.drain()
                dve.scalar_tensor_tensor(out=xn_next[:, :], in0=xn_next[:, :], scalar=gst[:, R1:R1 + 1],
                                         in1=g_ffn[:, :], op0=ALU.mult, op1=ALU.mult).then_inc(xn_ready, 1)

            pairs = lambda ap: ap.rearrange("p (i j) -> p i j", i=TOPK)
            over_j = lambda ap: ap.unsqueeze(2).to_broadcast([T, TOPK, TOPK])
            over_i = lambda ap: ap.unsqueeze(1).to_broadcast([T, TOPK, TOPK])

            def choose_keys(n):
                dve.wait_ge(route_ready, n + 1)
                dve.tensor_copy(sc_sb[:, :], pb[0][:, 0:256]).then_inc(route_read, 1)
                dve.drain()
                seg = [slice(s * NK, (s + 1) * NK) for s in range(2)]
                for s in range(2):
                    dve.max(top1[:, s, 0:8], sc_sb[:, seg[s]])
                dve.drain()
                for s in range(2):
                    dve.match_replace(sc_lo[:, seg[s]], top1[:, s, 0:8], sc_sb[:, seg[s]], FMAX)
                    dve.max_index(ind1[:, s, 0:8], top1[:, s, 0:8], sc_sb[:, seg[s]])
                dve.drain()
                for s in range(2):
                    dve.max(top1[:, s, 8:16], sc_lo[:, seg[s]])
                dve.drain()
                dve.tensor_tensor(pairs(cand[:, :]), over_j(top1[:, 0, :]), over_i(top1[:, 1, :]), ALU.add)
                for s in range(2):
                    dve.max_index(ind1[:, s, 8:16], top1[:, s, 8:16], sc_lo[:, seg[s]])

            def choose_pairs(n, par):
                hold(dve, top_exp, n + 1)
                dve.drain()
                dve.max(top2[:, 0:8], cand[:, :])
                dve.drain()
                dve.match_replace(cand_lo[:, :], top2[:, 0:8], cand[:, :], FMAX)
                dve.max_index(ind2[:, 0:8], top2[:, 0:8], cand[:, :])
                dve.drain()
                dve.max(top2[:, 8:16], cand_lo[:, :])
                dve.tensor_scalar(gst[:, NTOP + par:NTOP + par + 1], top2[:, 0:1], -1.0, None, ALU.mult
                                  ).then_inc(top_ready, 1)
                dve.tensor_copy(ind1f[:, :, :], ind1[:, :, :])
                dve.drain()
                dve.max_index(ind2[:, 8:16], top2[:, 8:16], cand_lo[:, :])
                dve.drain()
                dve.tensor_scalar(ab[:, 0, :], ind2[:, :], 4, None, ALU.logical_shift_right)
                dve.tensor_scalar(ab[:, 1, :], ind2[:, :], 15, None, ALU.bitwise_and)
                dve.drain()
                dve.tensor_copy(abf[:, :, :], ab[:, :, :])
                dve.drain()
                tmp = (cand, cand_lo)
                for s in range(2):
                    dve.tensor_tensor(pairs(tmp[s][:, :]), over_j(abf[:, s, :]), over_i(iota[:, :]),
                                      ALU.is_equal)
                dve.drain()
                for s in range(2):
                    dve.tensor_tensor(pairs(tmp[s][:, :]), pairs(tmp[s][:, :]), over_i(ind1f[:, s, :]),
                                      ALU.mult)
                dve.drain()
                for s in range(2):
                    dve.tensor_reduce(pick[:, s, :], pairs(tmp[s][:, :]), AX.X, ALU.add)
                dve.drain()
                dve.scalar_tensor_tensor(out=idx[:, par, :], in0=pick[:, 0, :], scalar=float(NK),
                                         in1=pick[:, 1, :], op0=ALU.mult, op1=ALU.add).then_inc(idx_ready, 1)

            def gates(n, par):
                dve.wait_ge(top_exp, n + 2)
                dve.reciprocal(gst[:, EREC + par:EREC + par + 1], gst[:, ESUM + par:ESUM + par + 1])
                dve.drain()
                dve.tensor_scalar(gate[:, par, :], ex[:, par, :], gst[:, EREC + par:EREC + par + 1], None,
                                  ALU.mult)

            def dot(r, par, j, use):
                dve.wait_ge(gathered[r], use)
                return dve.tensor_tensor_reduce(ring[:, r, 0:D], ring[:, r, 0:D], xn_cur[:, :],
                                                1.0, 0.0, ALU.mult, ALU.add, hdot[:, par, j:j + 1])

            def dots(n, par, k):
                for j in range(k * B, (k + 1) * B):
                    ins = dot(j % RING, par, j, n * 32 + (j // RING) * 16 + 16)
                ins.then_inc(dots_done, 1)

            def coefficients(n, par, k, rows):
                dve.wait_ge(gelu_done, n * NB + k + 1)
                hold(dve, slot_free, n * TOPK + (k + 1) * B)
                for j in range(k * B, (k + 1) * B):
                    ins = dve.tensor_scalar(diag[:, j % RING, :], rows[:, :], hgelu[:, par, j:j + 1],
                                            gate[:, par, j:j + 1], ALU.mult, ALU.mult)
                ins.then_inc(diag_ready, 1)

            def step(n, par, after={}, dotted={}, rows=ident):
                for k in range(NB):
                    dots(n, par, k)
                    if k in dotted:
                        dotted[k]()
                    coefficients(n, par, k, rows)
                    if k in after:
                        after[k]()

            def close_sum(t, slots=PH * TOPK):
                dve.wait_ge(x1_in, t * 16 + 16)
                hold(dve, slot_free, t * (PH * TOPK) + slots + RING)
                for c in range(2):
                    half_c = slice(c * W4, (c + 1) * W4)
                    dve.tensor_tensor(x2[:, half_c], x2[:, half_c], sc[:, c, :], ALU.add).then_inc(x2_ready, 1)
                for c in range(2):
                    dve.wait_ge(x2_turned, t * 2 + c + 1)
                    dve.tensor_tensor(x2T[:, 4 * c:4 * c + 4, :],
                                      tb[c][:, :].rearrange("p (a b) -> p a b", a=4),
                                      g_pl[:, 4 * c:4 * c + 4].unsqueeze(2).to_broadcast([T, 4, T]),
                                      ALU.mult).then_inc(x2T_ready, 1)
                dve.tensor_tensor_reduce(junk, x2[:, :], x2[:, :], 1.0, 0.0, ALU.mult, ALU.add,
                                         gst[:, NS2:NS2 + 1])
                mean_eps(gst[:, NS2:NS2 + 1], D).then_inc(x2_sq, 1)
                dve.wait_ge(x2_root, t + 1)
                dve.reciprocal(gst[:, R2:R2 + 1], gst[:, RT2:RT2 + 1]).then_inc(r2_ready, 1)

            def open_tile():
                dve.tensor_copy(xn_cur[:, :], xn_next[:, :]).then_inc(xn_moved, 1)
                dve.drain()

            def gate_and_embed(t):
                for c in range(2):
                    half_c = slice(c * W4, (c + 1) * W4)
                    hold(dve, sig_ready, t * 2 + c + 1)
                    dve.wait_ge(ple_ready, t * 2 + c + 1)
                    dve.tensor_tensor(sg[:, :], sg[:, :], (pb[1], tb[1])[c][:, :], ALU.mult
                                      ).then_inc(ple_read, 1)
                    dve.drain()
                    dve.tensor_tensor(x2[:, half_c], x2[:, half_c], sg[:, :], ALU.add).then_inc(sig_read, 1)
                dve.drain()
                dve.tensor_tensor_reduce(junk, x2[:, :], x2[:, :], 1.0, 0.0, ALU.mult, ALU.add,
                                         gst[:, NS3:NS3 + 1])
                mean_eps(gst[:, NS3:NS3 + 1], D).then_inc(y_sq, 1)
                dve.wait_ge(y_root, t + 1)
                dve.reciprocal(gst[:, R3:R3 + 1], gst[:, RT3:RT3 + 1])
                dve.drain()
                dve.scalar_tensor_tensor(out=x2[:, :], in0=x2[:, :], scalar=gst[:, R3:R3 + 1],
                                         in1=g_fin[:, :], op0=ALU.mult, op1=ALU.mult).then_inc(y_ready, 1)

            def first_step(t, rows=ident):
                n = t * PH
                open_tile()
                step(n, 0, {0: lambda: choose_keys(n + 1), 1: lambda: choose_pairs(n + 1, 1),
                            4: lambda: gates(n + 1, 1),
                            GATE_AT: lambda: gate_and_embed(t - 1)},
                     {0: lambda: close_sum(t - 1)}, rows)

            def first_heads(t):
                n = t * PH
                first_step(t)
                step(n + 1, 1, {1: lambda: choose_keys(n + 2), 2: lambda: choose_pairs(n + 2, 0),
                                4: lambda: gates(n + 2, 0)})

            def later_heads(t):
                with dve.Fori(1, PH // 2 - 1) as hh:
                    for par in range(2):
                        n = t * PH + hh * 2 + par
                        step(n, par, {0: lambda: choose_keys(n + 1), 1: lambda: choose_pairs(n + 1, 1 - par),
                                      4: lambda: gates(n + 1, 1 - par)})
                n = t * PH + PH - 2
                step(n, 0, {0: lambda: choose_keys(n + 1), 1: lambda: choose_pairs(n + 1, 1),
                            2: lambda: norm_next(t + 1),
                            4: lambda: gates(n + 1, 1)})
                step(n + 1, 1, {2: lambda: choose_keys(n + 2), 3: lambda: choose_pairs(n + 2, 0),
                                5: lambda: gates(n + 2, 0)})

            dve.wait_ge(early_in, 16 * 2)
            norm_next(0)
            finish(SI, 0, NS)
            choose_keys(0)
            choose_pairs(0, 0)
            gates(0, 0)
            dve.wait_ge(g_in, 16 * 4)
            dve.drain()
            open_tile()
            step(0, 0, {0: lambda: choose_keys(1), 1: lambda: choose_pairs(1, 1), 4: lambda: gates(1, 1)})
            step(1, 1, {0: lambda: choose_keys(2), 1: lambda: choose_pairs(2, 0), 4: lambda: gates(2, 0)})
            with dve.Fori(0, NT - 1) as t:
                later_heads(t)
                first_heads(t + 1)
            later_heads(NT - 1)
            first_step(NT, fold)
            step(N0 + 1, 1, rows=fold)
            close_sum(NT, SG * TOPK)
            gate_and_embed(NT)


def onehot_buckets():
    n = SPAN + T - 1 - np.arange(STRIP)
    exact = BUCKETS // 2
    pos = np.maximum(n, 1).astype(np.float32) / np.float32(exact)
    large = exact + (np.log(pos) / np.float32(np.log(MAX_DIST / exact)) * np.float32(BUCKETS - exact)
                     ).astype(np.int32)
    bucket = np.where(n < exact, n, np.minimum(large, BUCKETS - 1))
    bucket = np.where(n < 0, BUCKETS, bucket)
    return (np.arange(BUCKETS + 1)[:, None] == bucket[None, :]).astype(np.float32)


def bands():
    cur = np.zeros((NT, T, H, T), np.float32)
    prev = np.zeros((T, H, T), np.float32)
    s, t = np.arange(T)[:, None], np.arange(T)[None, :]
    for g, w in enumerate(WINDOWS):
        inside = ((s <= t) & (s > t - w)).astype(np.float32)
        for k in range(NT):
            cur[k, :, g, :] = inside / np.minimum(k * T + t + 1, w) - (s == t)
        prev[:, g, :] = (s - T > t - w) / np.float32(w)
    return cur.reshape(NT * T, H * T), prev


def sample_bands():
    cur = np.zeros((NS, H, NS), np.float32)
    old = np.zeros((DB * PAD, H, NS), np.float32)
    for g, w in enumerate(WINDOWS):
        for b in range(DB):
            for i in range(DS):
                at = PAD + i
                for r in range(at - w + 1, at + 1):
                    if r < PAD:
                        old[b * PAD + r, g, b * DS + i] += 1.0 / w
                    else:
                        cur[b * DS + r - PAD, g, b * DS + i] += 1.0 / w
                cur[b * DS + i, g, b * DS + i] -= 1.0
    return cur.reshape(NS, H * NS), old.reshape(DB * PAD, H * NS)


def head_rows():
    row = np.arange(T)
    batch, head, i = row // (2 * H * DS), (row // DS) % H, row % DS
    out = np.zeros((T, 2, H, NS), np.float32)
    for g in range(2):
        out[row, g, head, (g * (DB // 2) + batch) * DS + i] = 1.0
    return out.reshape(T, 2 * H * NS)


_OUTS = [(SEQ, D), (NS, D), (SEQ, W4), (SEQ, W4), (PAD, W4), (NS, W4), (NS, W4), (DB, PAD, W4)]
_SHAPES = [(1, SEQ, D), (DB, DS, D), (1, 1, SEQ, H, 2 * QK), (1, 1, SEQ, H, HV), (1, 1, PAD, W4),
           (1, DB, DS, H, 2 * QK), (1, DB, DS, H, HV), (1, DB, PAD, W4)]


def kernel(**inputs):
    import concourse.bacc as bacc
    from concourse.bass_utils import run_bass_kernel_spmd

    a = {k: np.asarray(v) for k, v in inputs.items()}
    cur, prev = bands()
    s_cur, s_old = sample_bands()
    rows = np.arange(T)
    mask = np.where(np.arange(NS)[:, None] // DS == np.arange(DB)[None, :], 0.0, NEG).astype(np.float32)
    first_half = (rows // (H * DS)) % 2 == 0
    laid = [
        ("x", a["x_prompt"].reshape(SEQ, D)), ("xs", a["x_sample"].reshape(NS, D)),
        ("cache_k", a["cache_k"].reshape(-1, W4)), ("cache_v", a["cache_v"].reshape(-1, W4)),
        ("page_table", a["page_table"]), ("state", a["state_pool"].reshape(DB * PAD, W4)),
        ("p_t", np.concatenate([a["p_prompt"].reshape(SEQ, PLE), a["p_sample"].reshape(NS, PLE),
                                np.zeros((T - NS, PLE), np.float32)]).T),
        ("norm_attn_g", a["norm_attn_g"].reshape(KD, T).T), ("w_in", a["w_in"][0]),
        ("lams", np.concatenate([a["lambda_q1"], a["lambda_k1"], a["lambda_q2"], a["lambda_k2"]])),
        ("subln_g", a["subln_g"].reshape(HV, 1)), ("rel_bias", a["rel_bias"]),
        ("pool_w", a["pool_w"][0].transpose(1, 0, 2)), ("pool_scale", a["pool_scale"].reshape(H, T).T),
        ("w_out", a["w_out"][0]), ("norm_ffn_g", a["norm_ffn_g"].reshape(D)),
        ("wq_t", a["peer_wq"][0].T), ("keys_t", a["peer_keys"].reshape(2 * PH, NK, NK).transpose(0, 2, 1)),
        ("uv", np.concatenate([a["peer_u"][0], a["peer_v"][0]], axis=1)),
        ("norm_pl_g", a["norm_pl_g"].reshape(KD, T).T), ("w_pl", a["w_pl"][0]),
        ("w_gate", a["w_pl_gate"][0]), ("final_g", a["final_norm_g"]),
        ("c_ident", np.eye(T, dtype=np.float32)), ("c_onehot", onehot_buckets()),
        ("c_bands", cur), ("c_band_prev", prev), ("c_band_s", s_cur), ("c_band_sp", s_old),
        ("c_mask_s", mask), ("c_half", np.stack([first_half, ~first_half], 1).astype(np.float32)),
        ("c_row", rows.astype(np.float32)[:, None]), ("c_iota", np.arange(TOPK, dtype=np.float32)),
        ("c_fold", (rows[:, None] % NS == rows[None, :] % NS).astype(np.float32)),
        ("c_pick_h", head_rows()),
    ]
    nc = bacc.Bacc("TRN2", target_bir_lowering=False, num_devices=1)
    arrays, args = {}, []
    for name, v in laid:
        v = np.ascontiguousarray(v)
        arrays[f"in_{name}"] = v
        args.append(nc.dram_tensor(f"in_{name}", v.shape, mybir.dt.from_np(v.dtype), kind="ExternalInput").ap())
    outs = [nc.dram_tensor(f"out_{i}", s, mybir.dt.float32, kind="ExternalOutput").ap()
            for i, s in enumerate(_OUTS)]
    front_and_experts(nc, *args, outs)
    r = run_bass_kernel_spmd(nc, [arrays], core_ids=[0])
    return tuple(r.results[0][f"out_{i}"].reshape(s) for i, s in enumerate(_SHAPES))
```
